# Optimizing a Trainium2 kernel written in Bass

```python
import math
import jax, jax.numpy as jnp
from jax import lax
import numpy as np

D_MODEL = 1024
BATCH = 1
SEQ = 256
DEPTH = 2

N_MIXERS = 2
N_ATTN_LAYERS = (DEPTH + 1) // 2
N_HGRN_LAYERS = DEPTH // 2

ATT_HEADS = 16
ATT_HEAD_DIM = 64
ATT_KV_HEADS = 2
Q_LORA_RANK = 256
IDX_HEADS = 8
IDX_DIM = 128
INDEX_TOPK = 256
Q_BLOCK = 128
ATT_KV_DIM = ATT_KV_HEADS * ATT_HEAD_DIM
ATT_IN_DIM = Q_LORA_RANK + 2 * ATT_KV_DIM + IDX_DIM + IDX_HEADS

HGRN_EXPAND = 128
HGRN_HEADS = D_MODEL // HGRN_EXPAND
HGRN_F_DIM = HGRN_HEADS * HGRN_EXPAND
HGRN_V_DIM = D_MODEL // HGRN_HEADS
HGRN_CHUNK = 64
HGRN_IN_DIM = 2 * HGRN_F_DIM + D_MODEL + D_MODEL

D_FF = -(-8 * D_MODEL // (3 * 256)) * 256

ROPE_THETA = 500000.0
ATT_ROT_DIM = ATT_HEAD_DIM // 4
IDX_ROT_DIM = IDX_DIM // 4
DEEPNORM_ALPHA = (2 * DEPTH) ** 0.25
DEEPNORM_BETA = (8 * DEPTH) ** -0.25
LN_EPS = 1e-5
RMS_EPS = 1e-6


def layer_norm(x, g, b):
    xf = x.astype(jnp.float32)
    mu = jnp.mean(xf, axis=-1, keepdims=True)
    var = jnp.mean(jnp.square(xf - mu), axis=-1, keepdims=True)
    return ((xf - mu) * lax.rsqrt(var + LN_EPS) * g.astype(jnp.float32) + b.astype(jnp.float32)).astype(x.dtype)

def rms_norm(x, g):
    xf = x.astype(jnp.float32)
    ms = jnp.mean(jnp.square(xf), axis=-1, keepdims=True)
    return (xf * lax.rsqrt(ms + RMS_EPS) * g.astype(jnp.float32)).astype(x.dtype)

def rope_tables(positions, rot_dim):
    inv = ROPE_THETA ** (-jnp.arange(0, rot_dim, 2, dtype=jnp.float32) / rot_dim)
    ang = positions.astype(jnp.float32)[..., None] * inv
    return jnp.cos(ang), jnp.sin(ang)

def apply_rope(x, cos, sin):
    half = cos.shape[-1]
    cos = cos.astype(x.dtype)
    sin = sin.astype(x.dtype)
    x1 = x[..., :half]
    x2 = x[..., half:2 * half]
    return jnp.concatenate([x1 * cos - x2 * sin, x2 * cos + x1 * sin, x[..., 2 * half:]], axis=-1)

def dsa_mixer(x, cos_q, sin_q, cos_i, sin_i, w_in, g_cq, w_uq, w_iq, g_ik, b_ik, w_o):
    B, T, _ = x.shape
    dt = x.dtype
    h = x @ w_in
    c_q, k, v, k_idx, w_idx = jnp.split(
        h, [Q_LORA_RANK, Q_LORA_RANK + ATT_KV_DIM, Q_LORA_RANK + 2 * ATT_KV_DIM,
            Q_LORA_RANK + 2 * ATT_KV_DIM + IDX_DIM], axis=-1)
    c_q = rms_norm(c_q, g_cq)
    q = (c_q @ w_uq).reshape(B, T, ATT_HEADS, ATT_HEAD_DIM)
    q_idx = (c_q @ w_iq).reshape(B, T, IDX_HEADS, IDX_DIM)
    k = k.reshape(B, T, ATT_KV_HEADS, ATT_HEAD_DIM)
    v = v.reshape(B, T, ATT_KV_HEADS, ATT_HEAD_DIM)
    k_idx = layer_norm(k_idx, g_ik, b_ik)
    q = apply_rope(q, cos_q[:, :, None], sin_q[:, :, None])
    k = apply_rope(k, cos_q[:, :, None], sin_q[:, :, None])
    q_idx = apply_rope(q_idx, cos_i[:, :, None], sin_i[:, :, None])
    k_idx = apply_rope(k_idx, cos_i, sin_i)
    w_idx = w_idx * (IDX_HEADS ** -0.5 * IDX_DIM ** -0.5)

    topk = min(INDEX_TOPK, T // 4)
    nb = T // Q_BLOCK
    group = ATT_HEADS // ATT_KV_HEADS
    key_pos = jnp.arange(T)

    def blocks(a):
        return jnp.moveaxis(a.reshape(B, nb, Q_BLOCK, *a.shape[2:]), 1, 0)

    def attend_block(args):
        qb, qib, wb, start = args
        t_pos = start + jnp.arange(Q_BLOCK)
        causal = key_pos[None, :] <= t_pos[:, None]
        rel = jax.nn.relu(jnp.einsum('bqhd,bsd->bhqs', qib, k_idx))
        score = jnp.einsum('bqh,bhqs->bqs', wb, rel).astype(jnp.float32)
        score = jnp.where(causal[None], score, -jnp.inf)
        _, sel = lax.top_k(score, topk)
        valid = sel <= t_pos[None, :, None]
        k_sel = jax.vmap(lambda kk, ii: kk[ii])(k, sel)
        v_sel = jax.vmap(lambda vv, ii: vv[ii])(v, sel)
        qg = qb.reshape(B, Q_BLOCK, ATT_KV_HEADS, group, ATT_HEAD_DIM)
        logits = jnp.einsum('bqgrd,bqkgd->bqgrk', qg, k_sel).astype(jnp.float32) * (ATT_HEAD_DIM ** -0.5)
        logits = jnp.where(valid[:, :, None, None, :], logits, -jnp.inf)
        p = jax.nn.softmax(logits, axis=-1).astype(dt)
        o = jnp.einsum('bqgrk,bqkgd->bqgrd', p, v_sel)
        return o.reshape(B, Q_BLOCK, ATT_HEADS * ATT_HEAD_DIM)

    out = lax.map(attend_block, (blocks(q), blocks(q_idx), blocks(w_idx), jnp.arange(nb) * Q_BLOCK))
    out = jnp.moveaxis(out, 0, 1).reshape(B, T, ATT_HEADS * ATT_HEAD_DIM)
    return out @ w_o

def chunk_gated_linear(q, k, v, logf):
    B, H, T, K = q.shape
    V = v.shape[-1]
    C = HGRN_CHUNK
    nc = T // C
    mask = jnp.tril(jnp.ones((C, C), dtype=bool))

    def to_chunks(a):
        return jnp.moveaxis(a.reshape(B, H, nc, C, a.shape[-1]), 2, 0)

    def step(S, inp):
        qc, kc, vc, gc = inp
        b = jnp.cumsum(gc, axis=-2)
        diff = b[..., :, None, :] - b[..., None, :, :]
        decay = jnp.exp(jnp.where(mask[:, :, None], diff, -jnp.inf))
        attn = jnp.einsum('bhtsk,bhsk->bhts', decay * qc[..., :, None, :], kc)
        o = jnp.einsum('bhts,bhsv->bhtv', attn, vc) + jnp.einsum('bhtk,bhkv->bhtv', qc * jnp.exp(b), S)
        b_last = b[..., -1:, :]
        S = jnp.exp(b_last[..., 0, :])[..., None] * S + jnp.einsum('bhsk,bhsv->bhkv', kc * jnp.exp(b_last - b), vc)
        return S, o

    S0 = jnp.zeros((B, H, K, V), jnp.float32)
    _, o = lax.scan(step, S0, (to_chunks(q), to_chunks(k), to_chunks(v), to_chunks(logf)))
    return jnp.moveaxis(o, 0, 2).reshape(B, H, T, V)

def hgrn2_mixer(x, lb, w_in, g_norm, w_o):
    B, T, _ = x.shape
    dt = x.dtype
    h = x @ w_in
    q, f, i, g = jnp.split(h, [HGRN_F_DIM, 2 * HGRN_F_DIM, 2 * HGRN_F_DIM + D_MODEL], axis=-1)
    q = jax.nn.silu(q.astype(jnp.float32))
    fg = lb + (1.0 - lb) * jax.nn.sigmoid(f.astype(jnp.float32))
    k = 1.0 - fg
    logf = jnp.log(fg)

    def heads(a, d):
        return jnp.transpose(a.reshape(B, T, HGRN_HEADS, d), (0, 2, 1, 3))

    o = chunk_gated_linear(heads(q, HGRN_EXPAND), heads(k, HGRN_EXPAND),
                           heads(i.astype(jnp.float32), HGRN_V_DIM), heads(logf, HGRN_EXPAND))
    o = jnp.transpose(o, (0, 2, 1, 3))
    o = rms_norm(o, g_norm) * jax.nn.silu(g.astype(jnp.float32).reshape(B, T, HGRN_HEADS, HGRN_V_DIM))
    return o.reshape(B, T, D_MODEL).astype(dt) @ w_o

def swiglu(x, w_gate, w_up, w_down):
    return (jax.nn.silu(x @ w_gate) * (x @ w_up)) @ w_down

def first_inputs(seed: int = 0) -> dict:
    key = jax.random.key(seed)
    ks = jax.random.split(key, 32)
    f32 = jnp.float32
    nA, nB, D = N_ATTN_LAYERS, N_HGRN_LAYERS, D_MODEL

    def nrm(k, shape, fan_in, scale=1.0):
        return jax.random.normal(k, shape, f32) * (fan_in ** -0.5) * scale

    x = jax.random.normal(ks[0], (BATCH, SEQ, D), f32)
    offset = jax.random.randint(ks[1], (BATCH, 1), 0, 1024, dtype=jnp.int32)
    positions = offset + jnp.arange(SEQ, dtype=jnp.int32)[None, :]

    att_w_in = jnp.concatenate([
        nrm(ks[2], (nA, D, Q_LORA_RANK), D),
        nrm(ks[3], (nA, D, ATT_KV_DIM), D),
        nrm(ks[4], (nA, D, ATT_KV_DIM), D, DEEPNORM_BETA),
        nrm(ks[5], (nA, D, IDX_DIM), D),
        nrm(ks[6], (nA, D, IDX_HEADS), D)], axis=-1)
    att_g_cq = 1.0 + 0.02 * jax.random.normal(ks[7], (nA, Q_LORA_RANK), f32)
    att_w_uq = nrm(ks[8], (nA, Q_LORA_RANK, ATT_HEADS * ATT_HEAD_DIM), Q_LORA_RANK)
    att_w_iq = nrm(ks[9], (nA, Q_LORA_RANK, IDX_HEADS * IDX_DIM), Q_LORA_RANK)
    att_g_ik = 1.0 + 0.02 * jax.random.normal(ks[10], (nA, IDX_DIM), f32)
    att_b_ik = 0.02 * jax.random.normal(ks[11], (nA, IDX_DIM), f32)
    att_w_o = nrm(ks[12], (nA, ATT_HEADS * ATT_HEAD_DIM, D), ATT_HEADS * ATT_HEAD_DIM, DEEPNORM_BETA)

    hgrn_lb_logits = 0.5 * jax.random.normal(ks[13], (DEPTH, HGRN_F_DIM), f32)
    hgrn_w_in = jnp.concatenate([
        nrm(ks[14], (nB, D, HGRN_F_DIM), D),
        nrm(ks[15], (nB, D, HGRN_F_DIM), D),
        nrm(ks[16], (nB, D, D), D, DEEPNORM_BETA),
        nrm(ks[17], (nB, D, D), D)], axis=-1)
    hgrn_g_norm = 1.0 + 0.02 * jax.random.normal(ks[18], (nB, HGRN_V_DIM), f32)
    hgrn_w_o = nrm(ks[19], (nB, D, D), D, DEEPNORM_BETA)

    ffn_w_gate = nrm(ks[20], (DEPTH, D, D_FF), D, DEEPNORM_BETA)
    ffn_w_up = nrm(ks[21], (DEPTH, D, D_FF), D, DEEPNORM_BETA)
    ffn_w_down = nrm(ks[22], (DEPTH, D_FF, D), D_FF, DEEPNORM_BETA)

    ln_g = 1.0 + 0.02 * jax.random.normal(ks[23], (DEPTH, 2, D), f32)
    ln_b = 0.02 * jax.random.normal(ks[24], (DEPTH, 2, D), f32)

    return {"x": x, "positions": positions,
            "att_w_in": att_w_in, "att_g_cq": att_g_cq, "att_w_uq": att_w_uq, "att_w_iq": att_w_iq,
            "att_g_ik": att_g_ik, "att_b_ik": att_b_ik, "att_w_o": att_w_o,
            "hgrn_lb_logits": hgrn_lb_logits, "hgrn_w_in": hgrn_w_in, "hgrn_g_norm": hgrn_g_norm,
            "hgrn_w_o": hgrn_w_o,
            "ffn_w_gate": ffn_w_gate, "ffn_w_up": ffn_w_up, "ffn_w_down": ffn_w_down,
            "ln_g": ln_g, "ln_b": ln_b}

def first_block(x, positions, att_w_in, att_g_cq, att_w_uq, att_w_iq, att_g_ik, att_b_ik, att_w_o,
              hgrn_lb_logits, hgrn_w_in, hgrn_g_norm, hgrn_w_o,
              ffn_w_gate, ffn_w_up, ffn_w_down, ln_g, ln_b):
    cos_q, sin_q = rope_tables(positions, ATT_ROT_DIM)
    cos_i, sin_i = rope_tables(positions, IDX_ROT_DIM)
    lb_all = jnp.cumsum(jax.nn.softmax(hgrn_lb_logits.astype(jnp.float32), axis=0), axis=0)
    lb_all = lb_all - lb_all[0]
    h = x
    for layer in range(DEPTH):
        j = layer // N_MIXERS
        if layer % N_MIXERS == 0:
            mix = dsa_mixer(h, cos_q, sin_q, cos_i, sin_i, att_w_in[j], att_g_cq[j], att_w_uq[j],
                            att_w_iq[j], att_g_ik[j], att_b_ik[j], att_w_o[j])
        else:
            mix = hgrn2_mixer(h, lb_all[layer], hgrn_w_in[j], hgrn_g_norm[j], hgrn_w_o[j])
        h = layer_norm(DEEPNORM_ALPHA * h + mix, ln_g[layer, 0], ln_b[layer, 0])
        ffn = swiglu(h, ffn_w_gate[layer], ffn_w_up[layer], ffn_w_down[layer])
        h = layer_norm(DEEPNORM_ALPHA * h + ffn, ln_g[layer, 1], ln_b[layer, 1])
    return h


DEPTH_2 = 1

N_HEADS = 16
HEAD_DIM = D_MODEL // N_HEADS
D_FF_2 = ((8 * D_MODEL // 3 + 255) // 256) * 256
CONV_WIDTH = 3
MOBA_BLOCK = 256
MOBA_TOPK = 3
MOBA_QCHUNK = 32
SB_QBLOCK = 128
REL_BUCKETS = 32
REL_MAX_DIST = 128
NORM_EPS = 1e-6
NEG = -1e30


def rms_norm_2(x, g):
    xf = x.astype(jnp.float32)
    y = xf * lax.rsqrt(jnp.mean(xf * xf, axis=-1, keepdims=True) + NORM_EPS)
    return (y * g.astype(jnp.float32)).astype(x.dtype)

def rel_bucket(dist):
    n = jnp.maximum(dist, 0)
    max_exact = REL_BUCKETS // 2
    nf = jnp.maximum(n, 1).astype(jnp.float32)
    large = max_exact + (jnp.log(nf / max_exact) / math.log(REL_MAX_DIST / max_exact)
                         * (REL_BUCKETS - max_exact)).astype(jnp.int32)
    large = jnp.minimum(large, REL_BUCKETS - 1)
    return jnp.where(n < max_exact, n, large)

def moba_attention(q, k, v, rel_bias):
    B, H, S, Dh = q.shape
    BS = MOBA_BLOCK
    QC = MOBA_QCHUNK
    nb = -(-S // BS)
    pad = nb * BS - S
    kp = jnp.pad(k, ((0, 0), (0, 0), (0, pad), (0, 0))).reshape(B, H, nb, BS, Dh)
    vp = jnp.pad(v, ((0, 0), (0, 0), (0, pad), (0, 0))).reshape(B, H, nb, BS, Dh)
    scale = Dh ** -0.5

    pos = jnp.arange(S)
    qblk = pos // BS
    kmean = jnp.mean(kp.astype(jnp.float32), axis=3)
    gate = jnp.einsum('bhsd,bhnd->bhsn', q.astype(jnp.float32), kmean)
    past = jnp.arange(nb)[None, :] < qblk[:, None]
    gate = jnp.where(past, gate, NEG)
    kk = min(MOBA_TOPK, nb)
    _, top_idx = lax.top_k(gate, kk)
    valid = jnp.arange(kk)[None, :] < qblk[:, None]

    nc = S // QC
    q_c = q.reshape(B, H, nc, QC, Dh).transpose(2, 0, 1, 3, 4)
    idx_c = top_idx.reshape(B, H, nc, QC, kk).transpose(2, 0, 1, 3, 4)
    valid_c = valid.reshape(nc, QC, kk)
    bi = jnp.arange(B)[:, None, None]
    hi = jnp.arange(H)[None, :, None]
    hi4 = jnp.arange(H)[None, :, None, None]
    offs = jnp.arange(BS)

    def chunk(args):
        ci, qi, idx, vld = args
        qpos = ci * QC + jnp.arange(QC)
        own = (ci * QC) // BS
        k_own = lax.dynamic_index_in_dim(kp, own, axis=2, keepdims=False)
        v_own = lax.dynamic_index_in_dim(vp, own, axis=2, keepdims=False)
        kpos_own = own * BS + offs
        s_own = jnp.einsum('bhqd,bhkd->bhqk', qi, k_own).astype(jnp.float32) * scale
        s_own = s_own + rel_bias[:, rel_bucket(qpos[:, None] - kpos_own[None, :])].astype(jnp.float32)
        s_own = jnp.where(kpos_own[None, :] <= qpos[:, None], s_own, NEG)
        logits = []
        for j in range(kk):
            blk = idx[..., j]
            kg = kp[bi, hi, blk]
            s = jnp.einsum('bhqd,bhqkd->bhqk', qi, kg).astype(jnp.float32) * scale
            kpos = blk[..., None] * BS + offs
            bias = rel_bias[hi4, rel_bucket(qpos[None, None, :, None] - kpos)].astype(jnp.float32)
            logits.append(jnp.where(vld[None, None, :, j, None], s + bias, NEG))
        logits.append(s_own)
        p = jax.nn.softmax(jnp.concatenate(logits, axis=-1), axis=-1).astype(v.dtype)
        out = jnp.einsum('bhqk,bhkd->bhqd', p[..., kk * BS:], v_own)
        for j in range(kk):
            vg = vp[bi, hi, idx[..., j]]
            out = out + jnp.einsum('bhqk,bhqkd->bhqd', p[..., j * BS:(j + 1) * BS], vg)
        return out

    out = lax.map(chunk, (jnp.arange(nc), q_c, idx_c, valid_c))
    return out.transpose(1, 2, 0, 3, 4).reshape(B, H, S, Dh)

def stick_breaking_attention(q, k, v):
    B, H, S, Dh = q.shape
    QB = SB_QBLOCK
    nq = S // QB
    scale = Dh ** -0.5
    kpos = jnp.arange(S)
    q_b = q.reshape(B, H, nq, QB, Dh).transpose(2, 0, 1, 3, 4)

    def block(args):
        bidx, qi = args
        qpos = bidx * QB + jnp.arange(QB)
        z = jnp.einsum('bhqd,bhkd->bhqk', qi, k).astype(jnp.float32) * scale
        strict = kpos[None, :] < qpos[:, None]
        log_beta = jax.nn.log_sigmoid(z)
        log_1mb = jnp.where(strict, jax.nn.log_sigmoid(-z), 0.0)
        tail = lax.cumsum(log_1mb, axis=3, reverse=True) - log_1mb
        a = jnp.where(strict, jnp.exp(log_beta + tail), 0.0)
        return jnp.einsum('bhqk,bhkd->bhqd', a.astype(v.dtype), v)

    out = lax.map(block, (jnp.arange(nq), q_b))
    return out.transpose(1, 2, 0, 3, 4).reshape(B, H, S, Dh)

def conv_ffn(y, w_up, conv_w, conv_b, w_down):
    u = y @ w_up
    c = u.shape[-1]
    u = lax.conv_general_dilated(u, conv_w[:, None, :], window_strides=(1,),
                                 padding=[(CONV_WIDTH - 1, 0)],
                                 dimension_numbers=('NWC', 'WIO', 'NWC'),
                                 feature_group_count=c) + conv_b
    gate, val = jnp.split(u, 2, axis=-1)
    return (jax.nn.silu(gate) * val) @ w_down

def second_inputs(seed: int = 0) -> dict:
    key = jax.random.key(seed)
    ks = jax.random.split(key, 12)
    D, F = D_MODEL, D_FF_2
    f32 = jnp.float32
    return {
        "x": jax.random.normal(ks[0], (BATCH, SEQ, D), f32),
        "attn_norm": 1.0 + 0.02 * jax.random.normal(ks[1], (DEPTH_2, D), f32),
        "w_qkv": jax.random.normal(ks[2], (DEPTH_2, D, 3 * D), f32) * D ** -0.5,
        "w_o": jax.random.normal(ks[3], (DEPTH_2, D, D), f32) * D ** -0.5,
        "rel_bias": 0.5 * jax.random.normal(ks[4], (N_HEADS, REL_BUCKETS), f32),
        "ffn_norm": 1.0 + 0.02 * jax.random.normal(ks[5], (DEPTH_2, D), f32),
        "w_up": jax.random.normal(ks[6], (DEPTH_2, D, 2 * F), f32) * D ** -0.5,
        "conv_w": jax.random.normal(ks[7], (DEPTH_2, CONV_WIDTH, 2 * F), f32) * CONV_WIDTH ** -0.5,
        "conv_b": 0.02 * jax.random.normal(ks[8], (DEPTH_2, 2 * F), f32),
        "w_down": jax.random.normal(ks[9], (DEPTH_2, F, D), f32) * F ** -0.5,
        "final_norm": 1.0 + 0.02 * jax.random.normal(ks[10], (D,), f32),
    }

def second_block(x, attn_norm, w_qkv, w_o, rel_bias, ffn_norm, w_up, conv_w, conv_b, w_down, final_norm):
    B, S, D = x.shape
    h = x
    for i in range(DEPTH_2):
        y = rms_norm_2(h, attn_norm[i])
        qkv = (y @ w_qkv[i]).reshape(B, S, 3, N_HEADS, HEAD_DIM)
        q = qkv[:, :, 0].transpose(0, 2, 1, 3)
        k = qkv[:, :, 1].transpose(0, 2, 1, 3)
        v = qkv[:, :, 2].transpose(0, 2, 1, 3)
        if i % N_MIXERS == 0:
            o = moba_attention(q, k, v, rel_bias)
        else:
            o = stick_breaking_attention(q, k, v)
        h = h + o.transpose(0, 2, 1, 3).reshape(B, S, D) @ w_o[i]
        y = rms_norm_2(h, ffn_norm[i])
        h = h + conv_ffn(y, w_up[i], conv_w[i], conv_b[i], w_down[i])
    return rms_norm_2(h, final_norm)


def setup_inputs(seed=0):
    out = dict(first_inputs(seed))
    for name, value in second_inputs(seed + 1).items():
        if name != "x":
            out[name + "_2"] = value
    return out


def reference(
    x, positions, att_w_in, att_g_cq, att_w_uq, att_w_iq, att_g_ik, att_b_ik, att_w_o,
    hgrn_lb_logits, hgrn_w_in, hgrn_g_norm, hgrn_w_o, ffn_w_gate, ffn_w_up, ffn_w_down, ln_g,
    ln_b, attn_norm_2, w_qkv_2, w_o_2, rel_bias_2, ffn_norm_2, w_up_2, conv_w_2, conv_b_2,
    w_down_2, final_norm_2,
):
    x = first_block(
        x, positions, att_w_in, att_g_cq, att_w_uq, att_w_iq, att_g_ik, att_b_ik, att_w_o,
        hgrn_lb_logits, hgrn_w_in, hgrn_g_norm, hgrn_w_o, ffn_w_gate, ffn_w_up, ffn_w_down,
        ln_g, ln_b,
    )
    return second_block(
        x, attn_norm_2, w_qkv_2, w_o_2, rel_bias_2, ffn_norm_2, w_up_2, conv_w_2, conv_b_2,
        w_down_2, final_norm_2,
    )


_drawn_inputs = setup_inputs


def setup_inputs(seed=0):
    import zlib

    import numpy as np

    out = dict(_drawn_inputs(seed))
    spreads = {}
    factors = {'att_g_cq': 8.0,
     'att_g_ik': 8.0,
     'att_b_ik': 8.0,
     'hgrn_lb_logits': 4.135,
     'hgrn_g_norm': 8.0,
     'attn_norm_2': 7.371,
     'ffn_norm_2': 3.898,
     'conv_b_2': 3.909,
     'final_norm_2': 2.871}
    for name, (base, spread) in spreads.items():
        noise = np.random.default_rng([zlib.crc32(name.encode()), seed]).standard_normal(out[name].shape)
        drawn = base * np.exp(spread * noise) if base else spread * noise
        out[name] = __import__('jax').numpy.asarray(drawn.astype(out[name].dtype))
    for name, factor in factors.items():
        out[name] = (out[name] * factor).astype(out[name].dtype)
    return out
```

```python
from contextlib import ExitStack

import numpy as np

import concourse.bass as bass
from concourse import mybir

F32 = mybir.dt.float32
F32R = mybir.dt.float32r
I32 = mybir.dt.int32
U8 = mybir.dt.uint8
ALU = mybir.AluOpType
ACT = mybir.ActivationFunctionType
AXX = mybir.AxisListType.X

P = 128
T = 256
RT = T // P
D = 1024
KT = D // P
HALF = D // 2
RING = 3
UNIT = 2048

NQL, HQ, HD = 256, 16, 64
HI, DI = 8, 128
TOPK = 64
ROT, ROTI = 8, 16
IN_COLS = 648
C_K, C_V, C_KI, C_WI = 256, 384, 512, 640
FF = 2816
FC = 256
NFF = FF // FC
ALPHA = 4 ** 0.25
LN_EPS, RMS_EPS = 1e-5, 1e-6
HH, DH = 8, 128
CHUNK = 64
LEVELS = (32, 16, 8, 4, 2, 1)

BUCKETS, MAXD = 32, 128
REL_W = 384
FF2 = 2816

NEG = -1e30
CAUSAL_FILL = -2e38
TAKEN = -3e38

PI2_1 = 6.28125
PI2_2 = float(np.float32(np.floor((2 * np.pi - PI2_1) * 2 ** 20) / 2 ** 20))
PI2_3 = 2 * np.pi - PI2_1 - PI2_2
ROUND = 1.5 * 2 ** 23


def shape_constants():
    inv = [500000.0 ** (-np.arange(0, 2 * n, 2) / (2 * n)) for n in (ROT, ROTI)]
    inv = np.concatenate(inv).astype(np.float32)
    n = np.arange(T)
    exact = BUCKETS // 2
    large = exact + (np.log(np.maximum(n, 1).astype(np.float32) / np.float32(exact))
                     / np.float32(np.log(MAXD / exact)) * np.float32(BUCKETS - exact)).astype(np.int32)
    bucket = np.where(n < exact, n, np.minimum(large, BUCKETS - 1))
    hot = (bucket[::-1][None, :] == np.arange(BUCKETS)[:, None]).astype(np.float32)
    return inv.reshape(1, -1), np.ascontiguousarray(hot)


def weight_units(w):
    def up(m, c, n=512):
        v = m.rearrange("(t p) n -> p t n", p=P)
        return [[(0, 4, n, v[:, 4 * j:4 * j + 4, c:c + n])] for j in range(2)]

    def down(m, tiles):
        v = m.rearrange("(t p) n -> p t n", p=P)
        return [[(0, 2, D, v[:, 2 * j:2 * j + 2, :])] for j in range(tiles // 2)]

    w_in = w["att_w_in"]
    a = up(w_in, 0)
    a.append([(0, 8, IN_COLS - 512, w_in.rearrange("(t p) n -> p t n", p=P)[:, :, 512:IN_COLS])])
    a += down(w["att_w_iq"], 2) + down(w["att_w_uq"], 2) + down(w["att_w_o"], 8)
    h = []
    for c in (2, 3, 0, 1, 4, 5, 6, 7):
        h += up(w["hgrn_w_in"], 512 * c)
    h += down(w["hgrn_w_o"], 8)
    m = []
    for c in range(6):
        m += up(w["w_qkv_2"], 512 * c)
    m += down(w["w_o_2"], 8)
    return a, h, m


N_A, N_H, N_M, N_F = 9, 20, 16, 3 * NFF
U_IN, U_IQ, U_UQ, U_AO = 0, 3, 4, 5
U_F0 = N_A
U_H = U_F0 + N_F
U_HO = U_H + 16
U_F1 = U_H + N_H
U_M = U_F1 + N_F
U_MO = U_M + 12
U_F2 = U_M + N_M
U_ALL = U_F2 + N_F


class Chain:

    def __init__(self, eng, sem):
        self.eng, self.sem, self.n = eng, sem, 0

    def __call__(self, ins):
        self.n += 1
        ins.then_inc(self.sem, 1)
        self.eng.wait_ge(self.sem, self.n)


def build(nc, w, out):
    ctx = ExitStack()
    with ctx:
        def sb(name, shape, dt=F32):
            return ctx.enter_context(nc.sbuf_tensor(name, shape, dt))

        sems = {}

        def S(name):
            if name not in sems:
                sems[name] = ctx.enter_context(nc.semaphore(name))
            return sems[name]

        raw = sb("raw", [P, RING, UNIT])
        whi = sb("whi", [P, RING, UNIT], F32R)
        wlo = sb("wlo", [P, RING, UNIT], F32R)
        h = sb("h", [P, RT, D])
        xhi = sb("xhi", [P, KT, T], F32R)
        xlo = sb("xlo", [P, KT, T], F32R)
        fhi = sb("fhi", [P, 2, T], F32R)
        flo = sb("flo", [P, 2, T], F32R)
        gvec = sb("gvec", [P, D])
        bvec = sb("bvec", [P, D])
        ident = sb("ident", [P, P])
        nflip = sb("nflip", [P, P])
        stats = sb("stats", [P, RT, 2, 6])
        mv = sb("mv", [P, 4, 2])
        ve = sb("ve", [P, 16])
        rstd = sb("rstd", [P, 16])
        mhalf = sb("mhalf", [P, 16])
        work = sb("work", [P, 24500])
        maskt = sb("maskt", [P, 8, P], U8)
        cw = sb("cw", [P, 4, 2 * FF2 // P])
        cwi = sb("cwi", [P, 4, 2, 2])

        place = [0]

        def carve(*dims):
            n = int(np.prod(dims))
            a = work[:, place[0]:place[0] + n]
            place[0] += n
            assert place[0] <= 24500, place[0]
            if len(dims) == 1:
                return a
            names = "abcd"[:len(dims)]
            return a.rearrange(f"p ({' '.join(names)}) -> p {' '.join(names)}",
                               **{k: v for k, v in zip(names[1:], dims[1:])})

        PG = ctx.enter_context(nc.psum_tensor("PG", [P, 2, 512], F32))
        PA = ctx.enter_context(nc.psum_tensor("PA", [P, 4, 512], F32))
        TB = ctx.enter_context(nc.psum_tensor("TB", [P, 2, 512], F32))

        def flat(ap):
            return ap.rearrange("p a b -> p (a b)")

        qT = carve(KT, T)
        pr = carve(3, 384)
        pT = carve(3, 384)
        orow = carve(RT, D)
        amin = carve(HQ, 2)
        asum = carve(HQ, 2)
        arec = carve(HQ, 2)
        att_end = place[0]
        pin = carve(RT, IN_COLS)
        qi = carve(RT, D)
        qr = carve(RT, D)
        qiT = carve(HI, T)
        cqn = carve(RT, NQL)
        kd = carve(RT, 2, 2, HD)
        kT = carve(2, T)
        kiT = carve(T)
        sq = carve(RT, NQL)
        relu = carve(2, 384)
        score = carve(384)
        left = carve(384)
        mask = carve(384)
        m8 = carve(2, 8)
        wsc = carve(RT, HI)
        gcq = carve(NQL)
        gki = carve(DI)
        bki = carve(DI)
        posi = carve(RT)
        posf = carve(RT)
        inv = carve(24)
        ang = carve(RT, 2, 24)
        turns = carve(RT, 2, 24)
        trig = carve(RT, 2, 24)
        rt1 = carve(RT, 128)
        rt2 = carve(RT, 128)
        rt3 = carve(RT, 128)
        rt4 = carve(RT, 128)
        hot = carve(T)
        relrow = carve(BUCKETS)
        relT = carve(HQ)
        relv = carve(REL_W)
        cw4 = carve(4, P)
        place[0] = 0
        lb = carve(D)
        lb1 = carve(D)
        kr = carve(RT, D)
        lf = carve(RT, D)
        qh = carve(RT, D)
        vi = carve(RT, D)
        sg = carve(RT, D)
        bT = carve(HH, T)
        kTh = carve(HH, T)
        qTh = carve(HH, T)
        dl = lf.rearrange("p a b -> p (a b)").rearrange("p (a b) -> p a b", a=HH)
        dl2 = carve(HH, T)
        aT = carve(3, HH, P)
        ucum = carve(P)
        oh = qh
        sqh = kr
        ssq = carve(16)
        gno = carve(DH)
        place[0] = 0
        fe = carve(RT, FC)
        fh = carve(RT, FC)
        urow = carve(RT, 2 * FC)
        cv = carve(4, T)
        ce = carve(2, T)
        cgv = carve(2, T)
        fhT = carve(2, T)
        place[0] = att_end
        q2 = carve(RT, D)
        k2 = carve(RT, D)
        v2 = carve(RT, D)
        k2T = carve(KT, T)
        relb = carve(HQ, T)

        rel_dram = nc.dram_tensor("rel_scratch", [HQ, REL_W], F32, kind="Internal").ap()

        a_units, h_units, m_units = weight_units(w)
        units = {}
        for base, lst in ((U_IN, a_units), (U_H, h_units), (U_M, m_units)):
            for j, x in enumerate(lst):
                units[base + j] = x

        ev = {}
        n = 0
        for name, k in (("x", 4), ("c0", 2), ("cq", 1), ("ki", 2), ("qi", 4), ("q", 4), ("pt", HQ), ("ao", 4),
                        ("n1", 4), ("f0", 2 * NFF), ("n2", 4), ("hk", 4), ("hq", 4), ("ho", 4), ("n3", 4),
                        ("f1", 2 * NFF), ("y1", 4), ("q2", 4), ("k2", 4), ("pt2", HQ), ("ao2", 4),
                        ("y2", 4), ("f2", 2 * NFF)):
            ev[name] = n
            n += k

        def bc(row, n_):
            return bass.AP(row.tensor, row.offset, [[0, n_]] + [list(x) for x in row.ap])

        block = ctx.enter_context(nc.Block())

        VE = [4, 2, 2, 16, 2, 2, 2, 2, 2]
        GB = [("ln_g", 0, 0), ("ln_g", 0, 1), ("ln_g", 1, 0), ("ln_g", 1, 1), ("attn_norm_2", 0, None),
              ("ffn_norm_2", 0, None), ("final_norm_2", None, None)]
        GB_COUNT = np.cumsum([32, 32, 32, 32, 16, 16, 16]).tolist()

        @block.sync
        def _(sp):
            def slot_free(u):
                if u >= RING:
                    sp.wait_ge(S("w_lo"), u - RING + 1)

            def load(u):
                slot_free(u)
                for o, t, c, view in units[u]:
                    dst = raw[:, u % RING, o:o + t * c].rearrange("p (t c) -> p t c", t=t)
                    sp.dma_start(dst, view).then_inc(S(f"w_loaded{u % RING}"), 16)

            def load_up(slot, i, j, gate, val):
                dst = raw[:, slot, :].rearrange("p (t s c) -> p t s c", t=4, s=2)
                for s, m in enumerate((gate, val)):
                    v = m.rearrange("(t p) n -> p t n", p=P)[:, 4 * j:4 * j + 4, bass.ds(i * FC, FC)]
                    sp.dma_start(dst[:, :, s, :], v).then_inc(S(f"w_loaded{slot}"), 16)

            def load_down(slot, i, down):
                dst = raw[:, slot, :].rearrange("p (t c) -> p t c", t=2)
                v = down.rearrange("(g t p) n -> p g t n", p=P, t=2)[:, bass.ds(i, 1), :, :]
                sp.dma_start(dst, v.rearrange("p g t n -> p (g t) n")).then_inc(S(f"w_loaded{slot}"), 16)

            def ffn(U, gate, val, down):
                for j in range(2):
                    slot_free(U + j)
                    load_up((U + j) % RING, 0, j, gate, val)
                with sp.Fori(1, NFF) as i:
                    for j in range(2):
                        sp.wait_ge(S("w_lo"), i * 3 + (U - 3 + j))
                        load_up((U + 2 + j) % RING, i, j, gate, val)
                    sp.wait_ge(S("w_lo"), i * 3 + (U - 1))
                    load_down((U + 4) % RING, i - 1, down)
                slot_free(U + N_F - 1)
                load_down((U + N_F - 1) % RING, NFF - 1, down)

            hv = w["x"].rearrange("(r p) n -> p r n", p=P)
            for r in range(RT):
                sp.dma_start(h[:, r, :], hv[:, r, :]).then_inc(S("x_loaded"), 16)
            for u in range(N_A):
                load(u)
            ffn(U_F0, *w["ffn0"])
            for u in range(U_H, U_H + N_H):
                load(u)
            ffn(U_F1, *w["ffn1"])
            for u in range(U_M, U_M + N_M):
                load(u)
            ffn(U_F2, *w["ffn2"])
            ov = out.rearrange("(r p) n -> p r n", p=P)
            for r in range(RT):
                sp.wait_ge(S("norm"), 12 + r + 1)
                sp.dma_start(ov[:, r, :], h[:, r, :]).then_inc(S("stored"), 16)
            sp.wait_ge(S("stored"), 16 * RT)

        @block.gpsimd
        def _(pool):
            link = Chain(pool, S("pool_chain"))
            for r in range(RT):
                pool.dma_start(posi[:, r:r + 1].bitcast(I32),
                               w["positions"][r * P:(r + 1) * P].rearrange("(p o) -> p o", o=1)).then_inc(S("pos"), 16)
            pool.dma_start(inv, bc(w["inv"], P)).then_inc(S("pos"), 16)
            link(pool.memset(ident[:, :], 0.0))
            pool.affine_select(out=ident[:, :], in_=ident[:, :], compare_op=ALU.not_equal, fill=1.0, base=0,
                               pattern=[[-1, P]], channel_multiplier=1).then_inc(S("ident"), 1)
            for dst, src in ((gcq, w["att_g_cq"]), (gki, w["att_g_ik"]), (bki, w["att_b_ik"])):
                pool.dma_start(dst, bc(src, P)).then_inc(S("small"), 16)
            pool.dma_start(hot[0:BUCKETS, :], w["hot"]).then_inc(S("cst_loaded"), 16)
            pool.dma_start(relrow[0:HQ, :], w["rel_bias_2"]).then_inc(S("cst_loaded"), 16)
            pool.dma_start(cw4[0:44, 0:3, :], w["conv_w_2"].rearrange("j (c p) -> c j p", p=P))\
                .then_inc(S("cst_loaded"), 16)
            pool.dma_start(cw4[0:44, 3, :], w["conv_b_2"].rearrange("(c p) -> c p", p=P))\
                .then_inc(S("cst_loaded"), 16)
            link(pool.memset(nflip[:, :], 0.0))
            link(pool.affine_select(out=nflip[:, :], in_=nflip[:, :], compare_op=ALU.not_equal, fill=-1.0,
                                    base=-(P - 1), pattern=[[1, P]], channel_multiplier=1))
            link(pool.memset(mhalf[:, :], -0.5))

            def load_gb(k):
                name, a, b = GB[k]
                if k:
                    pool.wait_ge(S("norm"), 2 * k)
                if name == "ln_g":
                    pool.dma_start(gvec[:, :], bc(w["ln_g"][a, b], P)).then_inc(S("gb"), 16)
                    pool.dma_start(bvec[:, :], bc(w["ln_b"][a, b], P)).then_inc(S("gb"), 16)
                else:
                    pool.dma_start(gvec[:, :], bc(w[name], P)).then_inc(S("gb"), 16)

            def power(k):
                pool.wait_ge(S("ve"), k + 1)
                m = VE[k]
                pool.tensor_tensor(rstd[:, 0:m], ve[:, 0:m], mhalf[:, 0:m], ALU.pow).then_inc(S("rstd"), 1)

            load_gb(0)
            pool.wait_ge(S("relv"), 2)
            pool.dma_start(rel_dram, relv[0:HQ, :]).then_inc(S("rel_out"), 16)
            power(0)
            pool.wait_ge(S("iacc"), 2 * HI)
            for c in (0, 256):
                last = pool.affine_select(out=score[:, c:c + P], in_=score[:, c:c + P], compare_op=ALU.is_ge,
                                          fill=CAUSAL_FILL, base=0, pattern=[[-1, P]], channel_multiplier=1)
            last.then_inc(S("score_causal"), 1)
            pool.wait_ge(S("mask"), 1)
            for c in (0, 256):
                last = pool.affine_select(out=mask[:, c:c + P], in_=mask[:, c:c + P], compare_op=ALU.is_ge,
                                          fill=-NEG, base=0, pattern=[[-1, P]], channel_multiplier=1)
            last.then_inc(S("mask_causal"), 1)
            power(1)
            load_gb(1)
            power(2)
            load_gb(2)
            hf = dl2.rearrange("p a b -> p (a b)")[:, 0:P]
            for n_, m in enumerate((CHUNK,) + LEVELS):
                nb = P // (2 * m)
                link(pool.memset(hf, 0.0))
                link(pool.memset(hf.rearrange("p (b s m) -> p b s m", s=2, m=m)[:, :, 1, :], 1.0))
                v3 = hf.rearrange("p (b q) -> p b q", q=2 * m)
                link(pool.affine_select(out=v3, in_=v3, compare_op=ALU.is_ge, fill=0.0, base=0,
                                        pattern=[[-2 * m, nb], [0, 2 * m]], channel_multiplier=1))
                link(pool.affine_select(out=v3, in_=v3, compare_op=ALU.is_ge, fill=0.0, base=m - 1,
                                        pattern=[[2 * m, nb], [0, 2 * m]], channel_multiplier=-1))
                link(pool.tensor_copy(maskt[:, n_, :], hf))
            link(pool.tensor_copy(maskt[:, 7, :], ident[:, :]))
            link(pool.memset(ucum, 1.0))
            link(pool.affine_select(out=ucum, in_=ucum, compare_op=ALU.is_ge, fill=0.0, base=0,
                                    pattern=[[1, P]], channel_multiplier=-1))
            u3 = ucum[:, CHUNK:P]
            link(pool.affine_select(out=u3, in_=u3, compare_op=ALU.is_ge, fill=0.0, base=-CHUNK,
                                    pattern=[[0, CHUNK]], channel_multiplier=1))
            pool.dma_start(lb, bc(w["hgrn_lb_logits"][0], P)).then_inc(S("lb_loaded"), 16)
            pool.dma_start(lb1, bc(w["hgrn_lb_logits"][1], P)).then_inc(S("lb_loaded"), 16)
            pool.dma_start(gno, bc(w["hgrn_g_norm"], P)).then_inc(S("lb_loaded"), 16)
            pool.memset(aT[:, 0:2, :, :], 0.0).then_inc(S("hconst"), 1)

            pool.wait_ge(S("bT"), 4)
            for l, m in enumerate((CHUNK,) + LEVELS):
                d = (dl, dl2)[l % 2]
                if l >= 2:
                    pool.wait_ge(S("lv_full"), 4 * (l - 1))
                dv = d.rearrange("p h t -> p (h t)").rearrange("p (b s m) -> p b s m", s=2, m=m)
                bv = bT.rearrange("p h t -> p (h t)").rearrange("p (b s m) -> p b s m", s=2, m=m)
                nb = bv.shape[1]
                mid = bv[:, :, 0, m - 1:m].broadcast_to([P, nb, m])
                pool.tensor_tensor(dv[:, :, 0, :], mid, bv[:, :, 0, :], ALU.subtract).then_inc(S("lv_d"), 1)
                if l == 0:
                    pool.tensor_copy(dv[:, :, 1, :], bv[:, :, 1, :]).then_inc(S("lv_d"), 1)
                else:
                    pool.tensor_tensor(dv[:, :, 1, :], bv[:, :, 1, :], mid, ALU.subtract).then_inc(S("lv_d"), 1)
            pool.wait_ge(S("lv_full"), 4 * 6)
            dc = dl2.rearrange("p h (c t) -> p h c t", c=4)
            bvc = bT.rearrange("p h (c t) -> p h c t", c=4)
            end = lambda c: bvc[:, :, c, CHUNK - 1:CHUNK].broadcast_to([P, HH, CHUNK])
            link(pool.tensor_tensor(dc[:, :, 0, :], end(0), bvc[:, :, 0, :], ALU.subtract))
            pool.tensor_tensor(dc[:, :, 0, :], dc[:, :, 0, :], end(1), ALU.add).then_inc(S("lv_d"), 1)
            pool.tensor_tensor(dc[:, :, 1, :], end(1), bvc[:, :, 1, :], ALU.subtract).then_inc(S("lv_d"), 1)
            pool.tensor_copy(dc[:, :, 2, :], bvc[:, :, 2, :]).then_inc(S("lv_d"), 1)
            pool.tensor_tensor(dc[:, :, 3, :], bvc[:, :, 3, :], end(2), ALU.add).then_inc(S("lv_d"), 1)
            power(3)
            power(4)
            load_gb(3)
            power(5)
            load_gb(4)
            power(6)
            pool.wait_ge(S("rel_out"), 16)
            src = bass.AP(rel_dram.tensor, 0, [[1, P], [REL_W, HQ], [1, T]])
            pool.wait_ge(S("norm"), 10)
            pool.dma_start(relb, src).then_inc(S("relb"), 16)
            load_gb(5)
            power(7)
            load_gb(6)

            def gate_value(i):
                pool.wait_ge(S("t_free"), i * 2 + (ev["f2"] + 2))
                pool.tensor_tensor(cgv, cv[:, 0:2, :], cv[:, 2:4, :], ALU.mult).then_inc(S("cgv"), 1)

            gate_value(0)
            with pool.Fori(1, NFF) as i:
                gate_value(i)
            power(8)

        total = [0] * RING
        landed = []
        for u in range(U_ALL + RING):
            two = any(U <= u < U + N_F and (u - U < 2 or ((u - U) % 3 != 1 and u != U + N_F - 1))
                      for U in (U_F0, U_F1, U_F2))
            total[u % RING] += 32 if two else 16
            landed.append(total[u % RING])

        def unit_len(u):
            return 8 * (IN_COLS - 512) if u == 2 else UNIT

        def hi(u, i=0):
            if u >= U_ALL:
                return
            s = u % RING
            step = landed[u + RING] - landed[u]
            nc.scalar.wait_ge(S(f"w_loaded{s}"), i * step + landed[u])
            if u >= RING:
                nc.scalar.wait_ge(S("w_used"), i * 3 + (u - RING + 1))
            n_ = unit_len(u)
            nc.scalar.activation(whi[:, s, 0:n_], raw[:, s, 0:n_], ACT.Copy).then_inc(S("w_hi"), 1)

        def lo(u, i=0):
            if u >= U_ALL:
                return
            s = u % RING
            n_ = unit_len(u)
            nc.vector.wait_ge(S("w_hi"), i * 3 + (u + 1))
            nc.vector.tensor_tensor(wlo[:, s, 0:n_], raw[:, s, 0:n_], whi[:, s, 0:n_].bitcast(F32),
                                    ALU.subtract).then_inc(S("w_lo"), 1)

        @block.scalar
        def _(act):
            ac = nc.scalar
            link = Chain(act, S("act_chain"))

            def turned(e):
                act.wait_ge(S("t_full"), e + 1)

            def full(u):
                act.wait_ge(S("w_used"), u + 1)

            def x_hi(name, k=4):
                for g in range(k):
                    e = ev[name] + g
                    turned(e)
                    ac.activation(flat(xhi[:, 2 * g:2 * g + 2, :]), TB[:, e % 2, :], ACT.Copy)\
                      .then_inc(S("x_hi"), 1)

            def copy_turned(name, dst):
                for g in range(4):
                    e = ev[name] + g
                    turned(e)
                    ac.activation(flat(dst[:, 2 * g:2 * g + 2, :]), TB[:, e % 2, :], ACT.Copy)\
                      .then_inc(S("t_free"), 1)

            def attention(tag):
                for hd in range(HQ):
                    act.wait_ge(S("amin" + tag), 2 * hd + 2)
                    if hd >= 3:
                        act.wait_ge(S("t_full"), ev["pt" + tag] + hd - 2)
                    for r, (a, b) in enumerate(((0, 128), (128, 384))):
                        ac.activation(pr[:, hd % 3, a:b], PA[:, hd % 4, a:b], ACT.Exp, scale=-1.0,
                                      bias=amin[:, hd, r:r + 1], accum_out=asum[:, hd, r:r + 1])\
                          .then_inc(S("prob" + tag), 1)

            def ffn(k, U, name):
                T0 = ev[name]

                def f_hi(i):
                    for f in range(2):
                        act.wait_ge(S("t_full"), i * 2 + (T0 + f + 1))
                        ac.activation(fhi[:, f, :], TB[:, (T0 + f) % 2, 0:T], ACT.Copy).then_inc(S("x_hi"), 1)

                def exps(i, u):
                    act.wait_ge(S("w_used"), i * 3 + (u + 1))
                    if not (k == 0 and isinstance(i, int) and i == 0):
                        act.wait_ge(S("hidden"), i + k * NFF)
                    ac.activation(fe, PG[:, :, 0:FC], ACT.Exp, scale=-1.0).then_inc(S("fexp"), 1)

                def step(i):
                    at = (lambda u: hi(u, i)) if not isinstance(i, int) else (lambda u: hi(u + 3 * i))
                    f_hi(i - 1)
                    at(U + 2)
                    exps(i, U)
                    at(U + 3)
                    at(U + 4)

                hi(U + 3)
                full(U + 1)
                exps(0, U)
                hi(U + 4)
                with act.Fori(1, NFF - 1) as i:
                    step(i)
                step(NFF - 1)
                f_hi(NFF - 1)

            act.wait_ge(S("ang"), 1)
            ac.activation(trig.rearrange("p a b c -> p (a b c)"), ang.rearrange("p a b c -> p (a b c)"),
                          ACT.Sin).then_inc(S("trig"), 1)
            x_hi("x")
            for u in range(3):
                hi(u)
            full(1)
            ac.activation(pin[:, :, 0:512], PG[:, :, :], ACT.Copy).then_inc(S("pin"), 1)
            act.wait_ge(S("pin"), 1)
            for r in range(RT):
                ac.activation(sq[:, r, :], pin[:, r, 0:NQL], ACT.Square,
                              accum_out=ve[:, 8 + r:9 + r]).then_inc(S("ssq"), 1)
            hi(3)
            hi(4)
            turned(ev["cq"])
            ac.activation(flat(xhi[:, 0:2, :]), TB[:, ev["cq"] % 2, :], ACT.Copy).then_inc(S("x_hi"), 1)
            hi(5)
            full(U_IQ)
            ac.activation(qi[:, 0, :], flat(PA[:, 0:2, :]), ACT.Copy).then_inc(S("qi_a"), 1)
            hi(6)
            full(U_UQ)
            ac.activation(qr[:, 0, :], flat(PA[:, 0:2, :]), ACT.Copy, scale=-HD ** -0.5)\
              .then_inc(S("q_a"), 1)
            hi(7)
            copy_turned("qi", qiT)
            copy_turned("q", qT)
            for hd in range(HI):
                act.wait_ge(S("iscore"), hd + 1)
                if hd >= 2:
                    act.wait_ge(S("iacc"), 2 * (hd - 1))
                ac.activation(relu[:, hd % 2, :], PA[:, hd % 4, 0:384], ACT.Relu).then_inc(S("relu"), 1)
            attention("")
            x_hi("ao")
            for u in range(8, 12):
                hi(u)
            x_hi("n1")
            ffn(0, U_F0, "f0")
            hi(U_H + 2)
            x_hi("n2")
            act.wait_ge(S("lb_diff"), 1)
            ac.activation(lb1, lb1, ACT.Exp).then_inc(S("lb_exp"), 1)

            def sig_exp(dst, j, ps, what):
                ac.activation(dst[:, :, j * HALF:(j + 1) * HALF], ps, ACT.Exp, scale=-1.0)\
                  .then_inc(S(what), 1)

            hi(U_H + 3)
            full(U_H + 1)
            sig_exp(kr, 0, PG[:, :, :], "f_exp")
            hi(U_H + 4)
            hi(U_H + 5)
            full(U_H + 3)
            sig_exp(kr, 1, PA[:, 0:2, :], "f_exp")
            hi(U_H + 6)
            hi(U_H + 7)
            full(U_H + 5)
            sig_exp(qh, 0, PA[:, 2:4, :], "q_exp")
            hi(U_H + 8)
            for j in range(2):
                act.wait_ge(S("fg"), j + 1)
                lv = lf[:, :, j * HALF:(j + 1) * HALF]
                ac.activation(lv, lv, ACT.Ln).then_inc(S("logf"), 1)
            full(U_H + 7)
            sig_exp(qh, 1, PG[:, :, :], "q_exp")
            hi(U_H + 9)
            hi(U_H + 10)
            for b in range(4):
                act.wait_ge(S("cum"), b + 1)
                ac.activation(flat(bT[:, 2 * b:2 * b + 2, :]), PA[:, b, :], ACT.Copy).then_inc(S("bT"), 1)
            copy_turned("hk", kTh)
            copy_turned("hq", qTh)

            def level_exp(l):
                act.wait_ge(S("lv_d"), 2 * l + 2)
                d = flat((dl, dl2)[l % 2])
                ac.activation(d, d, ACT.Exp).then_inc(S("lv_e"), 1)

            level_exp(0)
            hi(U_H + 11)
            full(U_H + 9)
            ac.activation(vi[:, :, 0:HALF], PG[:, :, :], ACT.Copy).then_inc(S("vi"), 1)
            hi(U_H + 12)
            level_exp(1)
            hi(U_H + 13)
            full(U_H + 11)
            ac.activation(vi[:, :, HALF:D], PG[:, :, :], ACT.Copy).then_inc(S("vi"), 1)
            hi(U_H + 14)
            level_exp(2)
            hi(U_H + 15)
            full(U_H + 13)
            sig_exp(sg, 0, PG[:, :, :], "g_exp")
            hi(U_H + 16)
            level_exp(3)
            hi(U_H + 17)
            full(U_H + 15)
            sig_exp(sg, 1, PG[:, :, :], "g_exp")
            hi(U_H + 18)
            for l in range(4, 7):
                level_exp(l)
            act.wait_ge(S("lv_d"), 14 + 4)
            ac.activation(flat(dl2), flat(dl2), ACT.Exp).then_inc(S("lv_e"), 1)
            for b in range(4):
                act.wait_ge(S("ho"), b + 1)
                ac.activation(flat(sqh)[:, b * 512:(b + 1) * 512], PA[:, b, :], ACT.Square)\
                  .then_inc(S("ho_sq"), 1)
            x_hi("ho")
            for u in range(U_HO + 3, U_F1 + 3):
                hi(u)
            x_hi("n3")
            ffn(1, U_F1, "f1")
            hi(U_M + 2)
            x_hi("y1")

            dsts = (q2, q2, k2, k2, v2, v2)
            banks = (PG[:, :, :], PA[:, 0:2, :], PA[:, 2:4, :])
            for c in range(6):
                hi(U_M + 2 * c + 3)
                full(U_M + 2 * c + 1)
                dst = dsts[c][:, :, (c % 2) * HALF:(c % 2 + 1) * HALF]
                ac.activation(dst, banks[c % 3], ACT.Copy, scale=-HD ** -0.5 if c < 2 else 1.0)\
                  .then_inc(S("qkv"), 1)
                hi(U_M + 2 * c + 4)
            copy_turned("q2", qT)
            copy_turned("k2", k2T)
            attention("2")
            x_hi("ao2")
            for u in range(U_MO + 3, U_F2 + 3):
                hi(u)
            x_hi("y2")

            U, T0 = U_F2, ev["f2"]

            def rows_out(i, u):
                act.wait_ge(S("w_used"), i * 3 + (u + 1))
                if not isinstance(i, int) or i > 0:
                    act.wait_ge(S("t_full"), i * 2 + T0)
                ac.activation(urow, PG[:, :, :], ACT.Copy).then_inc(S("urow"), 1)

            def conv_first(i):
                act.wait_ge(S("cwi"), i + 1)
                if not isinstance(i, int) or i > 0:
                    act.wait_ge(S("hidden_t"), i)
                for s in range(2):
                    act.wait_ge(S("t_full"), i * 2 + (T0 + s + 1))
                    for f in range(2):
                        ac.activation(cv[:, 2 * s + f, :], TB[:, (T0 + s) % 2, f * T:(f + 1) * T], ACT.Identity,
                                      scale=cwi[:, 2, s, f:f + 1], bias=cwi[:, 3, s, f:f + 1])\
                          .then_inc(S("conv0"), 1)
                act.wait_ge(S("t_free"), i * 2 + (T0 + 2))
                ac.activation(ce, cv[:, 0:2, :], ACT.Exp, scale=-1.0).then_inc(S("cexp"), 1)

            def conv_hi(i):
                act.wait_ge(S("hidden_t"), i + 1)
                if not isinstance(i, int) or i > 0:
                    act.wait_ge(S("w_used"), i * 3 + (U + 2))
                ac.activation(fhi[:, :, :], fhT, ACT.Copy).then_inc(S("c_hi"), 1)

            def cstep(i):
                at = (lambda u: hi(u, i)) if not isinstance(i, int) else (lambda u: hi(u + 3 * i))
                conv_first(i - 1)
                at(U + 2)
                conv_hi(i - 1)
                rows_out(i, U)
                at(U + 3)
                at(U + 4)

            hi(U + 3)
            rows_out(0, U + 1)
            hi(U + 4)
            cstep(1)
            with act.Fori(2, NFF - 1) as i:
                cstep(i)
            cstep(NFF - 1)
            conv_first(NFF - 1)
            conv_hi(NFF - 1)

        @block.vector
        def _(vec):
            ve_ = nc.vector
            link = Chain(vec, S("vec_chain"))

            def turned(e):
                vec.wait_ge(S("t_full"), e + 1)

            def full(u):
                vec.wait_ge(S("w_used"), u + 1)

            nxhi = [0]

            def lo_of_bank(dst, e, src_hi):
                nxhi[0] += 1
                vec.wait_ge(S("x_hi"), nxhi[0])
                ve_.tensor_tensor(dst, TB[:, e % 2, 0:dst.shape[1]], src_hi.bitcast(F32), ALU.subtract)\
                   .then_inc(S("t_free"), 1)

            def x_lo(name, k=4):
                for g in range(k):
                    lo_of_bank(flat(xlo[:, 2 * g:2 * g + 2, :]), ev[name] + g, flat(xhi[:, 2 * g:2 * g + 2, :]))

            def rope(x, heads, half, c0):
                n_ = heads * half
                cos = trig[:, :, 0, c0:c0 + half].unsqueeze(2).broadcast_to([P, RT, heads, half])
                sin = trig[:, :, 1, c0:c0 + half].unsqueeze(2).broadcast_to([P, RT, heads, half])
                x1, x2 = x[:, :, :, 0:half], x[:, :, :, half:2 * half]
                r = [t[:, :, 0:n_].rearrange("p r (g c) -> p r g c", g=heads) for t in (rt1, rt2, rt3, rt4)]
                ve_.tensor_tensor(r[0], x1, cos, ALU.mult)
                ve_.tensor_tensor(r[1], x2, sin, ALU.mult)
                ve_.tensor_tensor(r[2], x2, cos, ALU.mult)
                link(ve_.tensor_tensor(r[3], x1, sin, ALU.mult))
                ve_.tensor_tensor(x1, r[0], r[1], ALU.subtract)
                return ve_.tensor_tensor(x2, r[2], r[3], ALU.add)

            def attention(tag):
                o_at = lambda g: PG[:, g % 2, :].rearrange("p (h r c) -> p h r c", h=4, r=2)

                def minima(hd):
                    vec.wait_ge(S("logit" + tag), hd + 1)
                    for r, (a, b) in enumerate(((0, 128), (128, 384))):
                        ve_.tensor_reduce(amin[:, hd, r:r + 1], PA[:, hd % 4, a:b], AXX, ALU.min)\
                           .then_inc(S("amin" + tag), 1)

                def turn_out(hd):
                    e = ev["pt" + tag] + hd
                    turned(e)
                    if hd >= 3:
                        vec.wait_ge(S("pv" + tag), hd - 2)
                    ve_.tensor_copy(pT[:, hd % 3, :], TB[:, e % 2, 0:384]).then_inc(S("t_free"), 1)

                def outputs(g):
                    vec.wait_ge(S("prob" + tag), 2 * (4 * g + 4))
                    link(ve_.reciprocal(arec[:, 4 * g:4 * g + 4, :], asum[:, 4 * g:4 * g + 4, :]))
                    vec.wait_ge(S("pv" + tag), 4 * g + 4)
                    for r in range(RT):
                        o = orow[:, r, 256 * g:256 * g + 256].rearrange("p (h c) -> p h c", h=4)
                        rb = arec[:, 4 * g:4 * g + 4, r:r + 1].broadcast_to([P, 4, HD])
                        ve_.tensor_tensor(o, o_at(g)[:, :, r, :], rb, ALU.mult).then_inc(S("orow" + tag), 1)

                for i in range(HQ + 3):
                    if i < HQ:
                        minima(i)
                    if 1 <= i <= HQ:
                        turn_out(i - 1)
                    if i >= 6 and (i - 6) % 4 == 0 and (i - 6) // 4 < 3:
                        outputs((i - 6) // 4)
                outputs(3)

            def residual(scale, u):
                full(u)
                for r in range(RT):
                    for f in range(2):
                        hv_ = h[:, r, f * HALF:(f + 1) * HALF]
                        ins = ve_.scalar_tensor_tensor(out=hv_, in0=hv_, scalar=scale, in1=PA[:, 2 * r + f, :],
                                                       op0=ALU.mult, op1=ALU.add)
                link(ins)

            nrm = [0]

            def moments(k):
                for r in range(RT):
                    for f in range(2):
                        ins = ve_.bn_stats(stats[:, r, f, :], h[:, r, f * HALF:(f + 1) * HALF])
                link(ins)
                for r in range(RT):
                    ins = ve_.bn_aggr(mv[:, r, :], stats[:, r, :, :].rearrange("p a b -> p (a b)"))
                link(ins)

            def layer_norm(k, call):
                moments(k)
                ve_.tensor_scalar(ve[:, 0:2], mv[:, 0:2, 1], LN_EPS, None, ALU.add).then_inc(S("ve"), 1)
                vec.wait_ge(S("rstd"), call + 1)
                vec.wait_ge(S("gb"), GB_COUNT[k])
                for r in range(RT):
                    link(ve_.tensor_scalar(h[:, r, :], h[:, r, :], mv[:, r, 0:1], rstd[:, r:r + 1],
                                           ALU.subtract, ALU.mult))
                    link(ve_.tensor_tensor(h[:, r, :], h[:, r, :], gvec[:, :], ALU.mult))
                    ve_.tensor_tensor(h[:, r, :], h[:, r, :], bvec[:, :], ALU.add).then_inc(S("norm"), 1)
                vec.wait_ge(S("norm"), 2 * k + 2)

            def rms_norm(k, call, dst):
                moments(k)
                link(ve_.tensor_tensor(ve[:, 8:10], mv[:, 0:2, 0], mv[:, 0:2, 0], ALU.mult))
                ve_.scalar_tensor_tensor(out=ve[:, 0:2], in0=ve[:, 8:10], scalar=RMS_EPS, in1=mv[:, 0:2, 1],
                                         op0=ALU.add, op1=ALU.add).then_inc(S("ve"), 1)
                vec.wait_ge(S("rstd"), call + 1)
                vec.wait_ge(S("gb"), GB_COUNT[k])
                for r in range(RT):
                    ve_.scalar_tensor_tensor(out=dst[:, r, :], in0=h[:, r, :], scalar=rstd[:, r:r + 1],
                                             in1=gvec[:, :], op0=ALU.mult, op1=ALU.mult).then_inc(S("norm"), 1)

            def ffn(k, U, name):
                T0 = ev[name]
                x0 = nxhi[0]

                def f_lo(i):
                    for f in range(2):
                        vec.wait_ge(S("x_hi"), i * 2 + (x0 + f + 1))
                        ve_.tensor_tensor(flo[:, f, :], TB[:, (T0 + f) % 2, 0:T], fhi[:, f, :].bitcast(F32),
                                          ALU.subtract).then_inc(S("t_free"), 1)

                def hidden(i):
                    vec.wait_ge(S("fexp"), i + (k * NFF + 1))
                    n0 = i * 3 + c0
                    for j, ins in enumerate((
                            lambda: ve_.tensor_scalar(fe, fe, 1.0, None, ALU.add),
                            lambda: ve_.reciprocal(fe, fe),
                            lambda: ve_.tensor_tensor(fh, PG[:, :, 0:FC], fe, ALU.mult))):
                        ins().then_inc(S("vec_chain"), 1)
                        vec.wait_ge(S("vec_chain"), n0 + (j + 1))
                    ve_.tensor_tensor(fh, fh, PG[:, :, FC:2 * FC], ALU.mult).then_inc(S("hidden"), 1)

                def step(i):
                    at = (lambda u: lo(u, i)) if not isinstance(i, int) else (lambda u: lo(u + 3 * i))
                    f_lo(i - 1)
                    at(U + 2)
                    hidden(i)
                    at(U + 3)
                    at(U + 4)

                c0 = link.n
                lo(U + 3)
                hidden(0)
                lo(U + 4)
                with vec.Fori(1, NFF - 1) as i:
                    step(i)
                step(NFF - 1)
                f_lo(NFF - 1)
                link.n += 3 * NFF
                nxhi[0] += 2 * NFF

            vec.wait_ge(S("pos"), 48)
            link(ve_.tensor_copy(posf, posi.bitcast(I32)))
            for r in range(RT):
                for s in range(2):
                    ins = ve_.tensor_scalar(ang[:, r, s, :], inv, posf[:, r:r + 1], None, ALU.mult)
            link(ins)
            for s in range(2):
                ins = ve_.tensor_scalar(turns[:, :, s, :], ang[:, :, s, :], 1 / (2 * np.pi), 0.25 * (1 - s),
                                        ALU.mult, ALU.add)
            link(ins)
            link(ve_.tensor_scalar(turns, turns, ROUND, ROUND, ALU.add, ALU.subtract))
            for part in (PI2_1, PI2_2, PI2_3):
                a2, t2 = (z.rearrange("p a b c -> p (a b c)") for z in (ang, turns))
                link(ve_.scalar_tensor_tensor(out=a2, in0=t2, scalar=-part, in1=a2, op0=ALU.mult, op1=ALU.add))
            link(ve_.tensor_scalar(ang[:, :, 0, :], ang[:, :, 0, :], np.pi / 2, None, ALU.add))
            lim = float(np.float32(3.1415925))
            ve_.tensor_scalar(ang, ang, lim, -lim, ALU.min, ALU.max).then_inc(S("ang"), 1)

            x_lo("x")
            for u in range(3):
                lo(u)
            e = ev["c0"]
            turned(e)
            ve_.tensor_copy(relT[0:BUCKETS, :], TB[0:BUCKETS, e % 2, 0:HQ]).then_inc(S("t_free"), 1)
            turned(e + 1)
            ve_.tensor_copy(cw[:, :, :], TB[:, (e + 1) % 2, 0:176].rearrange("p (j c) -> p j c", j=4))\
               .then_inc(S("t_free"), 1)
            vec.wait_ge(S("reldist"), 1)
            ve_.tensor_copy(relv[0:HQ, 0:T], PA[0:HQ, 2, 0:T]).then_inc(S("relv"), 1)
            ve_.memset(relv[0:HQ, T:REL_W], NEG).then_inc(S("relv"), 1)
            full(2)
            link(ve_.tensor_copy(pin[:, :, 512:IN_COLS], PA[:, 0:2, 0:IN_COLS - 512]))
            vec.wait_ge(S("small"), 48)
            for r in range(RT):
                ins = ve_.bn_stats(stats[:, r, 0, :], pin[:, r, C_KI:C_WI])
            link(ins)
            for r in range(RT):
                ins = ve_.bn_aggr(mv[:, 2 + r, :], stats[:, r, 0, :])
            link(ins)
            ve_.tensor_scalar(ve[:, 2:4], mv[:, 2:4, 1], LN_EPS, None, ALU.add)
            vec.wait_ge(S("ssq"), RT)
            ve_.tensor_scalar(ve[:, 0:2], ve[:, 8:10], 1.0 / NQL, RMS_EPS, ALU.mult, ALU.add).then_inc(S("ve"), 1)
            ve_.tensor_scalar(wsc, pin[:, :, C_WI:IN_COLS], HI ** -0.5 * DI ** -0.5, None, ALU.mult)
            vec.wait_ge(S("rstd"), 1)
            vec.wait_ge(S("pin"), 1)
            for r in range(RT):
                ins = ve_.scalar_tensor_tensor(out=cqn[:, r, :], in0=pin[:, r, 0:NQL], scalar=rstd[:, r:r + 1],
                                               in1=gcq, op0=ALU.mult, op1=ALU.mult)
            ins.then_inc(S("cqn"), 1)
            for r in range(RT):
                kv_ = pin[:, r, C_KI:C_WI]
                link(ve_.tensor_scalar(kv_, kv_, mv[:, 2 + r, 0:1], rstd[:, 2 + r:3 + r], ALU.subtract, ALU.mult))
                link(ve_.tensor_tensor(kv_, kv_, gki, ALU.mult))
                link(ve_.tensor_tensor(kv_, kv_, bki, ALU.add))
            lo_of_bank(flat(xlo[:, 0:2, :]), ev["cq"], flat(xhi[:, 0:2, :]))
            vec.wait_ge(S("trig"), 1)
            link(rope(pin[:, :, C_KI:C_WI].rearrange("p r (g c) -> p r g c", g=1), 1, ROTI, ROT))
            link(rope(pin[:, :, C_K:C_V].rearrange("p r (g c) -> p r g c", g=2), 2, ROT, 0))
            for r in range(RT):
                for c in range(2):
                    ins = ve_.tensor_copy(kd[:, r, :, c, :],
                                          pin[:, r, C_K:C_V].rearrange("p (g c) -> p g c", g=2))
            ins.then_inc(S("kd"), 1)
            lo(3)
            lo(4)
            lo(5)
            full(U_IQ)
            ve_.tensor_copy(qi[:, 1, :], flat(PA[:, 2:4, :])).then_inc(S("qi_b"), 1)
            vec.wait_ge(S("qi_b"), 1)
            vec.wait_ge(S("qi_a"), 1)
            rope(qi.rearrange("p r (g c) -> p r g c", g=HI), HI, ROTI, ROT).then_inc(S("qi_r"), 1)
            lo(6)
            e = ev["ki"]
            turned(e)
            ve_.tensor_copy(flat(kT), TB[:, e % 2, :]).then_inc(S("t_free"), 1)
            turned(e + 1)
            ve_.tensor_copy(kiT, TB[:, (e + 1) % 2, 0:T]).then_inc(S("t_free"), 1)
            full(U_UQ)
            link(ve_.tensor_scalar(qr[:, 1, :], flat(PA[:, 2:4, :]), -HD ** -0.5, None, ALU.mult))
            vec.wait_ge(S("q_a"), 1)
            rope(qr.rearrange("p r (g c) -> p r g c", g=HQ), HQ, ROT, 0).then_inc(S("q_r"), 1)
            lo(7)
            for hd in range(HI):
                vec.wait_ge(S("relu"), hd + 1)
                if hd:
                    vec.wait_ge(S("iacc"), 2 * hd)
                for r, (a, b) in enumerate(((0, 128), (128, 384))):
                    src, dst = relu[:, hd % 2, a:b], score[:, a:b]
                    wv = wsc[:, r, hd:hd + 1]
                    if hd == 0:
                        ins = ve_.tensor_scalar(dst, src, wv, None, ALU.mult)
                    else:
                        ins = ve_.scalar_tensor_tensor(out=dst, in0=src, scalar=wv, in1=dst,
                                                       op0=ALU.mult, op1=ALU.add)
                    ins.then_inc(S("iacc"), 1)
            vec.wait_ge(S("score_causal"), 1)
            for k in range(TOPK // 8):
                src = score if k == 0 else left
                for r, (a, b) in enumerate(((0, 128), (128, 384))):
                    ins = ve_.max(m8[:, r, :], src[:, a:b])
                link(ins)
                for r, (a, b) in enumerate(((0, 128), (128, 384))):
                    ins = ve_.match_replace(left[:, a:b], m8[:, r, :], src[:, a:b], TAKEN)
                link(ins)
            ve_.tensor_scalar(mask, left, (CAUSAL_FILL + TAKEN) / 2, -NEG, ALU.is_gt, ALU.mult)\
               .then_inc(S("mask"), 1)
            attention("")
            x_lo("ao")
            for u in range(8, 12):
                lo(u)
            residual(ALPHA, U_AO + 3)
            layer_norm(0, 1)
            x_lo("n1")
            ffn(0, U_F0, "f0")
            residual(ALPHA, U_F0 + N_F - 1)
            layer_norm(1, 2)
            x_lo("n2")
            lo(U_H + 2)

            vec.wait_ge(S("hconst"), 1)
            vec.wait_ge(S("lb_loaded"), 48)
            ve_.tensor_tensor(lb1, lb, lb1, ALU.subtract).then_inc(S("lb_diff"), 1)
            vec.wait_ge(S("lb_exp"), 1)
            link(ve_.tensor_scalar(lb1, lb1, 1.0, None, ALU.add))
            link(ve_.reciprocal(lb, lb1))
            link(ve_.tensor_scalar(lb1, lb, -1.0, 1.0, ALU.mult, ALU.add))

            def forget(j):
                cols = slice(j * HALF, (j + 1) * HALF)
                v = kr[:, :, cols]
                lbb = lb[:, cols].unsqueeze(1).broadcast_to([P, RT, HALF])
                lb1b = lb1[:, cols].unsqueeze(1).broadcast_to([P, RT, HALF])
                vec.wait_ge(S("f_exp"), j + 1)
                link(ve_.tensor_scalar(v, v, 1.0, None, ALU.add))
                link(ve_.reciprocal(v, v))
                link(ve_.tensor_tensor(v, v, lb1b, ALU.mult))
                link(ve_.tensor_tensor(v, v, lbb, ALU.add))
                ve_.tensor_scalar(lf[:, :, cols], v, 2.0 ** -63, None, ALU.max).then_inc(S("fg"), 1)
                ve_.tensor_scalar(v, v, -1.0, 1.0, ALU.mult, ALU.add).then_inc(S("kr"), 1)

            def silu(dst, j, ps, what, k, done):
                v = dst[:, :, j * HALF:(j + 1) * HALF]
                vec.wait_ge(S(what), k)
                link(ve_.tensor_scalar(v, v, 1.0, None, ALU.add))
                link(ve_.reciprocal(v, v))
                ve_.tensor_tensor(v, v, ps, ALU.mult).then_inc(S(done), 1)

            lo(U_H + 3)
            forget(0)
            lo(U_H + 4)
            lo(U_H + 5)
            forget(1)
            lo(U_H + 6)
            lo(U_H + 7)
            silu(qh, 0, PA[:, 2:4, :], "q_exp", 1, "qh")
            lo(U_H + 8)
            silu(qh, 1, PG[:, :, :], "q_exp", 2, "qh")
            lo(U_H + 9)
            lo(U_H + 10)

            def products(l):
                vec.wait_ge(S("lv_e"), l + 1)
                m = ((CHUNK,) + LEVELS)[l]
                d, k_, q_ = (flat(z).rearrange("p (b s m) -> p b s m", s=2, m=m)
                             for z in ((dl, dl2)[l % 2], kTh, qTh))
                ve_.tensor_tensor(d[:, :, 0, :], d[:, :, 0, :], k_[:, :, 0, :], ALU.mult).then_inc(S("lv_x"), 1)
                ve_.tensor_tensor(d[:, :, 1, :], d[:, :, 1, :], q_[:, :, 1, :], ALU.mult).then_inc(S("lv_x"), 1)

            def take(l):
                for b in range(4):
                    vec.wait_ge(S("lv_full"), 4 * l + b + 1)
                    mk = maskt[:, l, :].unsqueeze(1).broadcast_to([P, 2, P])
                    for r in range(RT):
                        ins = ve_.copy_predicated(aT[:, r, 2 * b:2 * b + 2, :], mk,
                                                  PA[:, b, r * 256:(r + 1) * 256].rearrange("p (h c) -> p h c", h=2))
                    ins.then_inc(S("lv_taken"), 1)

            vec.wait_ge(S("t_free"), ev["hq"] + 4)
            products(0)
            lo(U_H + 11)
            lo(U_H + 12)
            products(1)
            take(0)
            lo(U_H + 13)
            lo(U_H + 14)
            products(2)
            take(1)
            lo(U_H + 15)
            silu(sg, 0, PG[:, :, :], "g_exp", 1, "sg0")
            lo(U_H + 16)
            products(3)
            take(2)
            lo(U_H + 17)
            silu(sg, 1, PG[:, :, :], "g_exp", 2, "sg0")
            lo(U_H + 18)
            products(4)
            take(3)
            products(5)
            take(4)
            products(6)
            take(5)
            vec.wait_ge(S("lv_e"), 8)
            ve_.tensor_tensor(dl2[:, :, 0:P], dl2[:, :, 0:P], kTh[:, :, 0:P], ALU.mult).then_inc(S("lv_x"), 1)
            ve_.tensor_tensor(dl2[:, :, P:T], dl2[:, :, P:T], qTh[:, :, P:T], ALU.mult).then_inc(S("lv_x"), 1)
            take(6)
            take(7)
            for b in range(2):
                vec.wait_ge(S("lv_cross"), b + 1)
                ve_.tensor_copy(flat(aT[:, 2, 4 * b:4 * b + 4, :]), PA[:, b, :]).then_inc(S("aT2"), 1)
            vec.wait_ge(S("sg0"), 2)
            sv = flat(sg).rearrange("p (g c) -> p g c", c=DH)
            ve_.tensor_tensor(sv, sv, gno.unsqueeze(1).broadcast_to([P, RT * HH, DH]), ALU.mult)\
               .then_inc(S("sg"), 1)
            for b in range(4):
                vec.wait_ge(S("ho_sq"), b + 1)
                ins = ve_.tensor_reduce(ssq[:, 4 * b:4 * b + 4],
                                        flat(sqh)[:, b * 512:(b + 1) * 512].rearrange("p (g c) -> p g c", g=4),
                                        AXX, ALU.add)
            link(ins)
            ve_.tensor_scalar(ve[:, 0:16], ssq, 1.0 / DH, RMS_EPS, ALU.mult, ALU.add).then_inc(S("ve"), 1)
            vec.wait_ge(S("rstd"), 4)
            vec.wait_ge(S("sg"), 1)
            for b in range(4):
                for r in range(RT):
                    for c in range(2):
                        hd, g = 2 * b + c, 4 * b + 2 * r + c
                        cols = slice(hd * DH, (hd + 1) * DH)
                        ins = ve_.scalar_tensor_tensor(
                            out=oh[:, r, cols], in0=PA[:, b, (2 * r + c) * P:(2 * r + c + 1) * P],
                            scalar=rstd[:, g:g + 1], in1=sg[:, r, cols], op0=ALU.mult, op1=ALU.mult)
                ins.then_inc(S("oh"), 1)
            x_lo("ho")
            for u in range(U_HO + 3, U_F1 + 3):
                lo(u)
            residual(ALPHA, U_HO + 3)
            layer_norm(2, 4)
            x_lo("n3")
            ffn(1, U_F1, "f1")
            residual(ALPHA, U_F1 + N_F - 1)
            layer_norm(3, 5)

            rms_norm(4, 6, orow)
            x_lo("y1")
            for u in range(U_M + 2, U_M + 15):
                lo(u)
            attention("2")
            x_lo("ao2")
            for u in range(U_MO + 3, U_F2 + 3):
                lo(u)
            residual(1.0, U_MO + 3)
            rms_norm(5, 7, orow)
            x_lo("y2")

            U, T0 = U_F2, ev["f2"]
            c0 = link.n

            def conv(i):
                n0 = i * 2 + c0
                for f in range(4):
                    b_, o_ = (T0 + f // 2) % 2, (f % 2) * T
                    vec.wait_ge(S("conv0"), i * 4 + (2 * (f // 2) + 2))
                    ins = ve_.scalar_tensor_tensor(out=cv[:, f, 1:T], in0=TB[:, b_, o_:o_ + T - 1],
                                                   scalar=cwi[:, 1, f // 2, f % 2:f % 2 + 1], in1=cv[:, f, 1:T],
                                                   op0=ALU.mult, op1=ALU.add)
                ins.then_inc(S("vec_chain"), 1)
                vec.wait_ge(S("vec_chain"), n0 + 1)
                for f in range(4):
                    b_, o_ = (T0 + f // 2) % 2, (f % 2) * T
                    ins = ve_.scalar_tensor_tensor(out=cv[:, f, 2:T], in0=TB[:, b_, o_:o_ + T - 2],
                                                   scalar=cwi[:, 0, f // 2, f % 2:f % 2 + 1], in1=cv[:, f, 2:T],
                                                   op0=ALU.mult, op1=ALU.add)
                    if f % 2:
                        ins.then_inc(S("t_free"), 1)
                vec.wait_ge(S("cexp"), i + 1)
                ve_.tensor_scalar(ce, ce, 1.0, None, ALU.add).then_inc(S("vec_chain"), 1)
                vec.wait_ge(S("vec_chain"), n0 + 2)
                ve_.reciprocal(ce, ce).then_inc(S("crec"), 1)
                vec.wait_ge(S("crec"), i + 1)
                vec.wait_ge(S("cgv"), i + 1)
                if not isinstance(i, int) or i > 0:
                    vec.wait_ge(S("c_lo"), i)
                ve_.tensor_tensor(fhT, cgv, ce, ALU.mult).then_inc(S("hidden_t"), 1)

            def conv_lo(i):
                vec.wait_ge(S("c_hi"), i + 1)
                ve_.tensor_tensor(flo[:, :, :], fhT, fhi[:, :, :].bitcast(F32), ALU.subtract).then_inc(S("c_lo"), 1)

            def weights(i):
                if not isinstance(i, int) or i > 0:
                    vec.wait_ge(S("t_free"), i * 2 + T0)
                cwv = cw[:, :, :].rearrange("p j (s c) -> p j s c", s=2)
                ve_.tensor_copy(cwi[:, :, :, :], cwv[:, :, :, bass.ds(i * 2, 2)]).then_inc(S("cwi"), 1)

            def step(i):
                at = (lambda u: lo(u, i)) if not isinstance(i, int) else (lambda u: lo(u + 3 * i))
                weights(i - 1)
                conv(i - 1)
                conv_lo(i - 1)
                at(U + 2)
                at(U + 3)
                at(U + 4)

            lo(U + 3)
            lo(U + 4)
            step(1)
            with vec.Fori(2, NFF - 1) as i:
                step(i)
            step(NFF - 1)
            weights(NFF - 1)
            conv(NFF - 1)
            conv_lo(NFF - 1)
            link.n += 2 * NFF
            residual(1.0, U_F2 + N_F - 1)
            rms_norm(6, 8, h)

        @block.tensor
        def _(pe):
            mm = nc.tensor.matmul

            def t_bank(e):
                if e >= 2:
                    pe.wait_ge(S("t_free"), e - 1)

            def parts_ready(e):
                pe.wait_ge(S("t_free"), e + 1)

            def turn_rows(name, rows, ready=None):
                for g in range(4):
                    e = ev[name] + g
                    t_bank(e)
                    if ready:
                        ready(g)
                    for k in range(2):
                        for r in range(RT):
                            last = nc.tensor.transpose(TB[:, e % 2, (2 * k + r) * P:(2 * k + r + 1) * P],
                                                       rows[:, r, (2 * g + k) * P:(2 * g + k + 1) * P], ident[:, :])
                    last.then_inc(S("t_full"), 1)

            def products(dst, k, r, slot, cols, first, last_, xh=None, xl=None):
                xh, xl = (xhi if xh is None else xh), (xlo if xl is None else xl)
                rows = slice(r * P, (r + 1) * P)
                mm(dst, xl[:, k, rows], whi[:, slot, cols], start=first, stop=False)
                mm(dst, xh[:, k, rows], wlo[:, slot, cols], start=False, stop=False)
                return mm(dst, xh[:, k, rows], whi[:, slot, cols], start=False, stop=last_)

            def up(u, bank, j=0, x_event=None):
                for s in range(2):
                    slot = (u + s) % RING
                    pe.wait_ge(S("w_lo"), j * 3 + (u + s + 1))
                    for t in range(4):
                        k = 4 * s + t
                        if x_event is not None and k % 2 == 0:
                            parts_ready(x_event + k // 2)
                        for r in range(RT):
                            last = products(bank(r), k, r, slot, slice(t * 512, (t + 1) * 512), k == 0, k == KT - 1)
                    last.then_inc(S("w_used"), 1)

            def down(u, k0, first, last_, j=0, xh=None, xl=None):
                slot = u % RING
                pe.wait_ge(S("w_lo"), j * 3 + (u + 1))
                for t in range(2):
                    for r in range(RT):
                        for f in range(2):
                            last = products(PA[:, 2 * r + f, :], k0 + t, r, slot,
                                            slice(t * D + f * 512, t * D + (f + 1) * 512),
                                            first and t == 0, last_ and t == 1, xh, xl)
                last.then_inc(S("w_used"), 1)

            def attention(tag, keys, bias_l, bias_r, value):
                e0 = ev["pt" + tag]

                def logits(hd):
                    if hd >= 4:
                        pe.wait_ge(S("prob" + tag), 2 * (hd - 3))
                    rows = slice(HD * (hd % 2), HD * (hd % 2) + HD)
                    for r, (a, n_) in enumerate(((0, 128), (128, 256))):
                        dst = PA[:, hd % 4, a:a + n_]
                        mm(dst, qT[rows, hd // 2, r * P:(r + 1) * P], keys(hd)[rows, 0:n_], start=True, stop=False)
                        last = mm(dst, bias_l[:, :], bias_r(hd, r), start=False, stop=True)
                    last.then_inc(S("logit" + tag), 1)

                def turn(hd):
                    t_bank(e0 + hd)
                    pe.wait_ge(S("prob" + tag), 2 * hd + 2)
                    for c in range(3):
                        last = nc.tensor.transpose(TB[:, (e0 + hd) % 2, c * P:(c + 1) * P],
                                                   pr[:, hd % 3, c * P:(c + 1) * P], ident[:, :])
                    last.then_inc(S("t_full"), 1)

                def pv(hd):
                    parts_ready(e0 + hd)
                    g = hd // 4
                    if hd % 4 == 0 and g >= 2:
                        pe.wait_ge(S("orow" + tag), 2 * (g - 1))
                    c = (hd % 4) * P
                    mm(PG[:, g % 2, c:c + HD], pT[:, hd % 3, 0:P], value(hd, 0), start=True, stop=True)
                    mm(PG[:, g % 2, c + HD:c + P], pT[:, hd % 3, P:2 * P], value(hd, 0), start=True, stop=False)
                    mm(PG[:, g % 2, c + HD:c + P], pT[:, hd % 3, 2 * P:3 * P], value(hd, 1), start=False, stop=True)\
                        .then_inc(S("pv" + tag), 1)

                for i in range(HQ + 2):
                    if i < HQ:
                        logits(i)
                    if 1 <= i <= HQ:
                        turn(i - 1)
                    if i >= 2:
                        pv(i - 2)

            def out_proj(U, name):
                for j in range(4):
                    parts_ready(ev[name] + j)
                    down(U + j, 2 * j, j == 0, j == 3)

            def ffn(U, name, x_event, turn, hidden_ready, g_free):
                bank = lambda r: PG[:, r, :]
                up(U, bank, 0, x_event)
                def step(i):
                    ii = i if not isinstance(i, int) else i
                    turn(i - 1)
                    g_free(i - 1)
                    up(U + 2 - 3, bank, i)
                    hidden_ready(i - 1)
                    down(U + 4 - 3, 0, False, False, i, fhi, flo)
                turn(0)
                g_free(0)
                up(U + 2, bank)
                hidden_ready(0)
                down(U + 4, 0, True, False, 0, fhi, flo)
                with pe.Fori(2, NFF) as i:
                    step(i)
                turn(NFF - 1)
                hidden_ready(NFF - 1)
                down(U + N_F - 1, 0, False, True, 0, fhi, flo)

            def swiglu(k, U, name, x_event):
                T0 = ev[name]

                def turn(i):
                    pe.wait_ge(S("hidden"), i + (k * NFF + 1))
                    for f in range(2):
                        pe.wait_ge(S("t_free"), i * 2 + (T0 + f - 1))
                        for r in range(RT):
                            last = nc.tensor.transpose(TB[:, (T0 + f) % 2, r * P:(r + 1) * P],
                                                       fh[:, r, f * P:(f + 1) * P], ident[:, :])
                        last.then_inc(S("t_full"), 1)

                ffn(U, name, x_event, turn, lambda i: pe.wait_ge(S("t_free"), i * 2 + (T0 + 2)), lambda i: None)

            pe.wait_ge(S("ident"), 1)
            pe.wait_ge(S("x_loaded"), 32)
            turn_rows("x", h)
            pe.wait_ge(S("cst_loaded"), 64)
            e = ev["c0"]
            t_bank(e)
            nc.tensor.transpose(TB[0:BUCKETS, e % 2, 0:HQ], relrow[0:HQ, :], ident[0:HQ, 0:HQ]).then_inc(S("t_full"), 1)
            t_bank(e + 1)
            for j in range(4):
                last = nc.tensor.transpose(TB[:, (e + 1) % 2, 44 * j:44 * j + 44], cw4[0:44, j, :], ident[0:44, 0:44])
            last.then_inc(S("t_full"), 1)
            up(U_IN, lambda r: PG[:, r, :], 0, ev["x"])
            pe.wait_ge(S("w_lo"), 3)
            for k in range(KT):
                for r in range(RT):
                    last = products(PA[:, r, 0:136], k, r, 2, slice(k * 136, (k + 1) * 136), k == 0, k == KT - 1)
            last.then_inc(S("w_used"), 1)
            parts_ready(e)
            mm(PA[0:HQ, 2, 0:T], relT[0:BUCKETS, :], hot[0:BUCKETS, :], start=True, stop=True).then_inc(S("reldist"), 1)
            e = ev["cq"]
            pe.wait_ge(S("cqn"), 1)
            t_bank(e)
            for k in range(2):
                for r in range(RT):
                    last = nc.tensor.transpose(TB[:, e % 2, (2 * k + r) * P:(2 * k + r + 1) * P],
                                               cqn[:, r, k * P:(k + 1) * P], ident[:, :])
            last.then_inc(S("t_full"), 1)
            parts_ready(e)
            pe.wait_ge(S("relv"), 1)
            down(U_IQ, 0, True, True)
            e = ev["ki"]
            pe.wait_ge(S("kd"), 1)
            t_bank(e)
            for g in range(2):
                for r in range(RT):
                    last = nc.tensor.transpose(TB[:, e % 2, (2 * g + r) * P:(2 * g + r + 1) * P],
                                               kd[:, r, g, :, :].rearrange("p a b -> p (a b)"), ident[:, :])
            last.then_inc(S("t_full"), 1)
            t_bank(e + 1)
            for r in range(RT):
                last = nc.tensor.transpose(TB[:, (e + 1) % 2, r * P:(r + 1) * P], pin[:, r, C_KI:C_WI], ident[:, :])
            last.then_inc(S("t_full"), 1)
            pe.wait_ge(S("qi_a"), 1)
            pe.wait_ge(S("qi_b"), 1)
            down(U_UQ, 0, True, True)
            parts_ready(ev["ki"] + 1)
            pe.wait_ge(S("qi_r"), 1)
            turn_rows("qi", qi)
            pe.wait_ge(S("q_r"), 1)
            turn_rows("q", qr)
            parts_ready(ev["q"] + 3)
            for hd in range(HI):
                if hd >= 4:
                    pe.wait_ge(S("relu"), hd - 3)
                mm(PA[:, hd % 4, 0:128], qiT[:, hd, 0:P], kiT[:, 0:P], start=True, stop=True)
                mm(PA[:, hd % 4, 128:384], qiT[:, hd, P:T], kiT, start=True, stop=True).then_inc(S("iscore"), 1)
            pe.wait_ge(S("mask_causal"), 1)
            attention("", lambda hd: kT[:, hd // 8, :], ident, lambda hd, r: mask[:, 0:128] if r == 0 else mask[:, 128:384],
                      lambda hd, r: pin[:, r, C_V + HD * (hd // 8):C_V + HD * (hd // 8) + HD])
            turn_rows("ao", orow, lambda g: pe.wait_ge(S("orow"), 2 * g + 2))
            out_proj(U_AO, "ao")
            turn_rows("n1", h, lambda g: pe.wait_ge(S("norm"), 2))
            swiglu(0, U_F0, "f0", ev["n1"])
            turn_rows("n2", h, lambda g: pe.wait_ge(S("norm"), 4))

            up(U_H, lambda r: PG[:, r, :], 0, ev["n2"])
            up(U_H + 2, lambda r: PA[:, r, :])
            up(U_H + 4, lambda r: PA[:, 2 + r, :])
            pe.wait_ge(S("f_exp"), 1)
            up(U_H + 6, lambda r: PG[:, r, :])
            pe.wait_ge(S("f_exp"), 2)
            pe.wait_ge(S("qh"), 1)
            pe.wait_ge(S("logf"), 2)
            for b in range(4):
                for c in range(2):
                    for r in range(RT):
                        last = mm(PA[:, b, (2 * c + r) * P:(2 * c + r + 1) * P],
                                  lf[:, r, (2 * b + c) * DH:(2 * b + c + 1) * DH], ucum, start=True, stop=True)
                last.then_inc(S("cum"), 1)
            pe.wait_ge(S("kr"), 2)
            turn_rows("hk", kr)
            pe.wait_ge(S("qh"), 2)
            turn_rows("hq", qh)
            parts_ready(ev["hq"] + 3)

            def level(l):
                pe.wait_ge(S("bT"), 4)
                if l < 7:
                    pe.wait_ge(S("lv_x"), 2 * l + 2)
                d = (dl, dl2)[l % 2]
                kk, qq = (d, d) if l < 7 else (kTh, qTh)
                for b in range(4):
                    if l:
                        pe.wait_ge(S("lv_taken"), 4 * (l - 1) + b + 1)
                    for r in range(RT):
                        for c in range(2):
                            rows = slice(r * P, (r + 1) * P)
                            last = mm(PA[:, b, (2 * r + c) * P:(2 * r + c + 1) * P],
                                      kk[:, 2 * b + c, rows], qq[:, 2 * b + c, rows], start=True, stop=True)
                    last.then_inc(S("lv_full"), 1)

            up(U_H + 8, lambda r: PG[:, r, :])
            level(0)
            pe.wait_ge(S("vi"), 1)
            up(U_H + 10, lambda r: PG[:, r, :])
            level(1)
            pe.wait_ge(S("vi"), 2)
            up(U_H + 12, lambda r: PG[:, r, :])
            level(2)
            pe.wait_ge(S("sg0"), 1)
            up(U_H + 14, lambda r: PG[:, r, :])
            for l in range(3, 8):
                level(l)
            pe.wait_ge(S("lv_x"), 16)
            for b in range(2):
                pe.wait_ge(S("lv_taken"), 4 * 7 + b + 1)
                for c in range(4):
                    last = mm(PA[:, b, c * P:(c + 1) * P], dl2[:, 4 * b + c, 0:P], dl2[:, 4 * b + c, P:T],
                              start=True, stop=True)
                last.then_inc(S("lv_cross"), 1)
            for b in range(4):
                pe.wait_ge(S("lv_taken"), 32)
                pe.wait_ge(S("aT2"), 2)
                for c in range(2):
                    hd = 2 * b + c
                    cols = slice(hd * DH, (hd + 1) * DH)
                    o0, o1 = (PA[:, b, (2 * r + c) * P:(2 * r + c + 1) * P] for r in range(RT))
                    mm(o0, aT[:, 0, hd, :], vi[:, 0, cols], start=True, stop=True)
                    mm(o1, aT[:, 2, hd, :], vi[:, 0, cols], start=True, stop=False)
                    last = mm(o1, aT[:, 1, hd, :], vi[:, 1, cols], start=False, stop=True)
                last.then_inc(S("ho"), 1)
            turn_rows("ho", oh, lambda g: pe.wait_ge(S("oh"), g + 1))
            out_proj(U_HO, "ho")
            turn_rows("n3", h, lambda g: pe.wait_ge(S("norm"), 6))
            swiglu(1, U_F1, "f1", ev["n3"])

            turn_rows("y1", orow, lambda g: pe.wait_ge(S("norm"), 10))
            banks = (lambda r: PG[:, r, :], lambda r: PA[:, r, :], lambda r: PA[:, 2 + r, :])
            for c in range(6):
                if c >= 3:
                    pe.wait_ge(S("qkv"), c - 2)
                up(U_M + 2 * c, banks[c % 3], 0, ev["y1"] if c == 0 else None)
            pe.wait_ge(S("qkv"), 2)
            turn_rows("q2", q2)
            pe.wait_ge(S("qkv"), 6)
            turn_rows("k2", k2)
            parts_ready(ev["k2"] + 3)
            pe.wait_ge(S("relb"), 16)
            attention("2", lambda hd: k2T[:, hd // 2, :], nflip,
                      lambda hd, r: relb[:, hd, 128:256] if r == 0 else relb[:, hd, :],
                      lambda hd, r: v2[:, r, HD * hd:HD * hd + HD])
            turn_rows("ao2", orow, lambda g: pe.wait_ge(S("orow2"), 2 * g + 2))
            out_proj(U_MO, "ao2")
            turn_rows("y2", orow, lambda g: pe.wait_ge(S("norm"), 12))

            T0 = ev["f2"]

            def conv_turn(i):
                pe.wait_ge(S("urow"), i + 1)
                for s in range(2):
                    pe.wait_ge(S("t_free"), i * 2 + (T0 + s - 1))
                    for f in range(2):
                        for r in range(RT):
                            last = nc.tensor.transpose(TB[:, (T0 + s) % 2, (2 * f + r) * P:(2 * f + r + 1) * P],
                                                       urow[:, r, s * FC + f * P:s * FC + (f + 1) * P], ident[:, :])
                    last.then_inc(S("t_full"), 1)

            ffn(U_F2, "f2", ev["y2"], conv_turn, lambda i: pe.wait_ge(S("c_lo"), i + 1), lambda i: None)


INPUTS = ("x", "positions", "att_w_in", "att_g_cq", "att_w_uq", "att_w_iq", "att_g_ik", "att_b_ik", "att_w_o",
          "hgrn_lb_logits", "hgrn_w_in", "hgrn_g_norm", "hgrn_w_o", "ffn_w_gate", "ffn_w_up", "ffn_w_down",
          "ln_g", "ln_b", "attn_norm_2", "w_qkv_2", "w_o_2", "rel_bias_2", "ffn_norm_2", "w_up_2", "conv_w_2",
          "conv_b_2", "w_down_2", "final_norm_2")
ONE = ("x", "positions", "att_w_in", "att_g_cq", "att_w_uq", "att_w_iq", "att_g_ik", "att_b_ik", "att_w_o",
       "hgrn_w_in", "hgrn_g_norm", "hgrn_w_o", "attn_norm_2", "w_qkv_2", "w_o_2", "ffn_norm_2", "w_up_2",
       "conv_w_2", "conv_b_2", "w_down_2")


def kernel(**inputs):
    import concourse.bacc as bacc
    from concourse.bass_utils import run_bass_kernel_spmd as run

    nc = bacc.Bacc("TRN2", target_bir_lowering=False, num_devices=1)
    arrays = {name: np.ascontiguousarray(inputs[name]) for name in INPUTS}
    arrays["inv"], arrays["hot"] = shape_constants()
    feed, w = {}, {}
    for name, a in arrays.items():
        feed[f"in_{name}"] = a
        w[name] = nc.dram_tensor(f"in_{name}", a.shape, mybir.dt.from_np(a.dtype), kind="ExternalInput").ap()
        if name in ONE or name == "inv":
            w[name] = w[name][0]
    for k in range(2):
        w[f"ffn{k}"] = tuple(w[m][k] for m in ("ffn_w_gate", "ffn_w_up", "ffn_w_down"))
    w["ffn2"] = (w["w_up_2"][:, 0:FF2], w["w_up_2"][:, FF2:2 * FF2], w["w_down_2"])
    out = nc.dram_tensor("out_0", (1, T, D), F32, kind="ExternalOutput").ap()
    build(nc, w, out[0])
    r = run(nc, [feed], core_ids=[0])
    return r.results[0]["out_0"]
```

```python
from contextlib import ExitStack

import numpy as np

import concourse.bass as bass
from concourse import mybir

F32 = mybir.dt.float32
F32R = mybir.dt.float32r
I32 = mybir.dt.int32
U8 = mybir.dt.uint8
ALU = mybir.AluOpType
ACT = mybir.ActivationFunctionType
AXX = mybir.AxisListType.X

P = 128
T = 256
RT = T // P
D = 1024
KT = D // P
HALF = D // 2
RING = 3
UNIT = 2048

NQL, HQ, HD = 256, 16, 64
HI, DI = 8, 128
TOPK = 64
ROT, ROTI = 8, 16
IN_COLS = 648
C_K, C_V, C_KI, C_WI = 256, 384, 512, 640
FF = 2816
FC = 256
NFF = FF // FC
ALPHA = 4 ** 0.25
LN_EPS, RMS_EPS = 1e-5, 1e-6
HH, DH = 8, 128
CHUNK = 64
LEVELS = (32, 16, 8, 4, 2, 1)

BUCKETS, MAXD = 32, 128
REL_W = 384
FF2 = 2816

NEG = -1e30
CAUSAL_FILL = -2e38
TAKEN = -3e38

PI2_1 = 6.28125
PI2_2 = float(np.float32(np.floor((2 * np.pi - PI2_1) * 2 ** 20) / 2 ** 20))
PI2_3 = 2 * np.pi - PI2_1 - PI2_2
ROUND = 1.5 * 2 ** 23


def shape_constants():
    inv = [500000.0 ** (-np.arange(0, 2 * n, 2) / (2 * n)) for n in (ROT, ROTI)]
    inv = np.concatenate(inv).astype(np.float32)
    n = np.arange(T)
    exact = BUCKETS // 2
    large = exact + (np.log(np.maximum(n, 1).astype(np.float32) / np.float32(exact))
                     / np.float32(np.log(MAXD / exact)) * np.float32(BUCKETS - exact)).astype(np.int32)
    bucket = np.where(n < exact, n, np.minimum(large, BUCKETS - 1))
    hot = (bucket[::-1][None, :] == np.arange(BUCKETS)[:, None]).astype(np.float32)
    return inv.reshape(1, -1), np.ascontiguousarray(hot)


def weight_units(w):
    def up(m, c, n=512):
        v = m.rearrange("(t p) n -> p t n", p=P)
        return [[(0, 4, n, v[:, 4 * j:4 * j + 4, c:c + n])] for j in range(2)]

    def down(m, tiles):
        v = m.rearrange("(t p) n -> p t n", p=P)
        return [[(0, 2, D, v[:, 2 * j:2 * j + 2, :])] for j in range(tiles // 2)]

    w_in = w["att_w_in"]
    a = up(w_in, 0)
    a.append([(0, 8, IN_COLS - 512, w_in.rearrange("(t p) n -> p t n", p=P)[:, :, 512:IN_COLS])])
    a += down(w["att_w_iq"], 2) + down(w["att_w_uq"], 2) + down(w["att_w_o"], 8)
    h = []
    for c in (2, 3, 0, 1, 4, 5, 6, 7):
        h += up(w["hgrn_w_in"], 512 * c)
    h += down(w["hgrn_w_o"], 8)
    m = []
    for c in range(6):
        m += up(w["w_qkv_2"], 512 * c)
    m += down(w["w_o_2"], 8)
    return a, h, m


N_A, N_H, N_M, N_F = 9, 20, 16, 3 * NFF
U_IN, U_IQ, U_UQ, U_AO = 0, 3, 4, 5
U_F0 = N_A
U_H = U_F0 + N_F
U_HO = U_H + 16
U_F1 = U_H + N_H
U_M = U_F1 + N_F
U_MO = U_M + 12
U_F2 = U_M + N_M
U_ALL = U_F2 + N_F


class Chain:

    def __init__(self, eng, sem):
        self.eng, self.sem, self.n = eng, sem, 0

    def __call__(self, ins):
        self.n += 1
        ins.then_inc(self.sem, 1)
        self.eng.wait_ge(self.sem, self.n)


def build(nc, w, out):
    ctx = ExitStack()
    with ctx:
        def sb(name, shape, dt=F32):
            return ctx.enter_context(nc.sbuf_tensor(name, shape, dt))

        sems = {}

        def S(name):
            if name not in sems:
                sems[name] = ctx.enter_context(nc.semaphore(name))
            return sems[name]

        raw = sb("raw", [P, RING, UNIT])
        whi = sb("whi", [P, RING, UNIT], F32R)
        wlo = sb("wlo", [P, RING, UNIT], F32R)
        h = sb("h", [P, RT, D])
        xhi = sb("xhi", [P, KT, T], F32R)
        xlo = sb("xlo", [P, KT, T], F32R)
        fhi = sb("fhi", [P, 2, T], F32R)
        flo = sb("flo", [P, 2, T], F32R)
        gvec = sb("gvec", [P, D])
        bvec = sb("bvec", [P, D])
        ident = sb("ident", [P, P])
        stats = sb("stats", [P, RT, 2, 6])
        mv = sb("mv", [P, 4, 2])
        ve = sb("ve", [P, 16])
        rstd = sb("rstd", [P, 16])
        mhalf = sb("mhalf", [P, 16])
        work = sb("work", [P, 24500])
        maskt = sb("maskt", [P, 8, P], U8)
        cw = sb("cw", [P, 4, 2 * FF2 // P])
        cwi = sb("cwi", [P, 4, 2, 2])

        def flat(ap):
            return ap.rearrange("p a b -> p (a b)")

        place = [0]

        def carve(*dims):
            n = int(np.prod(dims))
            a = work[:, place[0]:place[0] + n]
            place[0] += n
            assert place[0] <= 24500, place[0]
            if len(dims) == 1:
                return a
            names = "abcd"[:len(dims)]
            return a.rearrange(f"p ({' '.join(names)}) -> p {' '.join(names)}",
                               **{k: v for k, v in zip(names[1:], dims[1:])})

        PG = ctx.enter_context(nc.psum_tensor("PG", [P, 2, 512], F32))
        PA = ctx.enter_context(nc.psum_tensor("PA", [P, 4, 512], F32))
        TB = ctx.enter_context(nc.psum_tensor("TB", [P, 2, 512], F32))

        qT = carve(KT, T)
        pr = carve(3, 384)
        pT = carve(3, 384)
        orow = carve(RT, D)
        amin = carve(HQ, 2)
        asum = carve(HQ, 2)
        arec = carve(HQ, 2)
        att_end = place[0]
        pin = carve(RT, IN_COLS)
        qi = carve(RT, D)
        qr = carve(RT, D)
        qiT = carve(HI, T)
        cqn = carve(RT, NQL)
        kd = carve(RT, 2, 2, HD)
        kT = carve(2, T)
        kiT = carve(T)
        sq = carve(RT, NQL)
        relu = carve(2, 384)
        score = carve(384)
        left = carve(384)
        mask = carve(384)
        m8 = carve(2, 8)
        wsc = carve(RT, HI)
        gcq = carve(NQL)
        gki = carve(DI)
        bki = carve(DI)
        posi = carve(RT)
        posf = carve(RT)
        inv = carve(24)
        ang = carve(RT, 2, 24)
        turns = carve(RT, 2, 24)
        trig = carve(RT, 2, 24)
        rt1 = carve(RT, 128)
        rt2 = carve(RT, 128)
        rt3 = carve(RT, 128)
        rt4 = carve(RT, 128)
        hot = carve(T)
        relrow = carve(BUCKETS)
        relT = carve(HQ)
        relv = carve(REL_W)
        cw4 = carve(4, P)
        place[0] = 0
        lb = carve(D)
        lb1 = carve(D)
        kr = carve(RT, D)
        lf = carve(RT, D)
        qh = carve(RT, D)
        vi = carve(RT, D)
        sg = carve(RT, D)
        bT = carve(HH, T)
        kTh = carve(HH, T)
        qTh = carve(HH, T)
        dl2 = carve(HH, T)
        dls = [flat(z).rearrange("p (a b) -> p a b", a=HH) for z in (lf, dl2, kr)]
        aT = carve(3, HH, P)
        ucum = carve(P)
        oh = qh
        sqh = dl2.rearrange("p a b -> p (a b)").rearrange("p (a b) -> p a b", a=RT)
        ssq = carve(16)
        gno = carve(DH)
        place[0] = 0
        fe = carve(RT, FC)
        fh = carve(RT, FC)
        urow = carve(RT, 2 * FC)
        cv = carve(4, T)
        ce = carve(2, T)
        cgv = carve(2, T)
        fhT = carve(2, T)
        place[0] = att_end
        q2 = carve(RT, D)
        k2 = carve(RT, D)
        v2 = carve(RT, D)
        k2T = carve(KT, T)
        relb = carve(HQ, T)

        rel_dram = nc.dram_tensor("rel_scratch", [HQ, P, REL_W], F32, kind="Internal").ap()

        a_units, h_units, m_units = weight_units(w)
        units = {}
        for base, lst in ((U_IN, a_units), (U_H, h_units), (U_M, m_units)):
            for j, x in enumerate(lst):
                units[base + j] = x

        ev = {}
        n = 0
        for name, k in (("x", 4), ("c0", 2), ("cq", 1), ("ki", 2), ("qi", 4), ("q", 4), ("pt", HQ), ("ao", 4),
                        ("n1", 4), ("f0", 2 * NFF), ("n2", 4), ("hk", 4), ("hq", 4), ("ho", 4), ("n3", 4),
                        ("f1", 2 * NFF), ("y1", 4), ("q2", 4), ("k2", 4), ("pt2", HQ), ("ao2", 4),
                        ("y2", 4), ("f2", 2 * NFF)):
            ev[name] = n
            n += k

        def bc(row, n_):
            return bass.AP(row.tensor, row.offset, [[0, n_]] + [list(x) for x in row.ap])

        block = ctx.enter_context(nc.Block())

        VE = [4, 2, 2, 16, 2, 2, 2, 2, 2]
        GB = [("ln_g", 0, 0), ("ln_g", 0, 1), ("ln_g", 1, 0), ("ln_g", 1, 1), ("attn_norm_2", 0, None),
              ("ffn_norm_2", 0, None), ("final_norm_2", None, None)]
        GB_COUNT = np.cumsum([32, 32, 32, 32, 16, 16, 16]).tolist()

        @block.sync
        def _(sp):
            def slot_free(u):
                if u >= RING:
                    sp.wait_ge(S("w_lo"), u - RING + 1)

            def load(u):
                slot_free(u)
                for o, t, c, view in units[u]:
                    dst = raw[:, u % RING, o:o + t * c].rearrange("p (t c) -> p t c", t=t)
                    sp.dma_start(dst, view).then_inc(S(f"w_loaded{u % RING}"), 16)

            def load_up(slot, i, j, gate, val):
                dst = raw[:, slot, :].rearrange("p (t s c) -> p t s c", t=4, s=2)
                for s, m in enumerate((gate, val)):
                    v = m.rearrange("(t p) n -> p t n", p=P)[:, 4 * j:4 * j + 4, bass.ds(i * FC, FC)]
                    sp.dma_start(dst[:, :, s, :], v).then_inc(S(f"w_loaded{slot}"), 16)

            def load_down(slot, i, down):
                dst = raw[:, slot, :].rearrange("p (t c) -> p t c", t=2)
                v = down.rearrange("(g t p) n -> p g t n", p=P, t=2)[:, bass.ds(i, 1), :, :]
                sp.dma_start(dst, v.rearrange("p g t n -> p (g t) n")).then_inc(S(f"w_loaded{slot}"), 16)

            def ffn(U, gate, val, down):
                for j in range(2):
                    slot_free(U + j)
                    load_up((U + j) % RING, 0, j, gate, val)
                with sp.Fori(1, NFF) as i:
                    for j in range(2):
                        sp.wait_ge(S("w_lo"), i * 3 + (U - 3 + j))
                        load_up((U + 2 + j) % RING, i, j, gate, val)
                    sp.wait_ge(S("w_lo"), i * 3 + (U - 1))
                    load_down((U + 4) % RING, i - 1, down)
                slot_free(U + N_F - 1)
                load_down((U + N_F - 1) % RING, NFF - 1, down)

            hv = w["x"].rearrange("(r p) n -> p r n", p=P)
            for r in range(RT):
                sp.dma_start(h[:, r, :], hv[:, r, :]).then_inc(S("x_loaded"), 16)
            for u in range(N_A):
                load(u)
            ffn(U_F0, *w["ffn0"])
            for u in range(U_H, U_H + N_H):
                load(u)
            ffn(U_F1, *w["ffn1"])
            for u in range(U_M, U_M + N_M):
                load(u)
            ffn(U_F2, *w["ffn2"])
            ov = out.rearrange("(r p) n -> p r n", p=P)
            for f in range(2):
                sp.wait_ge(S("norm"), 12 + f + 1)
                cols = slice(f * HALF, (f + 1) * HALF)
                sp.dma_start(ov[:, :, cols], h[:, :, cols]).then_inc(S("stored"), 16)
            sp.wait_ge(S("stored"), 16 * RT)

        @block.gpsimd
        def _(pool):
            link = Chain(pool, S("pool_chain"))
            for r in range(RT):
                pool.dma_start(posi[:, r:r + 1].bitcast(I32),
                               w["positions"][r * P:(r + 1) * P].rearrange("(p o) -> p o", o=1)).then_inc(S("pos"), 16)
            pool.dma_start(inv, bc(w["inv"], P)).then_inc(S("pos"), 16)
            link(pool.memset(ident[:, :], 0.0))
            pool.affine_select(out=ident[:, :], in_=ident[:, :], compare_op=ALU.not_equal, fill=1.0, base=0,
                               pattern=[[-1, P]], channel_multiplier=1).then_inc(S("ident"), 1)
            for dst, src in ((gcq, w["att_g_cq"]), (gki, w["att_g_ik"]), (bki, w["att_b_ik"])):
                pool.dma_start(dst, bc(src, P)).then_inc(S("small"), 16)
            pool.dma_start(hot[0:BUCKETS, :], w["hot"]).then_inc(S("cst_loaded"), 16)
            pool.dma_start(relrow[0:HQ, :], w["rel_bias_2"]).then_inc(S("cst_loaded"), 16)
            pool.dma_start(cw4[0:44, 0:3, :], w["conv_w_2"].rearrange("j (c p) -> c j p", p=P))\
                .then_inc(S("cst_loaded"), 16)
            pool.dma_start(cw4[0:44, 3, :], w["conv_b_2"].rearrange("(c p) -> c p", p=P))\
                .then_inc(S("cst_loaded"), 16)
            link(pool.memset(mhalf[:, :], -0.5))

            def load_gb(k):
                name, a, b = GB[k]
                if k:
                    pool.wait_ge(S("norm"), 2 * k)
                if name == "ln_g":
                    pool.dma_start(gvec[:, :], bc(w["ln_g"][a, b], P)).then_inc(S("gb"), 16)
                    pool.dma_start(bvec[:, :], bc(w["ln_b"][a, b], P)).then_inc(S("gb"), 16)
                else:
                    pool.dma_start(gvec[:, :], bc(w[name], P)).then_inc(S("gb"), 16)

            def power(k):
                pool.wait_ge(S("ve"), k + 1)
                m = VE[k]
                pool.tensor_tensor(rstd[:, 0:m], ve[:, 0:m], mhalf[:, 0:m], ALU.pow).then_inc(S("rstd"), 1)

            load_gb(0)
            pool.wait_ge(S("relv"), 2)
            pool.dma_start(rel_dram, relv[0:HQ, :].unsqueeze(1).broadcast_to([HQ, P, REL_W]))\
                .then_inc(S("rel_out"), 16)
            power(0)
            pool.wait_ge(S("iacc"), 2 * HI)
            for c in (0, 256):
                last = pool.affine_select(out=score[:, c:c + P], in_=score[:, c:c + P], compare_op=ALU.is_ge,
                                          fill=CAUSAL_FILL, base=0, pattern=[[-1, P]], channel_multiplier=1)
            last.then_inc(S("score_causal"), 1)
            pool.wait_ge(S("mask"), 1)
            for c in (0, 256):
                last = pool.affine_select(out=mask[:, c:c + P], in_=mask[:, c:c + P], compare_op=ALU.is_ge,
                                          fill=-NEG, base=0, pattern=[[-1, P]], channel_multiplier=1)
            last.then_inc(S("mask_causal"), 1)
            power(1)
            load_gb(1)
            power(2)
            load_gb(2)
            hf = dl2.rearrange("p a b -> p (a b)")[:, 0:P]
            for n_, m in enumerate((CHUNK,) + LEVELS):
                nb = P // (2 * m)
                link(pool.memset(hf, 0.0))
                link(pool.memset(hf.rearrange("p (b s m) -> p b s m", s=2, m=m)[:, :, 1, :], 1.0))
                v3 = hf.rearrange("p (b q) -> p b q", q=2 * m)
                link(pool.affine_select(out=v3, in_=v3, compare_op=ALU.is_ge, fill=0.0, base=0,
                                        pattern=[[-2 * m, nb], [0, 2 * m]], channel_multiplier=1))
                link(pool.affine_select(out=v3, in_=v3, compare_op=ALU.is_ge, fill=0.0, base=m - 1,
                                        pattern=[[2 * m, nb], [0, 2 * m]], channel_multiplier=-1))
                link(pool.tensor_copy(maskt[:, n_, :], hf))
            link(pool.tensor_copy(maskt[:, 7, :], ident[:, :]))
            link(pool.memset(ucum, 1.0))
            link(pool.affine_select(out=ucum, in_=ucum, compare_op=ALU.is_ge, fill=0.0, base=0,
                                    pattern=[[1, P]], channel_multiplier=-1))
            u3 = ucum[:, CHUNK:P]
            link(pool.affine_select(out=u3, in_=u3, compare_op=ALU.is_ge, fill=0.0, base=-CHUNK,
                                    pattern=[[0, CHUNK]], channel_multiplier=1))
            pool.dma_start(lb, bc(w["hgrn_lb_logits"][0], P)).then_inc(S("lb_loaded"), 16)
            pool.dma_start(lb1, bc(w["hgrn_lb_logits"][1], P)).then_inc(S("lb_loaded"), 16)
            pool.dma_start(gno, bc(w["hgrn_g_norm"], P)).then_inc(S("lb_loaded"), 16)
            pool.memset(aT[:, 0:2, :, :], 0.0).then_inc(S("hconst"), 1)

            pool.wait_ge(S("t_free"), ev["hq"])
            pool.wait_ge(S("bT"), 4)
            for l, m in enumerate((CHUNK,) + LEVELS):
                d = dls[l % 3]
                if l >= 3:
                    pool.wait_ge(S("lv_full"), 4 * (l - 2))
                dv = d.rearrange("p h t -> p (h t)").rearrange("p (b s m) -> p b s m", s=2, m=m)
                bv = bT.rearrange("p h t -> p (h t)").rearrange("p (b s m) -> p b s m", s=2, m=m)
                nb = bv.shape[1]
                mid = bv[:, :, 0, m - 1:m].broadcast_to([P, nb, m])
                pool.tensor_tensor(dv[:, :, 0, :], mid, bv[:, :, 0, :], ALU.subtract).then_inc(S("lv_d"), 1)
                if l == 0:
                    pool.tensor_copy(dv[:, :, 1, :], bv[:, :, 1, :]).then_inc(S("lv_d"), 1)
                else:
                    pool.tensor_tensor(dv[:, :, 1, :], bv[:, :, 1, :], mid, ALU.subtract).then_inc(S("lv_d"), 1)
            pool.wait_ge(S("lv_full"), 4 * 5)
            dc = dls[7 % 3].rearrange("p h (c t) -> p h c t", c=4)
            bvc = bT.rearrange("p h (c t) -> p h c t", c=4)
            end = lambda c: bvc[:, :, c, CHUNK - 1:CHUNK].broadcast_to([P, HH, CHUNK])
            link(pool.tensor_tensor(dc[:, :, 0, :], end(0), bvc[:, :, 0, :], ALU.subtract))
            pool.tensor_tensor(dc[:, :, 0, :], dc[:, :, 0, :], end(1), ALU.add).then_inc(S("lv_d"), 1)
            pool.tensor_tensor(dc[:, :, 1, :], end(1), bvc[:, :, 1, :], ALU.subtract).then_inc(S("lv_d"), 1)
            pool.tensor_copy(dc[:, :, 2, :], bvc[:, :, 2, :]).then_inc(S("lv_d"), 1)
            pool.tensor_tensor(dc[:, :, 3, :], bvc[:, :, 3, :], end(2), ALU.add).then_inc(S("lv_d"), 1)
            power(3)
            power(4)
            load_gb(3)
            power(5)
            load_gb(4)
            power(6)
            pool.wait_ge(S("rel_out"), 16)
            src = bass.AP(rel_dram.tensor, P - 1, [[REL_W - 1, P], [P * REL_W, HQ], [1, T]])
            pool.wait_ge(S("norm"), 10)
            pool.dma_start(relb, src).then_inc(S("relb"), 16)
            load_gb(5)
            power(7)
            load_gb(6)

            def gate_value(i):
                pool.wait_ge(S("t_free"), i * 2 + (ev["f2"] + 2))
                pool.tensor_tensor(cgv, cv[:, 0:2, :], cv[:, 2:4, :], ALU.mult).then_inc(S("cgv"), 1)

            gate_value(0)
            with pool.Fori(1, NFF) as i:
                gate_value(i)
            power(8)

        total = [0] * RING
        landed = []
        for u in range(U_ALL + RING):
            two = any(U <= u < U + N_F and (u - U < 2 or ((u - U) % 3 != 1 and u != U + N_F - 1))
                      for U in (U_F0, U_F1, U_F2))
            total[u % RING] += 32 if two else 16
            landed.append(total[u % RING])

        def unit_len(u):
            return 8 * (IN_COLS - 512) if u == 2 else UNIT

        def hi(u, i=0):
            if u >= U_ALL:
                return
            s = u % RING
            step = landed[u + RING] - landed[u]
            nc.scalar.wait_ge(S(f"w_loaded{s}"), i * step + landed[u])
            if u >= RING:
                nc.scalar.wait_ge(S("w_used"), i * 3 + (u - RING + 1))
            n_ = unit_len(u)
            nc.scalar.activation(whi[:, s, 0:n_], raw[:, s, 0:n_], ACT.Copy).then_inc(S("w_hi"), 1)

        def lo(u, i=0):
            if u >= U_ALL:
                return
            s = u % RING
            n_ = unit_len(u)
            nc.vector.wait_ge(S("w_hi"), i * 3 + (u + 1))
            nc.vector.tensor_tensor(wlo[:, s, 0:n_], raw[:, s, 0:n_], whi[:, s, 0:n_].bitcast(F32),
                                    ALU.subtract).then_inc(S("w_lo"), 1)

        @block.scalar
        def _(act):
            ac = nc.scalar
            link = Chain(act, S("act_chain"))

            def turned(e):
                act.wait_ge(S("t_full"), e + 1)

            def full(u):
                act.wait_ge(S("w_used"), u + 1)

            def x_hi(name, k=4):
                for g in range(k):
                    e = ev[name] + g
                    turned(e)
                    ac.activation(flat(xhi[:, 2 * g:2 * g + 2, :]), TB[:, e % 2, :], ACT.Copy)\
                      .then_inc(S("x_hi"), 1)

            def copy_turned(name, dst):
                for g in range(4):
                    e = ev[name] + g
                    turned(e)
                    ac.activation(flat(dst[:, 2 * g:2 * g + 2, :]), TB[:, e % 2, :], ACT.Copy)\
                      .then_inc(S("t_free"), 1)

            def attention(tag):
                for hd in range(HQ):
                    act.wait_ge(S("amin" + tag), 2 * hd + 2)
                    for r, (a, b) in enumerate(((0, 128), (128, 384))):
                        ac.activation(pr[:, hd % 3, a:b], pr[:, hd % 3, a:b], ACT.Exp, scale=-1.0,
                                      bias=amin[:, hd, r:r + 1], accum_out=asum[:, hd, r:r + 1])\
                          .then_inc(S("prob" + tag), 1)

            def ffn(k, U, name):
                T0 = ev[name]

                def f_hi(i):
                    for f in range(2):
                        act.wait_ge(S("t_full"), i * 2 + (T0 + f + 1))
                        ac.activation(fhi[:, f, :], TB[:, (T0 + f) % 2, 0:T], ACT.Copy).then_inc(S("x_hi"), 1)

                def gates(i, u):
                    act.wait_ge(S("w_used"), i * 3 + (u + 1))
                    if not (k == 0 and isinstance(i, int) and i == 0):
                        act.wait_ge(S("hidden"), i + k * NFF)
                    ac.activation(fe, PG[:, :, 0:FC], ACT.Sigmoid).then_inc(S("gate"), 1)

                def step(i):
                    at = (lambda u: hi(u, i)) if not isinstance(i, int) else (lambda u: hi(u + 3 * i))
                    f_hi(i - 1)
                    at(U + 2)
                    gates(i, U)
                    at(U + 3)
                    at(U + 4)

                hi(U + 3)
                full(U + 1)
                gates(0, U)
                hi(U + 4)
                with act.Fori(1, NFF - 1) as i:
                    step(i)
                step(NFF - 1)
                f_hi(NFF - 1)

            act.wait_ge(S("ang"), 1)
            ac.activation(trig.rearrange("p a b c -> p (a b c)"), ang.rearrange("p a b c -> p (a b c)"),
                          ACT.Sin).then_inc(S("trig"), 1)
            x_hi("x")
            for u in range(3):
                hi(u)
            full(1)
            ac.activation(pin[:, :, 0:512], PG[:, :, :], ACT.Copy).then_inc(S("pin"), 1)
            act.wait_ge(S("pin"), 1)
            for r in range(RT):
                ac.activation(sq[:, r, :], pin[:, r, 0:NQL], ACT.Square,
                              accum_out=ve[:, 8 + r:9 + r]).then_inc(S("ssq"), 1)
            hi(3)
            hi(4)
            turned(ev["cq"])
            ac.activation(flat(xhi[:, 0:2, :]), TB[:, ev["cq"] % 2, :], ACT.Copy).then_inc(S("x_hi"), 1)
            hi(5)
            full(U_IQ)
            ac.activation(qi[:, 0, :], flat(PA[:, 0:2, :]), ACT.Copy).then_inc(S("qi_a"), 1)
            hi(6)
            full(U_UQ)
            ac.activation(qr[:, 0, :], flat(PA[:, 0:2, :]), ACT.Copy, scale=-HD ** -0.5)\
              .then_inc(S("q_a"), 1)
            hi(7)
            copy_turned("qi", qiT)
            copy_turned("q", qT)
            for hd in range(HI):
                act.wait_ge(S("iscore"), hd + 1)
                if hd >= 2:
                    act.wait_ge(S("iacc"), 2 * (hd - 1))
                ac.activation(relu[:, hd % 2, :], PA[:, hd % 4, 0:384], ACT.Relu).then_inc(S("relu"), 1)
            attention("")
            x_hi("ao")
            for u in range(8, 12):
                hi(u)
            x_hi("n1")
            ffn(0, U_F0, "f0")
            hi(U_H + 2)
            x_hi("n2")
            act.wait_ge(S("lb_diff"), 1)
            ac.activation(lb1, lb1, ACT.Exp).then_inc(S("lb_exp"), 1)

            def gate(dst, j, ps, what):
                ac.activation(dst[:, :, j * HALF:(j + 1) * HALF], ps, ACT.Sigmoid).then_inc(S(what), 1)

            hi(U_H + 3)
            full(U_H + 1)
            gate(kr, 0, PG[:, :, :], "f_sig")
            hi(U_H + 4)
            hi(U_H + 5)
            full(U_H + 3)
            gate(kr, 1, PA[:, 0:2, :], "f_sig")
            hi(U_H + 6)
            hi(U_H + 7)
            full(U_H + 5)
            gate(qh, 0, PA[:, 2:4, :], "q_sig")
            hi(U_H + 8)
            hi(U_H + 9)
            full(U_H + 7)
            gate(qh, 1, PG[:, :, :], "q_sig")
            for j in range(2):
                act.wait_ge(S("fg"), j + 1)
                lv = lf[:, :, j * HALF:(j + 1) * HALF]
                ac.activation(lv, lv, ACT.Ln).then_inc(S("logf"), 1)
            hi(U_H + 10)
            hi(U_H + 11)
            full(U_H + 9)
            ac.activation(vi[:, :, 0:HALF], PA[:, 0:2, :], ACT.Copy).then_inc(S("vi"), 1)
            for b in range(4):
                act.wait_ge(S("cum"), b + 1)
                ac.activation(flat(bT[:, 2 * b:2 * b + 2, :]), PA[:, 2 + b % 2, :], ACT.Copy).then_inc(S("bT"), 1)
            hi(U_H + 12)
            copy_turned("hk", kTh)
            copy_turned("hq", qTh)

            def level_exp(l):
                act.wait_ge(S("lv_d"), 2 * l + 2)
                d = flat(dls[l % 3])
                ac.activation(d, d, ACT.Exp).then_inc(S("lv_e"), 1)

            level_exp(0)
            hi(U_H + 13)
            full(U_H + 11)
            ac.activation(vi[:, :, HALF:D], PG[:, :, :], ACT.Copy).then_inc(S("vi"), 1)
            level_exp(1)
            hi(U_H + 14)
            level_exp(2)
            hi(U_H + 15)
            full(U_H + 13)
            ac.activation(sg[:, :, 0:HALF], PG[:, :, :], ACT.Copy).then_inc(S("g_raw"), 1)
            hi(U_H + 16)
            level_exp(3)
            hi(U_H + 17)
            level_exp(4)
            full(U_H + 15)
            ac.activation(sg[:, :, HALF:D], PG[:, :, :], ACT.Copy).then_inc(S("g_raw"), 1)
            hi(U_H + 18)
            level_exp(5)
            level_exp(6)
            act.wait_ge(S("lv_d"), 14 + 4)
            ac.activation(flat(dls[7 % 3]), flat(dls[7 % 3]), ACT.Exp).then_inc(S("lv_e"), 1)
            act.wait_ge(S("g_raw"), 2)
            ac.activation(flat(bT), flat(sg), ACT.Sigmoid).then_inc(S("g_sig"), 1)
            for b in range(4):
                act.wait_ge(S("ho"), b + 1)
                ac.activation(flat(sqh)[:, b * 512:(b + 1) * 512], PA[:, b, :], ACT.Square)\
                  .then_inc(S("ho_sq"), 1)
            x_hi("ho")
            for u in range(U_HO + 3, U_F1 + 3):
                hi(u)
            x_hi("n3")
            ffn(1, U_F1, "f1")
            hi(U_M + 2)
            x_hi("y1")

            dsts = (q2, q2, k2, k2, v2, v2)
            banks = (PG[:, :, :], PA[:, 0:2, :], PA[:, 2:4, :])
            for c in range(6):
                hi(U_M + 2 * c + 3)
                full(U_M + 2 * c + 1)
                dst = dsts[c][:, :, (c % 2) * HALF:(c % 2 + 1) * HALF]
                ac.activation(dst, banks[c % 3], ACT.Copy, scale=-HD ** -0.5 if c < 2 else 1.0)\
                  .then_inc(S("qkv"), 1)
                hi(U_M + 2 * c + 4)
            copy_turned("q2", qT)
            copy_turned("k2", k2T)
            attention("2")
            x_hi("ao2")
            for u in range(U_MO + 3, U_F2 + 3):
                hi(u)
            x_hi("y2")

            U, T0 = U_F2, ev["f2"]

            def rows_out(i, u):
                act.wait_ge(S("w_used"), i * 3 + (u + 1))
                if not isinstance(i, int) or i > 0:
                    act.wait_ge(S("t_full"), i * 2 + T0)
                ac.activation(urow, PG[:, :, :], ACT.Copy).then_inc(S("urow"), 1)

            def conv_first(i):
                act.wait_ge(S("cwi"), i + 1)
                if not isinstance(i, int) or i > 0:
                    act.wait_ge(S("hidden_t"), i)
                for s in range(2):
                    act.wait_ge(S("t_full"), i * 2 + (T0 + s + 1))
                    for f in range(2):
                        ac.activation(cv[:, 2 * s + f, :], TB[:, (T0 + s) % 2, f * T:(f + 1) * T], ACT.Identity,
                                      scale=cwi[:, 2, s, f:f + 1], bias=cwi[:, 3, s, f:f + 1])\
                          .then_inc(S("conv0"), 1)
                act.wait_ge(S("t_free"), i * 2 + (T0 + 2))
                ac.activation(ce, cv[:, 0:2, :], ACT.Sigmoid).then_inc(S("cgate"), 1)

            def conv_hi(i):
                act.wait_ge(S("hidden_t"), i + 1)
                if not isinstance(i, int) or i > 0:
                    act.wait_ge(S("w_used"), i * 3 + (U + 2))
                ac.activation(fhi[:, :, :], fhT, ACT.Copy).then_inc(S("c_hi"), 1)

            def cstep(i):
                at = (lambda u: hi(u, i)) if not isinstance(i, int) else (lambda u: hi(u + 3 * i))
                conv_first(i - 1)
                at(U + 2)
                conv_hi(i - 1)
                rows_out(i, U)
                at(U + 3)
                at(U + 4)

            hi(U + 3)
            rows_out(0, U + 1)
            hi(U + 4)
            cstep(1)
            with act.Fori(2, NFF - 1) as i:
                cstep(i)
            cstep(NFF - 1)
            conv_first(NFF - 1)
            conv_hi(NFF - 1)

        @block.vector
        def _(vec):
            ve_ = nc.vector
            link = Chain(vec, S("vec_chain"))

            def turned(e):
                vec.wait_ge(S("t_full"), e + 1)

            def full(u):
                vec.wait_ge(S("w_used"), u + 1)

            nxhi = [0]

            def lo_of_bank(dst, e, src_hi):
                nxhi[0] += 1
                vec.wait_ge(S("x_hi"), nxhi[0])
                ve_.tensor_tensor(dst, TB[:, e % 2, 0:dst.shape[1]], src_hi.bitcast(F32), ALU.subtract)\
                   .then_inc(S("t_free"), 1)

            def x_lo(name, k=4):
                for g in range(k):
                    lo_of_bank(flat(xlo[:, 2 * g:2 * g + 2, :]), ev[name] + g, flat(xhi[:, 2 * g:2 * g + 2, :]))

            def rope(x, heads, half, c0):
                n_ = heads * half
                cos = trig[:, :, 0, c0:c0 + half].unsqueeze(2).broadcast_to([P, RT, heads, half])
                sin = trig[:, :, 1, c0:c0 + half].unsqueeze(2).broadcast_to([P, RT, heads, half])
                x1, x2 = x[:, :, :, 0:half], x[:, :, :, half:2 * half]
                r = [t[:, :, 0:n_].rearrange("p r (g c) -> p r g c", g=heads) for t in (rt1, rt2, rt3, rt4)]
                ve_.tensor_tensor(r[0], x1, cos, ALU.mult)
                ve_.tensor_tensor(r[1], x2, sin, ALU.mult)
                ve_.tensor_tensor(r[2], x2, cos, ALU.mult)
                link(ve_.tensor_tensor(r[3], x1, sin, ALU.mult))
                ve_.tensor_tensor(x1, r[0], r[1], ALU.subtract)
                return ve_.tensor_tensor(x2, r[2], r[3], ALU.add)

            def attention(tag, bias):
                o_at = lambda g: PG[:, g % 2, :].rearrange("p (h r c) -> p h r c", h=4, r=2)

                def minima(hd):
                    vec.wait_ge(S("logit" + tag), hd + 1)
                    if hd >= 3:
                        vec.wait_ge(S("t_full"), ev["pt" + tag] + hd - 2)
                    for r, (a, b) in enumerate(((0, 128), (128, 384))):
                        ve_.tensor_tensor_reduce(pr[:, hd % 3, a:b], PA[:, hd % 4, a:b], bias(hd, r), 1.0, 3e38,
                                                 ALU.add, ALU.min, amin[:, hd, r:r + 1])\
                           .then_inc(S("amin" + tag), 1)

                def turn_out(hd):
                    e = ev["pt" + tag] + hd
                    turned(e)
                    if hd >= 3:
                        vec.wait_ge(S("pv" + tag), hd - 2)
                    ve_.tensor_copy(pT[:, hd % 3, :], TB[:, e % 2, 0:384]).then_inc(S("t_free"), 1)

                def outputs(g):
                    vec.wait_ge(S("prob" + tag), 2 * (4 * g + 4))
                    link(ve_.reciprocal(arec[:, 4 * g:4 * g + 4, :], asum[:, 4 * g:4 * g + 4, :]))
                    vec.wait_ge(S("pv" + tag), 4 * g + 4)
                    for r in range(RT):
                        o = orow[:, r, 256 * g:256 * g + 256].rearrange("p (h c) -> p h c", h=4)
                        rb = arec[:, 4 * g:4 * g + 4, r:r + 1].broadcast_to([P, 4, HD])
                        ve_.tensor_tensor(o, o_at(g)[:, :, r, :], rb, ALU.mult).then_inc(S("orow" + tag), 1)

                for i in range(HQ + 3):
                    if i < HQ:
                        minima(i)
                    if 1 <= i <= HQ:
                        turn_out(i - 1)
                    if i >= 6 and (i - 6) % 4 == 0 and (i - 6) // 4 < 3:
                        outputs((i - 6) // 4)
                outputs(3)

            def residual(scale, u):
                for r in range(RT):
                    if r == 0:
                        vec.wait_ge(S("first_rows"), res[0] + 1)
                    else:
                        full(u)
                    for f in range(2):
                        hv_ = h[:, r, f * HALF:(f + 1) * HALF]
                        ins = ve_.scalar_tensor_tensor(out=hv_, in0=hv_, scalar=scale, in1=PA[:, 2 * r + f, :],
                                                       op0=ALU.mult, op1=ALU.add)
                    link(ins)
                    for f in range(2):
                        ins = ve_.bn_stats(stats[:, r, f, :], h[:, r, f * HALF:(f + 1) * HALF])
                    link(ins)
                    ins = ve_.bn_aggr(mv[:, r, :], stats[:, r, :, :].rearrange("p a b -> p (a b)"))
                link(ins)
                res[0] += 1

            res = [0]

            def moments():
                for r in range(RT):
                    for f in range(2):
                        ins = ve_.bn_stats(stats[:, r, f, :], h[:, r, f * HALF:(f + 1) * HALF])
                link(ins)
                for r in range(RT):
                    ins = ve_.bn_aggr(mv[:, r, :], stats[:, r, :, :].rearrange("p a b -> p (a b)"))
                link(ins)

            def layer_norm(k, call):
                ve_.tensor_scalar(ve[:, 0:2], mv[:, 0:2, 1], LN_EPS, None, ALU.add).then_inc(S("ve"), 1)
                vec.wait_ge(S("rstd"), call + 1)
                vec.wait_ge(S("gb"), GB_COUNT[k])
                for f in range(2):
                    cols = slice(f * HALF, (f + 1) * HALF)
                    for r in range(RT):
                        ins = ve_.scalar_tensor_tensor(out=h[:, r, cols], in0=h[:, r, cols], scalar=mv[:, r, 0:1],
                                                       in1=gvec[:, cols], op0=ALU.subtract, op1=ALU.mult)
                    link(ins)
                    for r in range(RT):
                        ins = ve_.scalar_tensor_tensor(out=h[:, r, cols], in0=h[:, r, cols], scalar=rstd[:, r:r + 1],
                                                       in1=bvec[:, cols], op0=ALU.mult, op1=ALU.add)
                    ins.then_inc(S("norm"), 1)

            def rms_norm(k, call, dst):
                link(ve_.tensor_tensor(ve[:, 8:10], mv[:, 0:2, 0], mv[:, 0:2, 0], ALU.mult))
                ve_.scalar_tensor_tensor(out=ve[:, 0:2], in0=ve[:, 8:10], scalar=RMS_EPS, in1=mv[:, 0:2, 1],
                                         op0=ALU.add, op1=ALU.add).then_inc(S("ve"), 1)
                vec.wait_ge(S("rstd"), call + 1)
                vec.wait_ge(S("gb"), GB_COUNT[k])
                for f in range(2):
                    cols = slice(f * HALF, (f + 1) * HALF)
                    for r in range(RT):
                        ins = ve_.scalar_tensor_tensor(out=dst[:, r, cols], in0=h[:, r, cols],
                                                       scalar=rstd[:, r:r + 1], in1=gvec[:, cols],
                                                       op0=ALU.mult, op1=ALU.mult)
                    ins.then_inc(S("norm"), 1)

            def ffn(k, U, name):
                T0 = ev[name]
                x0 = nxhi[0]

                def f_lo(i):
                    for f in range(2):
                        vec.wait_ge(S("x_hi"), i * 2 + (x0 + f + 1))
                        ve_.tensor_tensor(flo[:, f, :], TB[:, (T0 + f) % 2, 0:T], fhi[:, f, :].bitcast(F32),
                                          ALU.subtract).then_inc(S("t_free"), 1)

                def hidden(i):
                    vec.wait_ge(S("gate"), i + (k * NFF + 1))
                    ve_.tensor_tensor(fh, PG[:, :, 0:FC], fe, ALU.mult).then_inc(S("vec_chain"), 1)
                    vec.wait_ge(S("vec_chain"), i + (c0 + 1))
                    ve_.tensor_tensor(fh, fh, PG[:, :, FC:2 * FC], ALU.mult).then_inc(S("hidden"), 1)

                def step(i):
                    at = (lambda u: lo(u, i)) if not isinstance(i, int) else (lambda u: lo(u + 3 * i))
                    f_lo(i - 1)
                    at(U + 2)
                    hidden(i)
                    at(U + 3)
                    if not isinstance(i, int):
                        at(U + 4)

                c0 = link.n
                lo(U + 3)
                hidden(0)
                lo(U + 4)
                with vec.Fori(1, NFF - 1) as i:
                    step(i)
                step(NFF - 1)
                f_lo(NFF - 1)
                link.n += NFF
                nxhi[0] += 2 * NFF

            vec.wait_ge(S("pos"), 48)
            link(ve_.tensor_copy(posf, posi.bitcast(I32)))
            for r in range(RT):
                for s in range(2):
                    ins = ve_.tensor_scalar(ang[:, r, s, :], inv, posf[:, r:r + 1], None, ALU.mult)
            link(ins)
            for s in range(2):
                ins = ve_.tensor_scalar(turns[:, :, s, :], ang[:, :, s, :], 1 / (2 * np.pi), 0.25 * (1 - s),
                                        ALU.mult, ALU.add)
            link(ins)
            link(ve_.tensor_scalar(turns, turns, ROUND, ROUND, ALU.add, ALU.subtract))
            for part in (PI2_1, PI2_2, PI2_3):
                a2, t2 = (z.rearrange("p a b c -> p (a b c)") for z in (ang, turns))
                link(ve_.scalar_tensor_tensor(out=a2, in0=t2, scalar=-part, in1=a2, op0=ALU.mult, op1=ALU.add))
            link(ve_.tensor_scalar(ang[:, :, 0, :], ang[:, :, 0, :], np.pi / 2, None, ALU.add))
            lim = float(np.float32(3.1415925))
            ve_.tensor_scalar(ang, ang, lim, -lim, ALU.min, ALU.max).then_inc(S("ang"), 1)

            x_lo("x")
            for u in range(3):
                lo(u)
            e = ev["c0"]
            turned(e)
            ve_.tensor_copy(relT[0:BUCKETS, :], TB[0:BUCKETS, e % 2, 0:HQ]).then_inc(S("t_free"), 1)
            turned(e + 1)
            ve_.tensor_copy(cw[:, :, :], TB[:, (e + 1) % 2, 0:176].rearrange("p (j c) -> p j c", j=4))\
               .then_inc(S("t_free"), 1)
            vec.wait_ge(S("reldist"), 1)
            ve_.tensor_scalar(relv[0:HQ, 0:T], PA[0:HQ, 2, 0:T], -1.0, None, ALU.mult).then_inc(S("relv"), 1)
            ve_.memset(relv[0:HQ, T:REL_W], -NEG).then_inc(S("relv"), 1)
            full(2)
            link(ve_.tensor_copy(pin[:, :, 512:IN_COLS], PA[:, 0:2, 0:IN_COLS - 512]))
            vec.wait_ge(S("small"), 48)
            for r in range(RT):
                ins = ve_.bn_stats(stats[:, r, 0, :], pin[:, r, C_KI:C_WI])
            link(ins)
            for r in range(RT):
                ins = ve_.bn_aggr(mv[:, 2 + r, :], stats[:, r, 0, :])
            link(ins)
            ve_.tensor_scalar(ve[:, 2:4], mv[:, 2:4, 1], LN_EPS, None, ALU.add)
            vec.wait_ge(S("ssq"), RT)
            ve_.tensor_scalar(ve[:, 0:2], ve[:, 8:10], 1.0 / NQL, RMS_EPS, ALU.mult, ALU.add).then_inc(S("ve"), 1)
            ve_.tensor_scalar(wsc, pin[:, :, C_WI:IN_COLS], HI ** -0.5 * DI ** -0.5, None, ALU.mult)
            vec.wait_ge(S("rstd"), 1)
            vec.wait_ge(S("pin"), 1)
            for r in range(RT):
                ins = ve_.scalar_tensor_tensor(out=cqn[:, r, :], in0=pin[:, r, 0:NQL], scalar=rstd[:, r:r + 1],
                                               in1=gcq, op0=ALU.mult, op1=ALU.mult)
            ins.then_inc(S("cqn"), 1)
            for r in range(RT):
                kv_ = pin[:, r, C_KI:C_WI]
                link(ve_.tensor_scalar(kv_, kv_, mv[:, 2 + r, 0:1], rstd[:, 2 + r:3 + r], ALU.subtract, ALU.mult))
                link(ve_.tensor_tensor(kv_, kv_, gki, ALU.mult))
                link(ve_.tensor_tensor(kv_, kv_, bki, ALU.add))
            lo_of_bank(flat(xlo[:, 0:2, :]), ev["cq"], flat(xhi[:, 0:2, :]))
            vec.wait_ge(S("trig"), 1)
            link(rope(pin[:, :, C_KI:C_WI].rearrange("p r (g c) -> p r g c", g=1), 1, ROTI, ROT))
            link(rope(pin[:, :, C_K:C_V].rearrange("p r (g c) -> p r g c", g=2), 2, ROT, 0))
            for r in range(RT):
                for c in range(2):
                    ins = ve_.tensor_copy(kd[:, r, :, c, :],
                                          pin[:, r, C_K:C_V].rearrange("p (g c) -> p g c", g=2))
            ins.then_inc(S("kd"), 1)
            lo(3)
            lo(4)
            lo(5)
            full(U_IQ)
            ve_.tensor_copy(qi[:, 1, :], flat(PA[:, 2:4, :])).then_inc(S("qi_b"), 1)
            vec.wait_ge(S("qi_b"), 1)
            vec.wait_ge(S("qi_a"), 1)
            rope(qi.rearrange("p r (g c) -> p r g c", g=HI), HI, ROTI, ROT).then_inc(S("qi_r"), 1)
            lo(6)
            e = ev["ki"]
            turned(e)
            ve_.tensor_copy(flat(kT), TB[:, e % 2, :]).then_inc(S("t_free"), 1)
            turned(e + 1)
            ve_.tensor_copy(kiT, TB[:, (e + 1) % 2, 0:T]).then_inc(S("t_free"), 1)
            full(U_UQ)
            link(ve_.tensor_scalar(qr[:, 1, :], flat(PA[:, 2:4, :]), -HD ** -0.5, None, ALU.mult))
            vec.wait_ge(S("q_a"), 1)
            rope(qr.rearrange("p r (g c) -> p r g c", g=HQ), HQ, ROT, 0).then_inc(S("q_r"), 1)
            lo(7)
            for hd in range(HI):
                vec.wait_ge(S("relu"), hd + 1)
                if hd:
                    vec.wait_ge(S("iacc"), 2 * hd)
                for r, (a, b) in enumerate(((0, 128), (128, 384))):
                    src, dst = relu[:, hd % 2, a:b], score[:, a:b]
                    wv = wsc[:, r, hd:hd + 1]
                    if hd == 0:
                        ins = ve_.tensor_scalar(dst, src, wv, None, ALU.mult)
                    else:
                        ins = ve_.scalar_tensor_tensor(out=dst, in0=src, scalar=wv, in1=dst,
                                                       op0=ALU.mult, op1=ALU.add)
                    ins.then_inc(S("iacc"), 1)
            vec.wait_ge(S("score_causal"), 1)
            for k in range(TOPK // 8):
                src = score if k == 0 else left
                for r, (a, b) in enumerate(((0, 128), (128, 384))):
                    ins = ve_.max(m8[:, r, :], src[:, a:b])
                link(ins)
                for r, (a, b) in enumerate(((0, 128), (128, 384))):
                    ins = ve_.match_replace(left[:, a:b], m8[:, r, :], src[:, a:b], TAKEN)
                link(ins)
            ve_.tensor_scalar(mask, left, (CAUSAL_FILL + TAKEN) / 2, -NEG, ALU.is_gt, ALU.mult)\
               .then_inc(S("mask"), 1)
            vec.wait_ge(S("mask_causal"), 1)
            attention("", lambda hd, r: mask[:, 0:128] if r == 0 else mask[:, 128:384])
            x_lo("ao")
            for u in range(U_AO + 3, U_F0 + 2):
                lo(u)
            residual(ALPHA, U_AO + 3)
            layer_norm(0, 1)
            x_lo("n1")
            lo(U_F0 + 2)
            ffn(0, U_F0, "f0")
            residual(ALPHA, U_F0 + N_F - 1)
            layer_norm(1, 2)
            x_lo("n2")
            lo(U_H + 1)
            lo(U_H + 2)

            vec.wait_ge(S("hconst"), 1)
            vec.wait_ge(S("lb_loaded"), 48)
            ve_.tensor_tensor(lb1, lb, lb1, ALU.subtract).then_inc(S("lb_diff"), 1)
            vec.wait_ge(S("lb_exp"), 1)
            link(ve_.tensor_scalar(lb1, lb1, 1.0, None, ALU.add))
            link(ve_.reciprocal(lb, lb1))
            link(ve_.tensor_scalar(lb1, lb, -1.0, 1.0, ALU.mult, ALU.add))

            def forget(j):
                cols = slice(j * HALF, (j + 1) * HALF)
                v = kr[:, :, cols]
                lbb = lb[:, cols].unsqueeze(1).broadcast_to([P, RT, HALF])
                lb1b = lb1[:, cols].unsqueeze(1).broadcast_to([P, RT, HALF])
                vec.wait_ge(S("f_sig"), j + 1)
                link(ve_.tensor_tensor(v, v, lb1b, ALU.mult))
                link(ve_.tensor_tensor(v, v, lbb, ALU.add))
                ve_.tensor_scalar(lf[:, :, cols], v, 2.0 ** -63, None, ALU.max).then_inc(S("fg"), 1)
                ve_.tensor_scalar(v, v, -1.0, 1.0, ALU.mult, ALU.add).then_inc(S("kr"), 1)

            def silu(j, ps):
                v = qh[:, :, j * HALF:(j + 1) * HALF]
                vec.wait_ge(S("q_sig"), j + 1)
                ve_.tensor_tensor(v, v, ps, ALU.mult).then_inc(S("qh"), 1)

            lo(U_H + 3)
            forget(0)
            lo(U_H + 4)
            lo(U_H + 5)
            forget(1)
            lo(U_H + 6)
            lo(U_H + 7)
            silu(0, PA[:, 2:4, :])
            lo(U_H + 8)
            lo(U_H + 9)
            silu(1, PG[:, :, :])
            lo(U_H + 10)
            lo(U_H + 11)

            def products(l):
                vec.wait_ge(S("lv_e"), l + 1)
                m = ((CHUNK,) + LEVELS)[l]
                d, k_, q_ = (flat(z).rearrange("p (b s m) -> p b s m", s=2, m=m)
                             for z in (dls[l % 3], kTh, qTh))
                ve_.tensor_tensor(d[:, :, 0, :], d[:, :, 0, :], k_[:, :, 0, :], ALU.mult).then_inc(S("lv_x"), 1)
                ve_.tensor_tensor(d[:, :, 1, :], d[:, :, 1, :], q_[:, :, 1, :], ALU.mult).then_inc(S("lv_x"), 1)

            def take(l):
                n_, n0 = (P, 0) if l == 7 else (P // 2, 4)
                for b in range(4):
                    vec.wait_ge(S("lv_full" if l < 7 else "diag_full"), 4 * l + b + 1 if l < 7 else b + 1)
                    for r in range(RT):
                        dst = aT[:, r, 2 * b:2 * b + 2, :]
                        src = PA[:, b, r * 2 * n_:(r + 1) * 2 * n_].rearrange("p (h c) -> p h c", h=2)
                        mk = maskt[:, l, :]
                        if l < 7:
                            m = ((CHUNK,) + LEVELS)[l]
                            dst = dst.rearrange("p h (b s m) -> p h b s m", s=2, m=m)[:, :, :, 1, :]
                            src = src.rearrange("p h (b m) -> p h b m", m=m)
                            mk = mk.rearrange("p (b s m) -> p b s m", s=2, m=m)[:, :, 1, :]
                        for c in range(2):
                            ins = ve_.copy_predicated(dst[:, c], mk, src[:, c])
                    ins.then_inc(S("lv_taken"), 1)

            lo(U_H + 12)
            vec.wait_ge(S("t_free"), ev["hq"] + 4)
            take(7)
            products(0)
            lo(U_H + 13)
            products(1)
            take(0)
            lo(U_H + 14)
            products(2)
            lo(U_H + 15)
            take(1)
            take(2)
            lo(U_H + 16)
            products(3)
            lo(U_H + 17)
            products(4)
            take(3)
            lo(U_H + 18)
            products(5)
            take(4)
            products(6)
            take(5)
            vec.wait_ge(S("lv_e"), 8)
            dx = dls[7 % 3]
            ve_.tensor_tensor(dx[:, :, 0:P], dx[:, :, 0:P], kTh[:, :, 0:P], ALU.mult).then_inc(S("lv_x"), 1)
            ve_.tensor_tensor(dx[:, :, P:T], dx[:, :, P:T], qTh[:, :, P:T], ALU.mult).then_inc(S("lv_x"), 1)
            take(6)
            for b in range(2):
                vec.wait_ge(S("lv_cross"), b + 1)
                ve_.tensor_copy(flat(aT[:, 2, 4 * b:4 * b + 4, :]), PG[:, b, :]).then_inc(S("aT2"), 1)
            vec.wait_ge(S("g_sig"), 1)
            link(ve_.tensor_tensor(flat(sg), flat(sg), flat(bT), ALU.mult))
            sv = flat(sg).rearrange("p (g c) -> p g c", c=DH)
            ve_.tensor_tensor(sv, sv, gno.unsqueeze(1).broadcast_to([P, RT * HH, DH]), ALU.mult)\
               .then_inc(S("sg"), 1)
            for b in range(4):
                vec.wait_ge(S("ho_sq"), b + 1)
                ins = ve_.tensor_reduce(ssq[:, 4 * b:4 * b + 4],
                                        flat(sqh)[:, b * 512:(b + 1) * 512].rearrange("p (g c) -> p g c", g=4),
                                        AXX, ALU.add)
            link(ins)
            ve_.tensor_scalar(ve[:, 0:16], ssq, 1.0 / DH, RMS_EPS, ALU.mult, ALU.add).then_inc(S("ve"), 1)
            vec.wait_ge(S("rstd"), 4)
            vec.wait_ge(S("sg"), 1)
            for b in range(4):
                for r in range(RT):
                    for c in range(2):
                        hd, g = 2 * b + c, 4 * b + 2 * r + c
                        cols = slice(hd * DH, (hd + 1) * DH)
                        ins = ve_.scalar_tensor_tensor(
                            out=oh[:, r, cols], in0=PA[:, b, (2 * r + c) * P:(2 * r + c + 1) * P],
                            scalar=rstd[:, g:g + 1], in1=sg[:, r, cols], op0=ALU.mult, op1=ALU.mult)
                ins.then_inc(S("oh"), 1)
            x_lo("ho")
            for u in range(U_HO + 3, U_F1 + 2):
                lo(u)
            residual(ALPHA, U_HO + 3)
            layer_norm(2, 4)
            x_lo("n3")
            lo(U_F1 + 2)
            ffn(1, U_F1, "f1")
            residual(ALPHA, U_F1 + N_F - 1)
            layer_norm(3, 5)

            vec.wait_ge(S("norm"), 8)
            moments()
            rms_norm(4, 6, orow)
            x_lo("y1")
            for u in range(U_M + 1, U_M + 15):
                lo(u)
            vec.wait_ge(S("relb"), 16)
            attention("2", lambda hd, r: relb[:, hd, 128:256] if r == 0 else relb[:, hd, :])
            x_lo("ao2")
            for u in range(U_MO + 3, U_F2 + 2):
                lo(u)
            residual(1.0, U_MO + 3)
            rms_norm(5, 7, orow)
            x_lo("y2")
            lo(U_F2 + 2)

            U, T0 = U_F2, ev["f2"]
            c0 = link.n

            def conv(i):
                for f in range(4):
                    b_, o_ = (T0 + f // 2) % 2, (f % 2) * T
                    vec.wait_ge(S("conv0"), i * 4 + (2 * (f // 2) + 2))
                    ins = ve_.scalar_tensor_tensor(out=cv[:, f, 1:T], in0=TB[:, b_, o_:o_ + T - 1],
                                                   scalar=cwi[:, 1, f // 2, f % 2:f % 2 + 1], in1=cv[:, f, 1:T],
                                                   op0=ALU.mult, op1=ALU.add)
                ins.then_inc(S("vec_chain"), 1)
                vec.wait_ge(S("vec_chain"), i + (c0 + 1))
                for f in range(4):
                    b_, o_ = (T0 + f // 2) % 2, (f % 2) * T
                    ins = ve_.scalar_tensor_tensor(out=cv[:, f, 2:T], in0=TB[:, b_, o_:o_ + T - 2],
                                                   scalar=cwi[:, 0, f // 2, f % 2:f % 2 + 1], in1=cv[:, f, 2:T],
                                                   op0=ALU.mult, op1=ALU.add)
                    if f % 2:
                        ins.then_inc(S("t_free"), 1)
                vec.wait_ge(S("cgate"), i + 1)
                vec.wait_ge(S("cgv"), i + 1)
                if not isinstance(i, int) or i > 0:
                    vec.wait_ge(S("c_lo"), i)
                ve_.tensor_tensor(fhT, cgv, ce, ALU.mult).then_inc(S("hidden_t"), 1)

            def conv_lo(i):
                vec.wait_ge(S("c_hi"), i + 1)
                ve_.tensor_tensor(flo[:, :, :], fhT, fhi[:, :, :].bitcast(F32), ALU.subtract).then_inc(S("c_lo"), 1)

            def weights(i):
                if not isinstance(i, int) or i > 0:
                    vec.wait_ge(S("t_free"), i * 2 + T0)
                cwv = cw[:, :, :].rearrange("p j (s c) -> p j s c", s=2)
                ve_.tensor_copy(cwi[:, :, :, :], cwv[:, :, :, bass.ds(i * 2, 2)]).then_inc(S("cwi"), 1)

            def step(i):
                at = (lambda u: lo(u, i)) if not isinstance(i, int) else (lambda u: lo(u + 3 * i))
                weights(i - 1)
                conv(i - 1)
                conv_lo(i - 1)
                at(U + 2)
                at(U + 3)
                at(U + 4)

            lo(U + 3)
            lo(U + 4)
            step(1)
            with vec.Fori(2, NFF - 1) as i:
                step(i)
            step(NFF - 1)
            weights(NFF - 1)
            conv(NFF - 1)
            conv_lo(NFF - 1)
            link.n += NFF
            residual(1.0, U_F2 + N_F - 1)
            rms_norm(6, 8, h)

        @block.tensor
        def _(pe):
            mm = nc.tensor.matmul

            def t_bank(e):
                if e >= 2:
                    pe.wait_ge(S("t_free"), e - 1)

            def parts_ready(e):
                pe.wait_ge(S("t_free"), e + 1)

            def turn_rows(name, rows, ready=None):
                for g in range(4):
                    e = ev[name] + g
                    t_bank(e)
                    if ready:
                        ready(g)
                    for k in range(2):
                        for r in range(RT):
                            last = nc.tensor.transpose(TB[:, e % 2, (2 * k + r) * P:(2 * k + r + 1) * P],
                                                       rows[:, r, (2 * g + k) * P:(2 * g + k + 1) * P], ident[:, :])
                    last.then_inc(S("t_full"), 1)

            def products(dst, k, r, slot, cols, first, last_, xh=None, xl=None):
                xh, xl = (xhi if xh is None else xh), (xlo if xl is None else xl)
                rows = slice(r * P, (r + 1) * P)
                mm(dst, xl[:, k, rows], whi[:, slot, cols], start=first, stop=False)
                mm(dst, xh[:, k, rows], wlo[:, slot, cols], start=False, stop=False)
                return mm(dst, xh[:, k, rows], whi[:, slot, cols], start=False, stop=last_)

            def up(u, bank, j=0, x_event=None):
                for s in range(2):
                    slot = (u + s) % RING
                    pe.wait_ge(S("w_lo"), j * 3 + (u + s + 1))
                    for t in range(4):
                        k = 4 * s + t
                        if x_event is not None and k % 2 == 0:
                            parts_ready(x_event + k // 2)
                        for r in range(RT):
                            last = products(bank(r), k, r, slot, slice(t * 512, (t + 1) * 512), k == 0, k == KT - 1)
                    last.then_inc(S("w_used"), 1)

            def down(u, k0, first, last_, j=0, xh=None, xl=None, ends=True):
                slot = u % RING
                pe.wait_ge(S("w_lo"), j * 3 + (u + 1))
                def tile(t, r):
                    for f in range(2):
                        ins = products(PA[:, 2 * r + f, :], k0 + t, r, slot,
                                       slice(t * D + f * 512, t * D + (f + 1) * 512),
                                       first and t == 0, last_ and t == 1, xh, xl)
                    return ins

                if not (last_ and ends):
                    for t in range(2):
                        for r in range(RT):
                            last = tile(t, r)
                    last.then_inc(S("w_used"), 1)
                    return
                for r in range(RT):
                    for t in range(2):
                        last = tile(t, r)
                    last.then_inc(S("w_used" if r else "first_rows"), 1)

            def attention(tag, keys, value):
                e0 = ev["pt" + tag]

                def logits(hd):
                    if hd >= 4:
                        pe.wait_ge(S("amin" + tag), 2 * (hd - 3))
                    rows = slice(HD * (hd % 2), HD * (hd % 2) + HD)
                    for r, (a, n_) in enumerate(((0, 128), (128, 256))):
                        dst = PA[:, hd % 4, a:a + n_]
                        last = mm(dst, qT[rows, hd // 2, r * P:(r + 1) * P], keys(hd)[rows, 0:n_],
                                  start=True, stop=True)
                    last.then_inc(S("logit" + tag), 1)

                def turn(hd):
                    t_bank(e0 + hd)
                    pe.wait_ge(S("prob" + tag), 2 * hd + 2)
                    for c in range(3):
                        last = nc.tensor.transpose(TB[:, (e0 + hd) % 2, c * P:(c + 1) * P],
                                                   pr[:, hd % 3, c * P:(c + 1) * P], ident[:, :])
                    last.then_inc(S("t_full"), 1)

                def pv(hd):
                    parts_ready(e0 + hd)
                    g = hd // 4
                    if hd % 4 == 0 and g >= 2:
                        pe.wait_ge(S("orow" + tag), 2 * (g - 1))
                    c = (hd % 4) * P
                    mm(PG[:, g % 2, c:c + HD], pT[:, hd % 3, 0:P], value(hd, 0), start=True, stop=True)
                    mm(PG[:, g % 2, c + HD:c + P], pT[:, hd % 3, P:2 * P], value(hd, 0), start=True, stop=False)
                    mm(PG[:, g % 2, c + HD:c + P], pT[:, hd % 3, 2 * P:3 * P], value(hd, 1), start=False, stop=True)\
                        .then_inc(S("pv" + tag), 1)

                for i in range(HQ + 2):
                    if i < HQ:
                        logits(i)
                    if 1 <= i <= HQ:
                        turn(i - 1)
                    if i >= 2:
                        pv(i - 2)

            def out_proj(U, name):
                for j in range(4):
                    parts_ready(ev[name] + j)
                    down(U + j, 2 * j, j == 0, j == 3)

            def ffn(U, name, x_event, turn, hidden_ready, g_free):
                bank = lambda r: PG[:, r, :]
                up(U, bank, 0, x_event)
                def step(i):
                    ii = i if not isinstance(i, int) else i
                    turn(i - 1)
                    g_free(i - 1)
                    up(U + 2 - 3, bank, i)
                    hidden_ready(i - 1)
                    down(U + 4 - 3, 0, False, False, i, fhi, flo)
                turn(0)
                g_free(0)
                up(U + 2, bank)
                hidden_ready(0)
                down(U + 4, 0, True, False, 0, fhi, flo)
                with pe.Fori(2, NFF) as i:
                    step(i)
                turn(NFF - 1)
                hidden_ready(NFF - 1)
                down(U + N_F - 1, 0, False, True, 0, fhi, flo)

            def swiglu(k, U, name, x_event):
                T0 = ev[name]

                def turn(i):
                    pe.wait_ge(S("hidden"), i + (k * NFF + 1))
                    for f in range(2):
                        pe.wait_ge(S("t_free"), i * 2 + (T0 + f - 1))
                        for r in range(RT):
                            last = nc.tensor.transpose(TB[:, (T0 + f) % 2, r * P:(r + 1) * P],
                                                       fh[:, r, f * P:(f + 1) * P], ident[:, :])
                        last.then_inc(S("t_full"), 1)

                ffn(U, name, x_event, turn, lambda i: pe.wait_ge(S("t_free"), i * 2 + (T0 + 2)), lambda i: None)

            pe.wait_ge(S("ident"), 1)
            pe.wait_ge(S("x_loaded"), 32)
            turn_rows("x", h)
            pe.wait_ge(S("cst_loaded"), 64)
            e = ev["c0"]
            t_bank(e)
            nc.tensor.transpose(TB[0:BUCKETS, e % 2, 0:HQ], relrow[0:HQ, :], ident[0:HQ, 0:HQ]).then_inc(S("t_full"), 1)
            t_bank(e + 1)
            for j in range(4):
                last = nc.tensor.transpose(TB[:, (e + 1) % 2, 44 * j:44 * j + 44], cw4[0:44, j, :], ident[0:44, 0:44])
            last.then_inc(S("t_full"), 1)
            up(U_IN, lambda r: PG[:, r, :], 0, ev["x"])
            pe.wait_ge(S("w_lo"), 3)
            for k in range(KT):
                for r in range(RT):
                    last = products(PA[:, r, 0:136], k, r, 2, slice(k * 136, (k + 1) * 136), k == 0, k == KT - 1)
            last.then_inc(S("w_used"), 1)
            parts_ready(e)
            mm(PA[0:HQ, 2, 0:T], relT[0:BUCKETS, :], hot[0:BUCKETS, :], start=True, stop=True).then_inc(S("reldist"), 1)
            e = ev["cq"]
            pe.wait_ge(S("cqn"), 1)
            t_bank(e)
            for k in range(2):
                for r in range(RT):
                    last = nc.tensor.transpose(TB[:, e % 2, (2 * k + r) * P:(2 * k + r + 1) * P],
                                               cqn[:, r, k * P:(k + 1) * P], ident[:, :])
            last.then_inc(S("t_full"), 1)
            parts_ready(e)
            pe.wait_ge(S("relv"), 1)
            down(U_IQ, 0, True, True, ends=False)
            e = ev["ki"]
            pe.wait_ge(S("kd"), 1)
            t_bank(e)
            for g in range(2):
                for r in range(RT):
                    last = nc.tensor.transpose(TB[:, e % 2, (2 * g + r) * P:(2 * g + r + 1) * P],
                                               kd[:, r, g, :, :].rearrange("p a b -> p (a b)"), ident[:, :])
            last.then_inc(S("t_full"), 1)
            t_bank(e + 1)
            for r in range(RT):
                last = nc.tensor.transpose(TB[:, (e + 1) % 2, r * P:(r + 1) * P], pin[:, r, C_KI:C_WI], ident[:, :])
            last.then_inc(S("t_full"), 1)
            pe.wait_ge(S("qi_a"), 1)
            pe.wait_ge(S("qi_b"), 1)
            down(U_UQ, 0, True, True, ends=False)
            parts_ready(ev["ki"] + 1)
            pe.wait_ge(S("qi_r"), 1)
            turn_rows("qi", qi)
            pe.wait_ge(S("q_r"), 1)
            turn_rows("q", qr)
            parts_ready(ev["q"] + 3)
            for hd in range(HI):
                if hd >= 4:
                    pe.wait_ge(S("relu"), hd - 3)
                mm(PA[:, hd % 4, 0:128], qiT[:, hd, 0:P], kiT[:, 0:P], start=True, stop=True)
                mm(PA[:, hd % 4, 128:384], qiT[:, hd, P:T], kiT, start=True, stop=True).then_inc(S("iscore"), 1)
            pe.wait_ge(S("mask_causal"), 1)
            attention("", lambda hd: kT[:, hd // 8, :],
                      lambda hd, r: pin[:, r, C_V + HD * (hd // 8):C_V + HD * (hd // 8) + HD])
            turn_rows("ao", orow, lambda g: pe.wait_ge(S("orow"), 2 * g + 2))
            out_proj(U_AO, "ao")
            turn_rows("n1", h, lambda g: pe.wait_ge(S("norm"), 1 + g // 2))
            swiglu(0, U_F0, "f0", ev["n1"])
            turn_rows("n2", h, lambda g: pe.wait_ge(S("norm"), 3 + g // 2))

            up(U_H, lambda r: PG[:, r, :], 0, ev["n2"])
            up(U_H + 2, lambda r: PA[:, r, :])
            up(U_H + 4, lambda r: PA[:, 2 + r, :])
            pe.wait_ge(S("f_sig"), 1)
            up(U_H + 6, lambda r: PG[:, r, :])
            pe.wait_ge(S("f_sig"), 2)
            up(U_H + 8, lambda r: PA[:, r, :])
            pe.wait_ge(S("qh"), 1)
            pe.wait_ge(S("logf"), 2)
            for b in range(4):
                if b >= 2:
                    pe.wait_ge(S("bT"), b - 1)
                for c in range(2):
                    for r in range(RT):
                        last = mm(PA[:, 2 + b % 2, (2 * c + r) * P:(2 * c + r + 1) * P],
                                  lf[:, r, (2 * b + c) * DH:(2 * b + c + 1) * DH], ucum, start=True, stop=True)
                last.then_inc(S("cum"), 1)
            pe.wait_ge(S("kr"), 2)
            turn_rows("hk", kr)
            pe.wait_ge(S("qh"), 2)
            turn_rows("hq", qh)
            parts_ready(ev["hq"] + 3)
            pe.wait_ge(S("bT"), 4)
            pe.wait_ge(S("vi"), 1)
            for b in range(4):
                for r in range(RT):
                    for c in range(2):
                        rows = slice(r * P, (r + 1) * P)
                        last = mm(PA[:, b, (2 * r + c) * P:(2 * r + c + 1) * P],
                                  kTh[:, 2 * b + c, rows], qTh[:, 2 * b + c, rows], start=True, stop=True)
                last.then_inc(S("diag_full"), 1)

            def level(l):
                pe.wait_ge(S("lv_x"), 2 * l + 2)
                d = dls[l % 3]
                m = ((CHUNK,) + LEVELS)[l]
                for b in range(4):
                    pe.wait_ge(S("lv_taken"), 4 * l + b + 1)
                    for r in range(RT):
                        for c in range(2):
                            dr = d[:, 2 * b + c, r * P:(r + 1) * P]
                            o = (2 * r + c) * CHUNK
                            last = mm(PA[:, b, o:o + CHUNK], dr,
                                      dr.rearrange("p (b s m) -> p b s m", s=2, m=m)[:, :, 1, :],
                                      start=True, stop=True)
                    last.then_inc(S("lv_full"), 1)

            up(U_H + 10, lambda r: PG[:, r, :])
            level(0)
            pe.wait_ge(S("vi"), 2)
            up(U_H + 12, lambda r: PG[:, r, :])
            level(1)
            level(2)
            pe.wait_ge(S("g_raw"), 1)
            up(U_H + 14, lambda r: PG[:, r, :])
            for l in range(3, 7):
                level(l)
            pe.wait_ge(S("lv_x"), 16)
            pe.wait_ge(S("g_raw"), 2)
            for b in range(2):
                for c in range(4):
                    last = mm(PG[:, b, c * P:(c + 1) * P], dls[7 % 3][:, 4 * b + c, 0:P],
                              dls[7 % 3][:, 4 * b + c, P:T], start=True, stop=True)
                last.then_inc(S("lv_cross"), 1)
            for b in range(4):
                pe.wait_ge(S("lv_taken"), 32)
                pe.wait_ge(S("aT2"), 2)
                for c in range(2):
                    hd = 2 * b + c
                    cols = slice(hd * DH, (hd + 1) * DH)
                    o0, o1 = (PA[:, b, (2 * r + c) * P:(2 * r + c + 1) * P] for r in range(RT))
                    mm(o0, aT[:, 0, hd, :], vi[:, 0, cols], start=True, stop=True)
                    mm(o1, aT[:, 2, hd, :], vi[:, 0, cols], start=True, stop=False)
                    last = mm(o1, aT[:, 1, hd, :], vi[:, 1, cols], start=False, stop=True)
                last.then_inc(S("ho"), 1)
            turn_rows("ho", oh, lambda g: pe.wait_ge(S("oh"), g + 1))
            out_proj(U_HO, "ho")
            turn_rows("n3", h, lambda g: pe.wait_ge(S("norm"), 5 + g // 2))
            swiglu(1, U_F1, "f1", ev["n3"])

            turn_rows("y1", orow, lambda g: pe.wait_ge(S("norm"), 9 + g // 2))
            banks = (lambda r: PG[:, r, :], lambda r: PA[:, r, :], lambda r: PA[:, 2 + r, :])
            for c in range(6):
                if c >= 3:
                    pe.wait_ge(S("qkv"), c - 2)
                up(U_M + 2 * c, banks[c % 3], 0, ev["y1"] if c == 0 else None)
            pe.wait_ge(S("qkv"), 2)
            turn_rows("q2", q2)
            pe.wait_ge(S("qkv"), 6)
            turn_rows("k2", k2)
            parts_ready(ev["k2"] + 3)
            attention("2", lambda hd: k2T[:, hd // 2, :],
                      lambda hd, r: v2[:, r, HD * hd:HD * hd + HD])
            turn_rows("ao2", orow, lambda g: pe.wait_ge(S("orow2"), 2 * g + 2))
            out_proj(U_MO, "ao2")
            turn_rows("y2", orow, lambda g: pe.wait_ge(S("norm"), 11 + g // 2))

            T0 = ev["f2"]

            def conv_turn(i):
                pe.wait_ge(S("urow"), i + 1)
                for s in range(2):
                    pe.wait_ge(S("t_free"), i * 2 + (T0 + s - 1))
                    for f in range(2):
                        for r in range(RT):
                            last = nc.tensor.transpose(TB[:, (T0 + s) % 2, (2 * f + r) * P:(2 * f + r + 1) * P],
                                                       urow[:, r, s * FC + f * P:s * FC + (f + 1) * P], ident[:, :])
                    last.then_inc(S("t_full"), 1)

            ffn(U_F2, "f2", ev["y2"], conv_turn, lambda i: pe.wait_ge(S("c_lo"), i + 1), lambda i: None)


INPUTS = ("x", "positions", "att_w_in", "att_g_cq", "att_w_uq", "att_w_iq", "att_g_ik", "att_b_ik", "att_w_o",
          "hgrn_lb_logits", "hgrn_w_in", "hgrn_g_norm", "hgrn_w_o", "ffn_w_gate", "ffn_w_up", "ffn_w_down",
          "ln_g", "ln_b", "attn_norm_2", "w_qkv_2", "w_o_2", "rel_bias_2", "ffn_norm_2", "w_up_2", "conv_w_2",
          "conv_b_2", "w_down_2", "final_norm_2")
ONE = ("x", "positions", "att_w_in", "att_g_cq", "att_w_uq", "att_w_iq", "att_g_ik", "att_b_ik", "att_w_o",
       "hgrn_w_in", "hgrn_g_norm", "hgrn_w_o", "attn_norm_2", "w_qkv_2", "w_o_2", "ffn_norm_2", "w_up_2",
       "conv_w_2", "conv_b_2", "w_down_2")


def kernel(**inputs):
    import concourse.bacc as bacc
    from concourse.bass_utils import run_bass_kernel_spmd as run

    nc = bacc.Bacc("TRN2", target_bir_lowering=False, num_devices=1)
    arrays = {name: np.ascontiguousarray(inputs[name]) for name in INPUTS}
    arrays["inv"], arrays["hot"] = shape_constants()
    feed, w = {}, {}
    for name, a in arrays.items():
        feed[f"in_{name}"] = a
        w[name] = nc.dram_tensor(f"in_{name}", a.shape, mybir.dt.from_np(a.dtype), kind="ExternalInput").ap()
        if name in ONE or name == "inv":
            w[name] = w[name][0]
    for k in range(2):
        w[f"ffn{k}"] = tuple(w[m][k] for m in ("ffn_w_gate", "ffn_w_up", "ffn_w_down"))
    w["ffn2"] = (w["w_up_2"][:, 0:FF2], w["w_up_2"][:, FF2:2 * FF2], w["w_down_2"])
    out = nc.dram_tensor("out_0", (1, T, D), F32, kind="ExternalOutput").ap()
    build(nc, w, out[0])
    r = run(nc, [feed], core_ids=[0])
    return r.results[0]["out_0"]
```

```python
from contextlib import ExitStack

import numpy as np

import concourse.bass as bass
from concourse import mybir

F32 = mybir.dt.float32
F32R = mybir.dt.float32r
I32 = mybir.dt.int32
U8 = mybir.dt.uint8
ALU = mybir.AluOpType
ACT = mybir.ActivationFunctionType
AXX = mybir.AxisListType.X

P = 128
T = 256
RT = T // P
D = 1024
KT = D // P
HALF = D // 2
RING = 3
UNIT = 2048

NQL, HQ, HD = 256, 16, 64
HI, DI = 8, 128
TOPK = 64
ROT, ROTI = 8, 16
IN_COLS = 648
C_K, C_V, C_KI, C_WI = 256, 384, 512, 640
FF = 2816
FC = 256
NFF = FF // FC
ALPHA = 4 ** 0.25
LN_EPS, RMS_EPS = 1e-5, 1e-6
HH, DH = 8, 128
CHUNK = 64
AHEAD = 3
LEVELS = (32, 16, 8, 4, 2, 1)

BUCKETS, MAXD = 32, 128
REL_W = 384
FF2 = 2816

NEG = -1e30
CAUSAL_FILL = -2e38
TAKEN = -3e38

PI2_1 = 6.28125
PI2_2 = float(np.float32(np.floor((2 * np.pi - PI2_1) * 2 ** 20) / 2 ** 20))
PI2_3 = 2 * np.pi - PI2_1 - PI2_2
ROUND = 1.5 * 2 ** 23


def shape_constants():
    inv = [500000.0 ** (-np.arange(0, 2 * n, 2) / (2 * n)) for n in (ROT, ROTI)]
    inv = np.concatenate(inv).astype(np.float32)
    n = np.arange(T)
    exact = BUCKETS // 2
    large = exact + (np.log(np.maximum(n, 1).astype(np.float32) / np.float32(exact))
                     / np.float32(np.log(MAXD / exact)) * np.float32(BUCKETS - exact)).astype(np.int32)
    bucket = np.where(n < exact, n, np.minimum(large, BUCKETS - 1))
    hot = (bucket[::-1][None, :] == np.arange(BUCKETS)[:, None]).astype(np.float32)
    return inv.reshape(1, -1), np.ascontiguousarray(hot)


def weight_units(w):
    def up(m, c, n=512):
        v = m.rearrange("(t p) n -> p t n", p=P)
        return [[(0, 4, n, v[:, 4 * j:4 * j + 4, c:c + n])] for j in range(2)]

    def down(m, tiles):
        v = m.rearrange("(t p) n -> p t n", p=P)
        return [[(0, 2, D, v[:, 2 * j:2 * j + 2, :])] for j in range(tiles // 2)]

    w_in = w["att_w_in"]
    a = up(w_in, 0)
    a.append([(0, 8, IN_COLS - 512, w_in.rearrange("(t p) n -> p t n", p=P)[:, :, 512:IN_COLS])])
    a += down(w["att_w_iq"], 2) + down(w["att_w_uq"], 2) + down(w["att_w_o"], 8)
    h = []
    for c in (2, 3, 0, 1, 4, 5, 6, 7):
        h += up(w["hgrn_w_in"], 512 * c)
    h += down(w["hgrn_w_o"], 8)
    m = []
    for c in range(6):
        m += up(w["w_qkv_2"], 512 * c)
    m += down(w["w_o_2"], 8)
    return a, h, m


N_A, N_H, N_M, N_F = 9, 20, 16, 3 * NFF
U_IN, U_IQ, U_UQ, U_AO = 0, 3, 4, 5
U_F0 = N_A
U_H = U_F0 + N_F
U_HO = U_H + 16
U_F1 = U_H + N_H
U_M = U_F1 + N_F
U_MO = U_M + 12
U_F2 = U_M + N_M
U_ALL = U_F2 + N_F


class Chain:

    def __init__(self, eng, sem):
        self.eng, self.sem, self.n = eng, sem, 0

    def __call__(self, ins):
        self.n += 1
        ins.then_inc(self.sem, 1)
        self.eng.wait_ge(self.sem, self.n)


def build(nc, w, out):
    ctx = ExitStack()
    with ctx:
        def sb(name, shape, dt=F32):
            return ctx.enter_context(nc.sbuf_tensor(name, shape, dt))

        sems = {}

        def S(name):
            if name not in sems:
                sems[name] = ctx.enter_context(nc.semaphore(name))
            return sems[name]

        raw = sb("raw", [P, RING, UNIT])
        whi = sb("whi", [P, RING, UNIT], F32R)
        wlo = sb("wlo", [P, RING, UNIT], F32R)
        h = sb("h", [P, RT, D])
        xhi = sb("xhi", [P, KT, T], F32R)
        xlo = sb("xlo", [P, KT, T], F32R)
        fhi = sb("fhi", [P, 2, T], F32R)
        flo = sb("flo", [P, 2, T], F32R)
        gvec = sb("gvec", [P, D])
        bvec = sb("bvec", [P, D])
        ident = sb("ident", [P, P])
        stats = sb("stats", [P, RT, 2, 6])
        mv = sb("mv", [P, 4, 2])
        ve = sb("ve", [P, 16])
        rstd = sb("rstd", [P, 16])
        mhalf = sb("mhalf", [P, 16])
        work = sb("work", [P, 24500])
        maskt = sb("maskt", [P, 8, P], U8)
        cw = sb("cw", [P, 4, 2 * FF2 // P])
        cwi = sb("cwi", [P, 4, 2, 2])

        def flat(ap):
            return ap.rearrange("p a b -> p (a b)")

        place = [0]

        def carve(*dims):
            n = int(np.prod(dims))
            a = work[:, place[0]:place[0] + n]
            place[0] += n
            assert place[0] <= 24500, place[0]
            if len(dims) == 1:
                return a
            names = "abcd"[:len(dims)]
            return a.rearrange(f"p ({' '.join(names)}) -> p {' '.join(names)}",
                               **{k: v for k, v in zip(names[1:], dims[1:])})

        PG = ctx.enter_context(nc.psum_tensor("PG", [P, 2, 512], F32))
        PA = ctx.enter_context(nc.psum_tensor("PA", [P, 4, 512], F32))
        TB = ctx.enter_context(nc.psum_tensor("TB", [P, 2, 512], F32))

        qT = carve(KT, T)
        pr = carve(3, 384)
        pT = carve(3, 384)
        orow = carve(RT, D)
        amin = carve(HQ, 2)
        asum = carve(HQ, 2)
        arec = carve(HQ, 2)
        att_end = place[0]
        pin = carve(RT, IN_COLS)
        qi = carve(RT, D)
        qr = carve(RT, D)
        qiT = carve(HI, T)
        cqn = carve(RT, NQL)
        kd = carve(RT, 2, 2, HD)
        kT = carve(2, T)
        kiT = carve(T)
        sq = carve(RT, NQL)
        relu = carve(2, 384)
        score = carve(384)
        left = carve(384)
        mask = carve(384)
        m8 = carve(2, 8)
        wsc = carve(RT, HI)
        gcq = carve(NQL)
        gki = carve(DI)
        bki = carve(DI)
        posi = carve(RT)
        posf = carve(RT)
        inv = carve(24)
        ang = carve(RT, 2, 24)
        turns = carve(RT, 2, 24)
        trig = carve(RT, 2, 24)
        rt1 = carve(RT, 128)
        rt2 = carve(RT, 128)
        rt3 = carve(RT, 128)
        rt4 = carve(RT, 128)
        hot = carve(T)
        relrow = carve(BUCKETS)
        relT = carve(HQ)
        relv = carve(REL_W)
        cw4 = carve(4, P)
        place[0] = 0
        lb = carve(D)
        lb1 = carve(D)
        kr = carve(RT, D)
        lf = carve(RT, D)
        qh = carve(RT, D)
        vi = carve(RT, D)
        sg = carve(RT, D)
        bT = carve(HH, T)
        kTh = carve(HH, T)
        qTh = carve(HH, T)
        dl2 = carve(HH, T)
        dls = [z.rearrange("p (a b) -> p a b", a=HH) for z in (flat(lf), flat(dl2), work[:, 0:2 * D], flat(kr))]
        TURN = {0: 0, 1: 1, 2: 2, 3: 3, 4: 4, "cross": 5, 5: 6, 6: 7}
        level_buf = lambda l: dls[TURN[l] % 4]
        aT = carve(3, HH, P)
        ucum = carve(P)
        oh = qh
        sqh = dl2.rearrange("p a b -> p (a b)").rearrange("p (a b) -> p a b", a=RT)
        ssq = carve(16)
        gno = carve(DH)
        place[0] = 0
        fe = carve(RT, FC)
        fh = carve(RT, FC)
        urow = carve(RT, 2 * FC)
        cv = carve(4, T)
        ce = carve(2, T)
        cgv = carve(2, T)
        fhT = carve(2, T)
        place[0] = att_end
        q2 = carve(RT, D)
        k2 = carve(RT, D)
        v2 = carve(RT, D)
        k2T = carve(KT, T)
        relb = carve(HQ, T)
        gatt = carve(D)
        squares = carve(2, HALF)

        rel_dram = nc.dram_tensor("rel_scratch", [HQ, P, REL_W], F32, kind="Internal").ap()

        a_units, h_units, m_units = weight_units(w)
        units = {}
        for base, lst in ((U_IN, a_units), (U_H, h_units), (U_M, m_units)):
            for j, x in enumerate(lst):
                units[base + j] = x

        ev = {}
        n = 0
        for name, k in (("x", 4), ("c0", 2), ("cq", 1), ("ki", 2), ("qi", 4), ("q", 4), ("pt", HQ), ("ao", 4),
                        ("n1", 4), ("f0", 2 * NFF), ("n2", 4), ("hk", 4), ("hq", 4), ("ho", 4), ("n3", 4),
                        ("f1", 2 * NFF), ("y1", 4), ("q2", 4), ("k2", 4), ("pt2", HQ), ("ao2", 4),
                        ("y2", 4), ("f2", 2 * NFF)):
            ev[name] = n
            n += k

        def bc(row, n_):
            return bass.AP(row.tensor, row.offset, [[0, n_]] + [list(x) for x in row.ap])

        block = ctx.enter_context(nc.Block())

        VE = [(0, 2), (2, 2)] + [(0, 1), (1, 1)] * 2 + [(4 * b, 4) for b in range(4)] + [(0, 1), (1, 1)] \
            + [(0, 1), (0, 1), (1, 1), (1, 1)] + [(0, 1), (1, 1)] * 2
        C_CQ, C_KEY, C_LN, C_HEADS, C_YLN, C_YRMS, C_FFN, C_FINAL = \
            0, 1, ((2, 3), (4, 5), (10, 11)), 6, (12, 14), (13, 15), (16, 17), (18, 19)
        GB = [("ln_g", 0, 0), ("ln_g", 0, 1), ("ln_g", 1, 0), ("ln_g", 1, 1),
              ("ffn_norm_2", 0, None), ("final_norm_2", None, None)]
        GB_COUNT = np.cumsum([32, 32, 32, 32, 16, 16]).tolist()

        def rope(eng, link, x, heads, half, c0):
            n_ = heads * half
            cos = trig[:, :, 0, c0:c0 + half].unsqueeze(2).broadcast_to([P, RT, heads, half])
            sin = trig[:, :, 1, c0:c0 + half].unsqueeze(2).broadcast_to([P, RT, heads, half])
            x1, x2 = x[:, :, :, 0:half], x[:, :, :, half:2 * half]
            r = [t[:, :, 0:n_].rearrange("p r (g c) -> p r g c", g=heads) for t in (rt1, rt2, rt3, rt4)]
            eng.tensor_tensor(r[0], x1, cos, ALU.mult)
            eng.tensor_tensor(r[1], x2, sin, ALU.mult)
            eng.tensor_tensor(r[2], x2, cos, ALU.mult)
            link(eng.tensor_tensor(r[3], x1, sin, ALU.mult))
            eng.tensor_tensor(x1, r[0], r[1], ALU.subtract)
            return eng.tensor_tensor(x2, r[2], r[3], ALU.add)

        def out_gates(eng, link, r):
            g = sg[:, r, :]
            link(eng.tensor_tensor(g, g, flat(bT)[:, r * D:(r + 1) * D], ALU.mult))
            gv = g.rearrange("p (g c) -> p g c", c=DH)
            return eng.tensor_tensor(gv, gv, gno.unsqueeze(1).broadcast_to([P, HH, DH]), ALU.mult)

        @block.sync
        def _(sp):
            def slot_free(u):
                if u >= RING:
                    sp.wait_ge(S("w_lo"), u - RING + 1)

            def load(u):
                slot_free(u)
                for o, t, c, view in units[u]:
                    dst = raw[:, u % RING, o:o + t * c].rearrange("p (t c) -> p t c", t=t)
                    sp.dma_start(dst, view).then_inc(S(f"w_loaded{u % RING}"), 16)

            def load_up(slot, i, j, gate, val):
                dst = raw[:, slot, :].rearrange("p (t s c) -> p t s c", t=4, s=2)
                for s, m in enumerate((gate, val)):
                    v = m.rearrange("(t p) n -> p t n", p=P)[:, 4 * j:4 * j + 4, bass.ds(i * FC, FC)]
                    sp.dma_start(dst[:, :, s, :], v).then_inc(S(f"w_loaded{slot}"), 16)

            def load_down(slot, i, down):
                dst = raw[:, slot, :].rearrange("p (t c) -> p t c", t=2)
                v = down.rearrange("(g t p) n -> p g t n", p=P, t=2)[:, bass.ds(i, 1), :, :]
                sp.dma_start(dst, v.rearrange("p g t n -> p (g t) n")).then_inc(S(f"w_loaded{slot}"), 16)

            def ffn(U, gate, val, down):
                for j in range(2):
                    slot_free(U + j)
                    load_up((U + j) % RING, 0, j, gate, val)
                with sp.Fori(1, NFF) as i:
                    for j in range(2):
                        sp.wait_ge(S("w_lo"), i * 3 + (U - 3 + j))
                        load_up((U + 2 + j) % RING, i, j, gate, val)
                    sp.wait_ge(S("w_lo"), i * 3 + (U - 1))
                    load_down((U + 4) % RING, i - 1, down)
                slot_free(U + N_F - 1)
                load_down((U + N_F - 1) % RING, NFF - 1, down)

            hv = w["x"].rearrange("(r p) n -> p r n", p=P)
            sp.dma_start(h[:, 0, :], hv[:, 0, :]).then_inc(S("x_loaded0"), 16)
            _, tiles, cols, view = units[0][0]
            for g, landed_ in enumerate(("first_loaded", "w_loaded0")):
                dst = raw[:, 0, g * UNIT // 2:(g + 1) * UNIT // 2].rearrange("p (t c) -> p t c", c=cols)
                sp.dma_start(dst, view[:, 2 * g:2 * g + 2, :]).then_inc(S(landed_), 16)
            sp.dma_start(h[:, 1, :], hv[:, 1, :]).then_inc(S("x_loaded1"), 16)
            for u in range(1, N_A):
                load(u)
            ffn(U_F0, *w["ffn0"])
            for u in range(U_H, U_H + N_H):
                load(u)
            ffn(U_F1, *w["ffn1"])
            for u in range(U_M, U_M + N_M):
                load(u)
            ffn(U_F2, *w["ffn2"])
            ov = out.rearrange("(r p) n -> p r n", p=P)
            for r in range(RT):
                sp.wait_ge(S("norm"), 4 * 5 + 2 * (r + 1))
                sp.dma_start(ov[:, r, :], h[:, r, :]).then_inc(S("stored"), 16)
            sp.wait_ge(S("stored"), 16 * RT)

        @block.gpsimd
        def _(pool):
            link = Chain(pool, S("pool_chain"))
            for r in range(RT):
                pool.dma_start(posi[:, r:r + 1].bitcast(I32),
                               w["positions"][r * P:(r + 1) * P].rearrange("(p o) -> p o", o=1)).then_inc(S("pos"), 16)
            pool.dma_start(inv, bc(w["inv"], P)).then_inc(S("pos"), 16)
            link(pool.memset(ident[:, :], 0.0))
            pool.affine_select(out=ident[:, :], in_=ident[:, :], compare_op=ALU.not_equal, fill=1.0, base=0,
                               pattern=[[-1, P]], channel_multiplier=1).then_inc(S("ident"), 1)
            for dst, src in ((gcq, w["att_g_cq"]), (gki, w["att_g_ik"]), (bki, w["att_b_ik"])):
                pool.dma_start(dst, bc(src, P)).then_inc(S("small"), 16)
            pool.dma_start(hot[0:BUCKETS, :], w["hot"]).then_inc(S("cst_loaded"), 16)
            pool.dma_start(relrow[0:HQ, :], w["rel_bias_2"]).then_inc(S("cst_loaded"), 16)
            pool.dma_start(cw4[0:44, 0:3, :], w["conv_w_2"].rearrange("j (c p) -> c j p", p=P))\
                .then_inc(S("cst_loaded"), 16)
            pool.dma_start(cw4[0:44, 3, :], w["conv_b_2"].rearrange("(c p) -> c p", p=P))\
                .then_inc(S("cst_loaded"), 16)
            link(pool.memset(mhalf[:, :], -0.5))

            def load_gb(k):
                name, a, b = GB[k]
                if k:
                    pool.wait_ge(S("norm"), 4 * k)
                if name == "ln_g":
                    pool.dma_start(gvec[:, :], bc(w["ln_g"][a, b], P)).then_inc(S("gb"), 16)
                    pool.dma_start(bvec[:, :], bc(w["ln_b"][a, b], P)).then_inc(S("gb"), 16)
                else:
                    pool.dma_start(gvec[:, :], bc(w[name], P)).then_inc(S("gb"), 16)

            def power(k):
                pool.wait_ge(S("ve"), k + 1)
                a, m = VE[k]
                pool.tensor_tensor(rstd[:, a:a + m], ve[:, a:a + m], mhalf[:, a:a + m], ALU.pow)\
                    .then_inc(S("rstd"), 1)

            load_gb(0)
            power(C_CQ)
            power(C_KEY)
            pool.wait_ge(S("relv"), 2)
            pool.dma_start(rel_dram, relv[0:HQ, :].unsqueeze(1).broadcast_to([HQ, P, REL_W]))\
                .then_inc(S("rel_out"), 16)
            pool.wait_ge(S("iacc"), 2 * HI)
            for c in (0, 256):
                last = pool.affine_select(out=score[:, c:c + P], in_=score[:, c:c + P], compare_op=ALU.is_ge,
                                          fill=CAUSAL_FILL, base=0, pattern=[[-1, P]], channel_multiplier=1)
            last.then_inc(S("score_causal"), 1)
            pool.wait_ge(S("trig"), 1)
            for f in range(2):
                pool.wait_ge(S("q_a"), f + 1)
                q_half = qr[:, :, f * HALF:(f + 1) * HALF].rearrange("p r (g c) -> p r g c", g=HQ // 2)
                rope(pool, link, q_half, HQ // 2, ROT, 0).then_inc(S("q_r"), 1)
                pool.wait_ge(S("q_r"), f + 1)
            pool.wait_ge(S("mask"), 1)
            for c in (0, 256):
                last = pool.affine_select(out=mask[:, c:c + P], in_=mask[:, c:c + P], compare_op=ALU.is_ge,
                                          fill=-NEG, base=0, pattern=[[-1, P]], channel_multiplier=1)
            last.then_inc(S("mask_causal"), 1)
            for r in range(RT):
                power(C_LN[0][r])
            load_gb(1)
            for r in range(RT):
                power(C_LN[1][r])
            pool.dma_start(lb, bc(w["hgrn_lb_logits"][0], P)).then_inc(S("lb_loaded"), 16)
            pool.dma_start(lb1, bc(w["hgrn_lb_logits"][1], P)).then_inc(S("lb_loaded"), 16)
            pool.dma_start(gno, bc(w["hgrn_g_norm"], P)).then_inc(S("lb_loaded"), 16)
            load_gb(2)
            pool.wait_ge(S("lb_loaded"), 48)
            pool.tensor_tensor(lb1, lb, lb1, ALU.subtract).then_inc(S("lb_diff"), 1)
            hf = dl2.rearrange("p a b -> p (a b)")[:, 0:P]
            for n_, m in enumerate((CHUNK,) + LEVELS):
                nb = P // (2 * m)
                link(pool.memset(hf, 0.0))
                link(pool.memset(hf.rearrange("p (b s m) -> p b s m", s=2, m=m)[:, :, 1, :], 1.0))
                v3 = hf.rearrange("p (b q) -> p b q", q=2 * m)
                link(pool.affine_select(out=v3, in_=v3, compare_op=ALU.is_ge, fill=0.0, base=0,
                                        pattern=[[-2 * m, nb], [0, 2 * m]], channel_multiplier=1))
                link(pool.affine_select(out=v3, in_=v3, compare_op=ALU.is_ge, fill=0.0, base=m - 1,
                                        pattern=[[2 * m, nb], [0, 2 * m]], channel_multiplier=-1))
                link(pool.tensor_copy(maskt[:, n_, :], hf))
            link(pool.tensor_copy(maskt[:, 7, :], ident[:, :]))
            link(pool.memset(ucum, 1.0))
            link(pool.affine_select(out=ucum, in_=ucum, compare_op=ALU.is_ge, fill=0.0, base=0,
                                    pattern=[[1, P]], channel_multiplier=-1))
            u3 = ucum[:, CHUNK:P]
            link(pool.affine_select(out=u3, in_=u3, compare_op=ALU.is_ge, fill=0.0, base=-CHUNK,
                                    pattern=[[0, CHUNK]], channel_multiplier=1))
            pool.memset(aT[:, 0:2, :, :], 0.0).then_inc(S("hconst"), 1)

            pool.wait_ge(S("t_free"), ev["hq"])
            pool.wait_ge(S("bT"), 4)

            def exponents(l):
                m = ((CHUNK,) + LEVELS)[l]
                d = level_buf(l)
                dv = d.rearrange("p h t -> p (h t)").rearrange("p (b s m) -> p b s m", s=2, m=m)
                bv = bT.rearrange("p h t -> p (h t)").rearrange("p (b s m) -> p b s m", s=2, m=m)
                nb = bv.shape[1]
                mid = bv[:, :, 0, m - 1:m].broadcast_to([P, nb, m])
                pool.tensor_tensor(dv[:, :, 0, :], mid, bv[:, :, 0, :], ALU.subtract).then_inc(S("lv_d"), 1)
                if l == 0:
                    pool.tensor_copy(dv[:, :, 1, :], bv[:, :, 1, :]).then_inc(S("lv_d"), 1)
                else:
                    pool.tensor_tensor(dv[:, :, 1, :], bv[:, :, 1, :], mid, ALU.subtract).then_inc(S("lv_d"), 1)

            for l in range(4):
                exponents(l)
            pool.wait_ge(S("lv_full"), 4)
            exponents(4)
            pool.wait_ge(S("lv_full"), 4 * 2)
            dc = level_buf("cross").rearrange("p h (c t) -> p h c t", c=4)
            bvc = bT.rearrange("p h (c t) -> p h c t", c=4)
            end = lambda c: bvc[:, :, c, CHUNK - 1:CHUNK].broadcast_to([P, HH, CHUNK])
            link(pool.tensor_tensor(dc[:, :, 0, :], end(0), bvc[:, :, 0, :], ALU.subtract))
            pool.tensor_tensor(dc[:, :, 0, :], dc[:, :, 0, :], end(1), ALU.add).then_inc(S("lv_d"), 1)
            pool.tensor_tensor(dc[:, :, 1, :], end(1), bvc[:, :, 1, :], ALU.subtract).then_inc(S("lv_d"), 1)
            pool.tensor_copy(dc[:, :, 2, :], bvc[:, :, 2, :]).then_inc(S("lv_d"), 1)
            pool.tensor_tensor(dc[:, :, 3, :], bvc[:, :, 3, :], end(2), ALU.add).then_inc(S("lv_d"), 1)
            pool.wait_ge(S("lv_full"), 4 * 3)
            exponents(5)
            pool.wait_ge(S("lv_full"), 4 * 4)
            exponents(6)
            pool.wait_ge(S("g_sig"), 1)
            out_gates(pool, link, 0).then_inc(S("sg"), 1)
            for b in range(4):
                power(C_HEADS + b)
            for r in range(RT):
                power(C_LN[2][r])
            load_gb(3)
            pool.dma_start(gatt, bc(w["attn_norm_2"], P)).then_inc(S("gatt"), 16)
            for r in range(RT):
                power(C_YLN[r])
                power(C_YRMS[r])
            pool.wait_ge(S("rel_out"), 16)
            src = bass.AP(rel_dram.tensor, P - 1, [[REL_W - 1, P], [P * REL_W, HQ], [1, T]])
            pool.dma_start(relb, src).then_inc(S("relb"), 16)
            load_gb(4)
            for r in range(RT):
                power(C_FFN[r])
            load_gb(5)

            def gate_value(i):
                pool.wait_ge(S("t_free"), i * 2 + (ev["f2"] + 2))
                pool.tensor_tensor(cgv, cv[:, 0:2, :], cv[:, 2:4, :], ALU.mult).then_inc(S("cgv"), 1)

            gate_value(0)
            with pool.Fori(1, NFF) as i:
                gate_value(i)
            for r in range(RT):
                power(C_FINAL[r])

        total = [0] * RING
        landed = []
        for u in range(U_ALL + RING):
            two = any(U <= u < U + N_F and (u - U < 2 or ((u - U) % 3 != 1 and u != U + N_F - 1))
                      for U in (U_F0, U_F1, U_F2))
            total[u % RING] += 32 if two else 16
            landed.append(total[u % RING])

        def unit_len(u):
            return 8 * (IN_COLS - 512) if u == 2 else UNIT

        def hi(u, i=0):
            if u >= U_ALL:
                return
            s = u % RING
            step = landed[u + RING] - landed[u]
            nc.scalar.wait_ge(S(f"w_loaded{s}"), i * step + landed[u])
            if u >= RING:
                nc.scalar.wait_ge(S("w_used"), i * 3 + (u - RING + 1))
            n_ = unit_len(u)
            nc.scalar.activation(whi[:, s, 0:n_], raw[:, s, 0:n_], ACT.Copy).then_inc(S("w_hi"), 1)

        def lo(u, i=0):
            if u >= U_ALL:
                return
            s = u % RING
            n_ = unit_len(u)
            nc.vector.wait_ge(S("w_hi"), i * 3 + (u + 1))
            nc.vector.tensor_tensor(wlo[:, s, 0:n_], raw[:, s, 0:n_], whi[:, s, 0:n_].bitcast(F32),
                                    ALU.subtract).then_inc(S("w_lo"), 1)

        def quarter(q):
            return slice(q * UNIT // 4, (q + 1) * UNIT // 4)

        def hi_quarter(u, q):
            s = u % RING
            if q == 0:
                nc.scalar.wait_ge(S(f"w_loaded{s}"), landed[u])
                nc.scalar.wait_ge(S("w_used"), u - RING + 1)
            ins = nc.scalar.activation(whi[:, s, quarter(q)], raw[:, s, quarter(q)], ACT.Copy)
            if q == 3:
                ins.then_inc(S("w_hi"), 1)

        def lo_quarter(u, q):
            s = u % RING
            nc.vector.wait_ge(S("w_hi"), u + 1)
            ins = nc.vector.tensor_tensor(wlo[:, s, quarter(q)], raw[:, s, quarter(q)],
                                          whi[:, s, quarter(q)].bitcast(F32), ALU.subtract)
            if q == 3:
                ins.then_inc(S("w_lo"), 1)

        @block.scalar
        def _(act):
            ac = nc.scalar
            link = Chain(act, S("act_chain"))

            def turned(e):
                act.wait_ge(S("t_full"), e + 1)

            def full(u):
                act.wait_ge(S("w_used"), u + 1)

            def x_hi(name, k=4):
                for g in range(k):
                    e = ev[name] + g
                    turned(e)
                    ac.activation(flat(xhi[:, 2 * g:2 * g + 2, :]), TB[:, e % 2, :], ACT.Copy)\
                      .then_inc(S("x_hi"), 1)

            def x_hi_rows(name, r):
                for g in range(2):
                    e = ev[name] + 2 * r + g
                    turned(e)
                    ac.activation(xhi[:, 4 * g:4 * g + 4, r * P:(r + 1) * P],
                                  TB[:, e % 2, :].rearrange("p (k c) -> p k c", k=4), ACT.Copy)\
                      .then_inc(S("x_hi"), 1)

            squared = [0]

            def row_squares(r, ready):
                for f in range(2):
                    ready(r, f)
                    if squared[0] >= 2:
                        act.wait_ge(S("h_sq"), squared[0] - 1)
                    squared[0] += 1
                    ac.activation(squares[:, f, :], h[:, r, f * HALF:(f + 1) * HALF], ACT.Square,
                                  accum_out=ve[:, 8 + 2 * r + f:9 + 2 * r + f]).then_inc(S("h_sq"), 1)

            def copy_turned(name, dst):
                for g in range(4):
                    e = ev[name] + g
                    turned(e)
                    ac.activation(flat(dst[:, 2 * g:2 * g + 2, :]), TB[:, e % 2, :], ACT.Copy)\
                      .then_inc(S("t_free"), 1)

            def attention(tag, between={}):
                for hd in range(HQ):
                    if hd in between:
                        hi_quarter(*between[hd])
                    act.wait_ge(S("amin" + tag), 2 * hd + 2)
                    for r, (a, b) in enumerate(((0, 128), (128, 384))):
                        ac.activation(pr[:, hd % 3, a:b], pr[:, hd % 3, a:b], ACT.Exp, scale=-1.0,
                                      bias=amin[:, hd, r:r + 1], accum_out=asum[:, hd, r:r + 1])\
                          .then_inc(S("prob" + tag), 1)

            def ffn(k, U, name):
                T0 = ev[name]

                def f_hi(i):
                    for f in range(2):
                        act.wait_ge(S("t_full"), i * 2 + (T0 + f + 1))
                        dst = xhi if isinstance(i, int) and i == NFF - 1 else fhi
                        ac.activation(dst[:, f, :], TB[:, (T0 + f) % 2, 0:T], ACT.Copy).then_inc(S("x_hi"), 1)

                def gates(i, u):
                    act.wait_ge(S("w_used"), i * 3 + (u + 1))
                    if not (k == 0 and isinstance(i, int) and i == 0):
                        act.wait_ge(S("hidden"), i + k * NFF)
                    sums = PA if isinstance(i, int) and i == 0 else PG
                    ac.activation(fe, sums[:, 0:2, 0:FC], ACT.Sigmoid).then_inc(S("gate"), 1)

                def step(i):
                    at = (lambda u: hi(u, i)) if not isinstance(i, int) else (lambda u: hi(u + 3 * i))
                    f_hi(i - 1)
                    at(U + 2)
                    gates(i, U)
                    at(U + 3)
                    if not isinstance(i, int):
                        at(U + 4)

                hi(U + 3)
                full(U + 1)
                gates(0, U)
                hi(U + 4)
                with act.Fori(1, NFF - 1) as i:
                    step(i)
                step(NFF - 1)
                f_hi(NFF - 1)
                hi(U + 3 * NFF + 1)

            x_hi_rows("x", 0)
            first = slice(0, UNIT // 2)
            act.wait_ge(S("first_loaded"), 16)
            ac.activation(whi[:, 0, first], raw[:, 0, first], ACT.Copy).then_inc(S("first_hi"), 1)
            act.wait_ge(S("w_loaded0"), landed[0])
            second = slice(UNIT // 2, UNIT)
            ac.activation(whi[:, 0, second], raw[:, 0, second], ACT.Copy).then_inc(S("w_hi"), 1)
            hi(1)
            x_hi_rows("x", 1)
            hi(2)
            act.wait_ge(S("ang"), 1)
            ac.activation(trig.rearrange("p a b c -> p (a b c)"), ang.rearrange("p a b c -> p (a b c)"),
                          ACT.Sin).then_inc(S("trig"), 1)
            full(1)
            ac.activation(pin[:, :, 0:512], PG[:, :, :], ACT.Copy).then_inc(S("pin"), 1)
            act.wait_ge(S("pin"), 1)
            for r in range(RT):
                ac.activation(sq[:, r, :], pin[:, r, 0:NQL], ACT.Square,
                              accum_out=ve[:, 8 + r:9 + r]).then_inc(S("ssq"), 1)
            hi(3)
            hi(4)
            turned(ev["cq"])
            ac.activation(flat(xhi[:, 0:2, :]), TB[:, ev["cq"] % 2, :], ACT.Copy).then_inc(S("x_hi"), 1)
            hi(5)
            full(U_IQ)
            ac.activation(qi[:, 0, :], flat(PA[:, 0:2, :]), ACT.Copy).then_inc(S("qi_a"), 1)
            e = ev["ki"]
            turned(e)
            ac.activation(flat(kT), TB[:, e % 2, :], ACT.Copy).then_inc(S("t_free"), 1)
            turned(e + 1)
            ac.activation(kiT, TB[:, (e + 1) % 2, 0:T], ACT.Copy).then_inc(S("t_free"), 1)
            copy_turned("qi", qiT)
            hi(6)
            for hd in range(HI):
                act.wait_ge(S("iscore"), hd + 1)
                if hd >= 2:
                    act.wait_ge(S("iacc"), 2 * (hd - 1))
                ac.activation(relu[:, hd % 2, :], PA[:, hd % 4, 0:384], ACT.Relu).then_inc(S("relu"), 1)
            for f in range(2):
                if f == 0:
                    act.wait_ge(S("first_q"), 1)
                else:
                    full(U_UQ)
                ac.activation(qr[:, :, f * HALF:(f + 1) * HALF],
                              PA[:, :, :].rearrange("p (f r) c -> p f r c", f=2)[:, f], ACT.Copy,
                              scale=-HD ** -0.5).then_inc(S("q_a"), 1)
            copy_turned("q", qT)
            act.wait_ge(S("ssq"), RT)
            ac.activation(sq[:, 0, 0:1], sq[:, 0, 0:1], ACT.Exp, scale=0.0)
            attention("", {3 + q: (7, q) for q in range(4)})
            x_hi("ao")
            for u in range(8, 11):
                hi(u)
            x_hi_rows("n1", 0)
            hi(U_F0 + 2)
            x_hi_rows("n1", 1)
            ffn(0, U_F0, "f0")
            x_hi_rows("n2", 0)
            hi(U_H + 2)
            x_hi_rows("n2", 1)
            act.wait_ge(S("lb_diff"), 1)
            ac.activation(lb, lb1, ACT.Sigmoid, scale=-1.0).then_inc(S("lb_sig"), 1)

            def gate(dst, j, ps, what):
                ac.activation(dst[:, :, j * HALF:(j + 1) * HALF], ps, ACT.Sigmoid).then_inc(S(what), 1)

            hi(U_H + 3)
            full(U_H + 1)
            gate(kr, 0, PG[:, :, :], "f_sig")
            hi(U_H + 4)
            hi(U_H + 5)
            full(U_H + 3)
            gate(kr, 1, PA[:, 0:2, :], "f_sig")
            hi(U_H + 6)
            hi(U_H + 7)
            full(U_H + 5)
            gate(qh, 0, PA[:, 2:4, :], "q_sig")
            hi(U_H + 8)
            hi(U_H + 9)
            full(U_H + 7)
            gate(qh, 1, PG[:, :, :], "q_sig")
            for j in range(2):
                act.wait_ge(S("fg"), j + 1)
                lv = lf[:, :, j * HALF:(j + 1) * HALF]
                ac.activation(lv, lv, ACT.Ln).then_inc(S("logf"), 1)
            hi(U_H + 10)
            hi(U_H + 11)
            full(U_H + 9)
            ac.activation(vi[:, :, 0:HALF], PA[:, 0:2, :], ACT.Copy).then_inc(S("vi"), 1)
            for b in range(4):
                act.wait_ge(S("cum"), b + 1)
                ac.activation(flat(bT[:, 2 * b:2 * b + 2, :]), PA[:, 2 + b % 2, :], ACT.Copy).then_inc(S("bT"), 1)
            hi(U_H + 12)
            copy_turned("hk", kTh)
            copy_turned("hq", qTh)

            def level_exp(l):
                act.wait_ge(S("lv_d"), {"cross": 14, 5: 16, 6: 18}.get(l) or 2 * l + 2)
                d = flat(level_buf(l))
                ac.activation(d, d, ACT.Exp).then_inc(S("lv_e"), 1)

            level_exp(0)
            hi(U_H + 13)
            full(U_H + 11)
            ac.activation(vi[:, :, HALF:D], PG[:, :, :], ACT.Copy).then_inc(S("vi"), 1)
            level_exp(1)
            hi(U_H + 14)
            level_exp(2)
            hi(U_H + 15)
            full(U_H + 13)
            ac.activation(sg[:, :, 0:HALF], PG[:, :, :], ACT.Copy).then_inc(S("g_raw"), 1)
            hi(U_H + 16)
            level_exp(3)
            level_exp(4)
            hi(U_H + 17)
            level_exp("cross")
            level_exp(5)
            level_exp(6)
            full(U_H + 15)
            ac.activation(sg[:, :, HALF:D], PG[:, :, :], ACT.Copy).then_inc(S("g_raw"), 1)
            hi(U_H + 18)
            act.wait_ge(S("g_raw"), 2)
            ac.activation(flat(bT), flat(sg), ACT.Sigmoid).then_inc(S("g_sig"), 1)
            for b in range(4):
                act.wait_ge(S("ho"), b + 1)
                ac.activation(flat(sqh)[:, b * 512:(b + 1) * 512], PA[:, b, :], ACT.Square)\
                  .then_inc(S("ho_sq"), 1)
            x_hi("ho")
            for u in range(U_HO + 3, U_F1 + 2):
                hi(u)
            x_hi_rows("n3", 0)
            hi(U_F1 + 2)
            x_hi_rows("n3", 1)
            ffn(1, U_F1, "f1")
            hi(U_M + 2)
            normed = lambda r, f: act.wait_ge(S("norm"), 4 * 3 + 2 * r + f + 1)
            row_squares(0, normed)
            x_hi_rows("y1", 0)
            row_squares(1, normed)
            x_hi_rows("y1", 1)

            dsts = (q2, q2, k2, k2, v2, v2)
            banks = (PG[:, :, :], PA[:, 0:2, :], PA[:, 2:4, :])
            for c in range(6):
                hi(U_M + 2 * c + 3)
                full(U_M + 2 * c + 1)
                dst = dsts[c][:, :, (c % 2) * HALF:(c % 2 + 1) * HALF]
                ac.activation(dst, banks[c % 3], ACT.Copy, scale=-HD ** -0.5 if c < 2 else 1.0)\
                  .then_inc(S("qkv"), 1)
                hi(U_M + 2 * c + 4)
            copy_turned("q2", qT)
            copy_turned("k2", k2T)
            attention("2")
            x_hi("ao2")
            for u in range(U_MO + 3, U_F2 + 2):
                hi(u)
            for r in range(RT):
                row_squares(r, lambda r, f: act.wait_ge(S("added"), 2 * r + f + 1))
            x_hi_rows("y2", 0)
            hi(U_F2 + 2)
            x_hi_rows("y2", 1)

            U, T0 = U_F2, ev["f2"]

            def rows_out(i, u):
                act.wait_ge(S("w_used"), i * 3 + (u + 1))
                if not isinstance(i, int) or i > 0:
                    act.wait_ge(S("t_full"), i * 2 + T0)
                sums = PA if isinstance(i, int) and i == 0 else PG
                ac.activation(urow, sums[:, 0:2, :], ACT.Copy).then_inc(S("urow"), 1)

            def conv_first(i):
                act.wait_ge(S("cwi"), i + 1)
                if not isinstance(i, int) or i > 0:
                    act.wait_ge(S("hidden_t"), i)
                for s in range(2):
                    act.wait_ge(S("t_full"), i * 2 + (T0 + s + 1))
                    for f in range(2):
                        ac.activation(cv[:, 2 * s + f, :], TB[:, (T0 + s) % 2, f * T:(f + 1) * T], ACT.Identity,
                                      scale=cwi[:, 2, s, f:f + 1], bias=cwi[:, 3, s, f:f + 1])\
                          .then_inc(S("conv0"), 1)

            def conv_gate(i):
                act.wait_ge(S("t_free"), i * 2 + (T0 + 2))
                ac.activation(ce, cv[:, 0:2, :], ACT.Sigmoid).then_inc(S("cgate"), 1)

            def conv_hi(i):
                act.wait_ge(S("hidden_t"), i + 1)
                dst = xhi if isinstance(i, int) and i == NFF - 1 else fhi
                if dst is fhi and (not isinstance(i, int) or i > 0):
                    act.wait_ge(S("w_used"), i * 3 + (U + 2))
                ac.activation(dst[:, 0:2, :], fhT, ACT.Copy).then_inc(S("c_hi"), 1)

            def cstep(i):
                at = (lambda u: hi(u, i)) if not isinstance(i, int) else (lambda u: hi(u + 3 * i))
                conv_first(i - 1)
                at(U + 1)
                conv_gate(i - 1)
                at(U + 2)
                conv_hi(i - 1)
                rows_out(i, U)
                at(U + 3)

            hi(U + 3)
            rows_out(0, U + 1)
            cstep(1)
            with act.Fori(2, NFF - 1) as i:
                cstep(i)
            cstep(NFF - 1)
            conv_first(NFF - 1)
            conv_gate(NFF - 1)
            conv_hi(NFF - 1)
            for r in range(RT):
                row_squares(r, lambda r, f: act.wait_ge(S("added"), 4 + 2 * r + f + 1))

        @block.vector
        def _(vec):
            ve_ = nc.vector
            link = Chain(vec, S("vec_chain"))

            def turned(e):
                vec.wait_ge(S("t_full"), e + 1)

            def full(u):
                vec.wait_ge(S("w_used"), u + 1)

            nxhi = [0]

            def lo_of_bank(dst, e, src_hi):
                nxhi[0] += 1
                vec.wait_ge(S("x_hi"), nxhi[0])
                ve_.tensor_tensor(dst, TB[:, e % 2, 0:dst.shape[1]], src_hi.bitcast(F32), ALU.subtract)\
                   .then_inc(S("t_free"), 1)

            def x_lo(name, k=4):
                for g in range(k):
                    lo_of_bank(flat(xlo[:, 2 * g:2 * g + 2, :]), ev[name] + g, flat(xhi[:, 2 * g:2 * g + 2, :]))

            def x_lo_rows(name, r):
                for g in range(2):
                    nxhi[0] += 1
                    vec.wait_ge(S("x_hi"), nxhi[0])
                    parts = (z[:, 4 * g:4 * g + 4, r * P:(r + 1) * P] for z in (xlo, xhi))
                    dst, src_hi = parts
                    bank = TB[:, (ev[name] + 2 * r + g) % 2, :].rearrange("p (k c) -> p k c", k=4)
                    ve_.tensor_tensor(dst, bank, src_hi.bitcast(F32), ALU.subtract).then_inc(S("t_free"), 1)

            def attention(tag, bias, between={}):
                o_at = lambda g: PG[:, g % 2, :].rearrange("p (h r c) -> p h r c", h=4, r=2)

                def minima(hd):
                    vec.wait_ge(S("logit" + tag), hd + 1)
                    if hd >= 3:
                        vec.wait_ge(S("t_full"), ev["pt" + tag] + hd - 2)
                    for r, (a, b) in enumerate(((0, 128), (128, 384))):
                        ve_.tensor_tensor_reduce(pr[:, hd % 3, a:b], PA[:, hd % 4, a:b], bias(hd, r), 1.0, 3e38,
                                                 ALU.add, ALU.min, amin[:, hd, r:r + 1])\
                           .then_inc(S("amin" + tag), 1)

                def turn_out(hd):
                    e = ev["pt" + tag] + hd
                    turned(e)
                    if hd >= 3:
                        vec.wait_ge(S("pv" + tag), hd - 2)
                    ve_.tensor_copy(pT[:, hd % 3, :], TB[:, e % 2, 0:384]).then_inc(S("t_free"), 1)

                def outputs(g):
                    vec.wait_ge(S("prob" + tag), 2 * (4 * g + 4))
                    link(ve_.reciprocal(arec[:, 4 * g:4 * g + 4, :], asum[:, 4 * g:4 * g + 4, :]))
                    vec.wait_ge(S("pv" + tag), 4 * g + 4)
                    for r in range(RT):
                        o = orow[:, r, 256 * g:256 * g + 256].rearrange("p (h c) -> p h c", h=4)
                        rb = arec[:, 4 * g:4 * g + 4, r:r + 1].broadcast_to([P, 4, HD])
                        ve_.tensor_tensor(o, o_at(g)[:, :, r, :], rb, ALU.mult).then_inc(S("orow" + tag), 1)

                for i in range(HQ + 3):
                    if i < HQ:
                        minima(i)
                    if 1 <= i <= HQ:
                        turn_out(i - 1)
                    if i in between:
                        lo_quarter(*between[i])
                    if i >= 6 and (i - 6) % 4 == 0 and (i - 6) // 4 < 3:
                        outputs((i - 6) // 4)
                outputs(3)

            def residual(scale, u, r, moment=True):
                if r == 0:
                    res[0] += 1
                    vec.wait_ge(S("first_rows"), res[0])
                else:
                    full(u)
                for f in range(2):
                    hv_ = h[:, r, f * HALF:(f + 1) * HALF]
                    ins = ve_.scalar_tensor_tensor(out=hv_, in0=hv_, scalar=scale, in1=PA[:, 2 * r + f, :],
                                                   op0=ALU.mult, op1=ALU.add)
                    if not moment:
                        ins.then_inc(S("added"), 1)
                        added[0] += 1
                if moment:
                    link(ins)

            res = [0]
            added = [0]
            squared = [0]

            def moments(r):
                for f in range(2):
                    ins = ve_.bn_stats(stats[:, r, f, :], h[:, r, f * HALF:(f + 1) * HALF])
                link(ins)
                link(ve_.bn_aggr(mv[:, r, :], stats[:, r, :, :].rearrange("p a b -> p (a b)")))

            def halves(step, sem=None):
                for f in range(2):
                    ins = step(slice(f * HALF, (f + 1) * HALF))
                    if sem:
                        ins.then_inc(S(sem), 1)
                return ins

            def ln_variance(r):
                ve_.tensor_scalar(ve[:, r:r + 1], mv[:, r, 1:2], LN_EPS, None, ALU.add).then_inc(S("ve"), 1)

            def ln_apply(k, r, call):
                vec.wait_ge(S("gb"), GB_COUNT[k])
                link(halves(lambda c: ve_.scalar_tensor_tensor(
                    out=h[:, r, c], in0=h[:, r, c], scalar=mv[:, r, 0:1], in1=gvec[:, c],
                    op0=ALU.subtract, op1=ALU.mult)))
                vec.wait_ge(S("rstd"), call + 1)
                halves(lambda c: ve_.scalar_tensor_tensor(
                    out=h[:, r, c], in0=h[:, r, c], scalar=rstd[:, r:r + 1], in1=bvec[:, c],
                    op0=ALU.mult, op1=ALU.add), "norm")

            def mean_square(r):
                squared[0] += 2
                vec.wait_ge(S("h_sq"), squared[0])
                s0 = 8 + 2 * r
                link(ve_.tensor_tensor(ve[:, 12 + r:13 + r], ve[:, s0:s0 + 1], ve[:, s0 + 1:s0 + 2], ALU.add))
                ve_.tensor_scalar(ve[:, r:r + 1], ve[:, 12 + r:13 + r], 1.0 / D, RMS_EPS, ALU.mult, ALU.add)\
                   .then_inc(S("ve"), 1)

            def rms_apply(r, call, dst, gain, sem):
                vec.wait_ge(S("rstd"), call + 1)
                halves(lambda c: ve_.scalar_tensor_tensor(
                    out=dst[:, r, c], in0=h[:, r, c], scalar=rstd[:, r:r + 1], in1=gain[:, c],
                    op0=ALU.mult, op1=ALU.mult), sem)

            def add_and_layer_norm(u, k, name):
                residual(ALPHA, u, 0)
                moments(0)
                ln_variance(0)
                ln_apply(k, 0, C_LN[k][0])
                residual(ALPHA, u, 1)
                x_lo_rows(name, 0)
                moments(1)
                ln_variance(1)
                ln_apply(k, 1, C_LN[k][1])
                x_lo_rows(name, 1)

            def add_and_rms_norm(u, k, calls, dst, name=None):
                residual(1.0, u, 0, moment=False)
                mean_square(0)
                residual(1.0, u, 1, moment=False)
                vec.wait_ge(S("gb"), GB_COUNT[k])
                vec.wait_ge(S("added"), added[0])
                rms_apply(0, calls[0], dst, gvec, "norm")
                if name:
                    x_lo_rows(name, 0)
                mean_square(1)
                rms_apply(1, calls[1], dst, gvec, "norm")
                if name:
                    x_lo_rows(name, 1)

            def ffn(k, U, name):
                T0 = ev[name]
                x0 = nxhi[0]

                def f_lo(i):
                    for f in range(2):
                        vec.wait_ge(S("x_hi"), i * 2 + (x0 + f + 1))
                        last = isinstance(i, int) and i == NFF - 1
                        h_, l_ = (xhi, xlo) if last else (fhi, flo)
                        ve_.tensor_tensor(l_[:, f, :], TB[:, (T0 + f) % 2, 0:T], h_[:, f, :].bitcast(F32),
                                          ALU.subtract).then_inc(S("t_free"), 1)

                def hidden(i):
                    vec.wait_ge(S("gate"), i + (k * NFF + 1))
                    sums = PA if isinstance(i, int) and i == 0 else PG
                    ve_.tensor_tensor(fh, sums[:, 0:2, 0:FC], fe, ALU.mult).then_inc(S("vec_chain"), 1)
                    vec.wait_ge(S("vec_chain"), i + (c0 + 1))
                    ve_.tensor_tensor(fh, fh, sums[:, 0:2, FC:2 * FC], ALU.mult).then_inc(S("hidden"), 1)

                def step(i):
                    at = (lambda u: lo(u, i)) if not isinstance(i, int) else (lambda u: lo(u + 3 * i))
                    f_lo(i - 1)
                    at(U + 2)
                    hidden(i)
                    if not isinstance(i, int):
                        at(U + 3)
                        at(U + 4)

                c0 = link.n
                lo(U + 3)
                hidden(0)
                lo(U + 4)
                with vec.Fori(1, NFF - 1) as i:
                    step(i)
                step(NFF - 1)
                f_lo(NFF - 1)
                lo(U + 3 * NFF)
                lo(U + 3 * NFF + 1)
                link.n += NFF
                nxhi[0] += 2 * NFF

            x_lo_rows("x", 0)
            for part, made, done in ((slice(0, UNIT // 2), "first_hi", "first_lo"),
                                     (slice(UNIT // 2, UNIT), "w_hi", "w_lo")):
                vec.wait_ge(S(made), 1)
                ve_.tensor_tensor(wlo[:, 0, part], raw[:, 0, part], whi[:, 0, part].bitcast(F32), ALU.subtract)\
                   .then_inc(S(done), 1)
            lo(1)
            x_lo_rows("x", 1)

            vec.wait_ge(S("pos"), 48)
            link(ve_.tensor_copy(posf, posi.bitcast(I32)))
            for r in range(RT):
                for s in range(2):
                    ins = ve_.tensor_scalar(ang[:, r, s, :], inv, posf[:, r:r + 1], None, ALU.mult)
            link(ins)
            for s in range(2):
                ins = ve_.tensor_scalar(turns[:, :, s, :], ang[:, :, s, :], 1 / (2 * np.pi), 0.25 * (1 - s),
                                        ALU.mult, ALU.add)
            link(ins)
            link(ve_.tensor_scalar(turns, turns, ROUND, ROUND, ALU.add, ALU.subtract))
            for part in (PI2_1, PI2_2, PI2_3):
                a2, t2 = (z.rearrange("p a b c -> p (a b c)") for z in (ang, turns))
                link(ve_.scalar_tensor_tensor(out=a2, in0=t2, scalar=-part, in1=a2, op0=ALU.mult, op1=ALU.add))
            link(ve_.tensor_scalar(ang[:, :, 0, :], ang[:, :, 0, :], np.pi / 2, None, ALU.add))
            lim = float(np.float32(3.1415925))
            ve_.tensor_scalar(ang, ang, lim, -lim, ALU.min, ALU.max).then_inc(S("ang"), 1)

            lo(2)
            vec.wait_ge(S("ssq"), RT)
            ve_.tensor_scalar(ve[:, 0:2], ve[:, 8:10], 1.0 / NQL, RMS_EPS, ALU.mult, ALU.add).then_inc(S("ve"), 1)
            e = ev["c0"]
            turned(e)
            ve_.tensor_copy(relT[0:BUCKETS, :], TB[0:BUCKETS, e % 2, 0:HQ]).then_inc(S("t_free"), 1)
            turned(e + 1)
            ve_.tensor_copy(cw[:, :, :], TB[:, (e + 1) % 2, 0:176].rearrange("p (j c) -> p j c", j=4))\
               .then_inc(S("t_free"), 1)
            vec.wait_ge(S("small"), 48)
            vec.wait_ge(S("rstd"), C_CQ + 1)
            vec.wait_ge(S("pin"), 1)
            for r in range(RT):
                ins = ve_.scalar_tensor_tensor(out=cqn[:, r, :], in0=pin[:, r, 0:NQL], scalar=rstd[:, r:r + 1],
                                               in1=gcq, op0=ALU.mult, op1=ALU.mult)
            ins.then_inc(S("cqn"), 1)
            lo(3)
            full(2)
            link(ve_.tensor_copy(pin[:, :, 512:IN_COLS], PA[:, 0:2, 0:IN_COLS - 512]))
            vec.wait_ge(S("reldist"), 1)
            ve_.tensor_scalar(relv[0:HQ, 0:T], PA[0:HQ, 2, 0:T], -1.0, None, ALU.mult).then_inc(S("relv"), 1)
            lo_of_bank(flat(xlo[:, 0:2, :]), ev["cq"], flat(xhi[:, 0:2, :]))
            for r in range(RT):
                ins = ve_.bn_stats(stats[:, r, 0, :], pin[:, r, C_KI:C_WI])
            link(ins)
            for r in range(RT):
                ins = ve_.bn_aggr(mv[:, 2 + r, :], stats[:, r, 0, :])
            link(ins)
            ve_.tensor_scalar(ve[:, 2:4], mv[:, 2:4, 1], LN_EPS, None, ALU.add).then_inc(S("ve"), 1)
            ve_.memset(relv[0:HQ, T:REL_W], -NEG).then_inc(S("relv"), 1)
            ve_.tensor_scalar(wsc, pin[:, :, C_WI:IN_COLS], HI ** -0.5 * DI ** -0.5, None, ALU.mult)
            vec.wait_ge(S("trig"), 1)
            link(rope(ve_, link, pin[:, :, C_K:C_V].rearrange("p r (g c) -> p r g c", g=2), 2, ROT, 0))
            vec.wait_ge(S("rstd"), C_KEY + 1)
            for r in range(RT):
                kv_ = pin[:, r, C_KI:C_WI]
                ins = ve_.tensor_scalar(kv_, kv_, mv[:, 2 + r, 0:1], rstd[:, 2 + r:3 + r], ALU.subtract, ALU.mult)
            link(ins)
            kv_ = pin[:, :, C_KI:C_WI]
            link(ve_.tensor_tensor(kv_, kv_, gki.unsqueeze(1).broadcast_to([P, RT, DI]), ALU.mult))
            link(ve_.tensor_tensor(kv_, kv_, bki.unsqueeze(1).broadcast_to([P, RT, DI]), ALU.add))
            link(rope(ve_, link, pin[:, :, C_KI:C_WI].rearrange("p r (g c) -> p r g c", g=1), 1, ROTI, ROT))
            for r in range(RT):
                for c in range(2):
                    ins = ve_.tensor_copy(kd[:, r, :, c, :],
                                          pin[:, r, C_K:C_V].rearrange("p (g c) -> p g c", g=2))
            ins.then_inc(S("kd"), 1)
            full(U_IQ)
            ve_.tensor_copy(qi[:, 1, :], flat(PA[:, 2:4, :])).then_inc(S("qi_b"), 1)
            vec.wait_ge(S("qi_b"), 1)
            vec.wait_ge(S("qi_a"), 1)
            rope(ve_, link, qi.rearrange("p r (g c) -> p r g c", g=HI), HI, ROTI, ROT).then_inc(S("qi_r"), 1)
            lo(4)
            for hd in range(HI):
                vec.wait_ge(S("relu"), hd + 1)
                if hd:
                    vec.wait_ge(S("iacc"), 2 * hd)
                for r, (a, b) in enumerate(((0, 128), (128, 384))):
                    src, dst = relu[:, hd % 2, a:b], score[:, a:b]
                    wv = wsc[:, r, hd:hd + 1]
                    if hd == 0:
                        ins = ve_.tensor_scalar(dst, src, wv, None, ALU.mult)
                    else:
                        ins = ve_.scalar_tensor_tensor(out=dst, in0=src, scalar=wv, in1=dst,
                                                       op0=ALU.mult, op1=ALU.add)
                    ins.then_inc(S("iacc"), 1)
            vec.wait_ge(S("score_causal"), 1)
            n_ = 0
            for k in range(TOPK // 8):
                src = score if k == 0 else left
                for find in (True, False):
                    for r, (a, b) in enumerate(((0, 128), (128, 384))):
                        if n_ >= 2:
                            vec.wait_ge(S("topk"), n_ - 1)
                        if find:
                            ins = ve_.max(m8[:, r, :], src[:, a:b])
                        else:
                            ins = ve_.match_replace(left[:, a:b], m8[:, r, :], src[:, a:b], TAKEN)
                        ins.then_inc(S("topk"), 1)
                        n_ += 1
            vec.wait_ge(S("topk"), n_)
            ve_.tensor_scalar(mask, left, (CAUSAL_FILL + TAKEN) / 2, -NEG, ALU.is_gt, ALU.mult)\
               .then_inc(S("mask"), 1)
            vec.wait_ge(S("mask_causal"), 1)
            attention("", lambda hd, r: mask[:, 0:128] if r == 0 else mask[:, 128:384], 
                      {2 + 4 * k + q: (5 + k, q) for k in range(3) for q in range(4)})
            x_lo("ao")
            for u in range(U_AO + 3, U_F0 + 2):
                lo(u)
            add_and_layer_norm(U_AO + 3, 0, "n1")
            lo(U_F0 + 2)
            ffn(0, U_F0, "f0")
            add_and_layer_norm(U_F0 + N_F - 1, 1, "n2")
            lo(U_H + 2)

            vec.wait_ge(S("lb_sig"), 1)
            link(ve_.tensor_scalar(lb1, lb, -1.0, 1.0, ALU.mult, ALU.add))

            def forget(j):
                cols = slice(j * HALF, (j + 1) * HALF)
                v = kr[:, :, cols]
                lbb = lb[:, cols].unsqueeze(1).broadcast_to([P, RT, HALF])
                lb1b = lb1[:, cols].unsqueeze(1).broadcast_to([P, RT, HALF])
                vec.wait_ge(S("f_sig"), j + 1)
                link(ve_.tensor_tensor(v, v, lb1b, ALU.mult))
                link(ve_.tensor_tensor(v, v, lbb, ALU.add))
                ve_.tensor_scalar(lf[:, :, cols], v, 2.0 ** -63, None, ALU.max).then_inc(S("fg"), 1)
                ve_.tensor_scalar(v, v, -1.0, 1.0, ALU.mult, ALU.add).then_inc(S("kr"), 1)

            def silu(j, ps):
                v = qh[:, :, j * HALF:(j + 1) * HALF]
                vec.wait_ge(S("q_sig"), j + 1)
                ve_.tensor_tensor(v, v, ps, ALU.mult).then_inc(S("qh"), 1)

            lo(U_H + 3)
            forget(0)
            lo(U_H + 4)
            lo(U_H + 5)
            forget(1)
            lo(U_H + 6)
            lo(U_H + 7)
            silu(0, PA[:, 2:4, :])
            lo(U_H + 8)
            lo(U_H + 9)
            silu(1, PG[:, :, :])
            lo(U_H + 10)
            lo(U_H + 11)

            def products(l):
                vec.wait_ge(S("lv_e"), TURN[l] + 1)
                m = ((CHUNK,) + LEVELS)[l]
                d, k_, q_ = (flat(z).rearrange("p (b s m) -> p b s m", s=2, m=m)
                             for z in (level_buf(l), kTh, qTh))
                ve_.tensor_tensor(d[:, :, 0, :], d[:, :, 0, :], k_[:, :, 0, :], ALU.mult).then_inc(S("lv_x"), 1)
                ve_.tensor_tensor(d[:, :, 1, :], d[:, :, 1, :], q_[:, :, 1, :], ALU.mult).then_inc(S("lv_x"), 1)

            def take(l):
                n_, n0 = (P, 0) if l == 7 else (P // 2, 4)
                for b in range(4):
                    vec.wait_ge(S("lv_full" if l < 7 else "diag_full"), 4 * l + b + 1 if l < 7 else b + 1)
                    for r in range(RT):
                        dst = aT[:, r, 2 * b:2 * b + 2, :]
                        src = PA[:, b, r * 2 * n_:(r + 1) * 2 * n_].rearrange("p (h c) -> p h c", h=2)
                        mk = maskt[:, l, :]
                        if l < 7:
                            m = ((CHUNK,) + LEVELS)[l]
                            dst = dst.rearrange("p h (b s m) -> p h b s m", s=2, m=m)[:, :, :, 1, :]
                            src = src.rearrange("p h (b m) -> p h b m", m=m)
                            mk = mk.rearrange("p (b s m) -> p b s m", s=2, m=m)[:, :, 1, :]
                        for c in range(2):
                            ins = ve_.copy_predicated(dst[:, c], mk, src[:, c])
                    ins.then_inc(S("lv_taken"), 1)

            lo(U_H + 12)
            vec.wait_ge(S("t_free"), ev["hq"] + 4)
            vec.wait_ge(S("hconst"), 1)
            take(7)
            products(0)
            lo(U_H + 13)
            products(1)
            take(0)
            lo(U_H + 14)
            products(2)
            lo(U_H + 15)
            take(1)
            take(2)
            lo(U_H + 16)
            products(3)
            products(4)
            take(3)
            vec.wait_ge(S("lv_e"), TURN["cross"] + 1)
            dx = level_buf("cross")
            ve_.tensor_tensor(dx[:, :, 0:P], dx[:, :, 0:P], kTh[:, :, 0:P], ALU.mult).then_inc(S("lv_x"), 1)
            ve_.tensor_tensor(dx[:, :, P:T], dx[:, :, P:T], qTh[:, :, P:T], ALU.mult).then_inc(S("lv_x"), 1)
            take(4)
            products(5)
            products(6)
            take(5)
            for b in range(2):
                vec.wait_ge(S("lv_cross"), b + 1)
                ve_.tensor_copy(flat(aT[:, 2, 4 * b:4 * b + 4, :]), PG[:, b, :]).then_inc(S("aT2"), 1)
            take(6)
            vec.wait_ge(S("g_sig"), 1)
            link(out_gates(ve_, link, 1))
            for b in range(4):
                vec.wait_ge(S("ho_sq"), b + 1)
                link(ve_.tensor_reduce(ssq[:, 4 * b:4 * b + 4],
                                       flat(sqh)[:, b * 512:(b + 1) * 512].rearrange("p (g c) -> p g c", g=4),
                                       AXX, ALU.add))
                ve_.tensor_scalar(ve[:, 4 * b:4 * b + 4], ssq[:, 4 * b:4 * b + 4], 1.0 / DH, RMS_EPS,
                                  ALU.mult, ALU.add).then_inc(S("ve"), 1)
            vec.wait_ge(S("sg"), 1)
            for b in range(4):
                vec.wait_ge(S("rstd"), C_HEADS + b + 1)
                for r in range(RT):
                    for c in range(2):
                        hd, g = 2 * b + c, 4 * b + 2 * r + c
                        cols = slice(hd * DH, (hd + 1) * DH)
                        ins = ve_.scalar_tensor_tensor(
                            out=oh[:, r, cols], in0=PA[:, b, (2 * r + c) * P:(2 * r + c + 1) * P],
                            scalar=rstd[:, g:g + 1], in1=sg[:, r, cols], op0=ALU.mult, op1=ALU.mult)
                ins.then_inc(S("oh"), 1)
            x_lo("ho")
            for u in range(U_HO + 1, U_F1 + 2):
                lo(u)
            add_and_layer_norm(U_HO + 3, 2, "n3")
            lo(U_F1 + 2)
            ffn(1, U_F1, "f1")

            def last_layer_norm(r):
                ln_apply(3, r, C_YLN[r])
                vec.wait_ge(S("norm"), 4 * 3 + 2 * (r + 1))

            residual(ALPHA, U_F1 + N_F - 1, 0)
            moments(0)
            ln_variance(0)
            last_layer_norm(0)
            mean_square(0)
            residual(ALPHA, U_F1 + N_F - 1, 1)
            vec.wait_ge(S("gatt"), 16)
            rms_apply(0, C_YRMS[0], orow, gatt, "y1_rows")
            moments(1)
            ln_variance(1)
            x_lo_rows("y1", 0)
            last_layer_norm(1)
            mean_square(1)
            rms_apply(1, C_YRMS[1], orow, gatt, "y1_rows")
            x_lo_rows("y1", 1)
            for u in range(U_M + 2, U_M + 15):
                lo(u)
            vec.wait_ge(S("relb"), 16)
            attention("2", lambda hd, r: relb[:, hd, 128:256] if r == 0 else relb[:, hd, :])
            x_lo("ao2")
            for u in range(U_MO + 3, U_F2 + 2):
                lo(u)
            add_and_rms_norm(U_MO + 3, 4, C_FFN, orow, "y2")
            lo(U_F2 + 2)

            U, T0 = U_F2, ev["f2"]
            c0 = link.n

            def conv(i):
                for f in range(4):
                    b_, o_ = (T0 + f // 2) % 2, (f % 2) * T
                    vec.wait_ge(S("conv0"), i * 4 + (2 * (f // 2) + 2))
                    ins = ve_.scalar_tensor_tensor(out=cv[:, f, 1:T], in0=TB[:, b_, o_:o_ + T - 1],
                                                   scalar=cwi[:, 1, f // 2, f % 2:f % 2 + 1], in1=cv[:, f, 1:T],
                                                   op0=ALU.mult, op1=ALU.add)
                ins.then_inc(S("vec_chain"), 1)
                vec.wait_ge(S("vec_chain"), i + (c0 + 1))
                for f in range(4):
                    b_, o_ = (T0 + f // 2) % 2, (f % 2) * T
                    ins = ve_.scalar_tensor_tensor(out=cv[:, f, 2:T], in0=TB[:, b_, o_:o_ + T - 2],
                                                   scalar=cwi[:, 0, f // 2, f % 2:f % 2 + 1], in1=cv[:, f, 2:T],
                                                   op0=ALU.mult, op1=ALU.add)
                    if f % 2:
                        ins.then_inc(S("t_free"), 1)

            def conv_hidden(i):
                vec.wait_ge(S("cgate"), i + 1)
                vec.wait_ge(S("cgv"), i + 1)
                if not isinstance(i, int) or i > 0:
                    vec.wait_ge(S("c_lo"), i)
                ve_.tensor_tensor(fhT, cgv, ce, ALU.mult).then_inc(S("hidden_t"), 1)

            def conv_lo(i):
                vec.wait_ge(S("c_hi"), i + 1)
                last = isinstance(i, int) and i == NFF - 1
                h_, l_ = (xhi, xlo) if last else (fhi, flo)
                ve_.tensor_tensor(l_[:, 0:2, :], fhT, h_[:, 0:2, :].bitcast(F32), ALU.subtract)\
                   .then_inc(S("c_lo"), 1)

            def weights(i):
                if not isinstance(i, int) or i > 0:
                    vec.wait_ge(S("t_free"), i * 2 + T0)
                cwv = cw[:, :, :].rearrange("p j (s c) -> p j s c", s=2)
                ve_.tensor_copy(cwi[:, :, :, :], cwv[:, :, :, bass.ds(i * 2, 2)]).then_inc(S("cwi"), 1)

            def step(i):
                at = (lambda u: lo(u, i)) if not isinstance(i, int) else (lambda u: lo(u + 3 * i))
                conv(i - 1)
                at(U + 1)
                conv_hidden(i - 1)
                conv_lo(i - 1)
                weights(i)
                at(U + 2)
                at(U + 3)

            weights(0)
            lo(U + 3)
            step(1)
            with vec.Fori(2, NFF - 1) as i:
                step(i)
            step(NFF - 1)
            conv(NFF - 1)
            conv_hidden(NFF - 1)
            conv_lo(NFF - 1)
            link.n += NFF
            add_and_rms_norm(U_F2 + N_F - 1, 5, C_FINAL, h)

        @block.tensor
        def _(pe):
            mm = nc.tensor.matmul

            def t_bank(e):
                if e >= 2:
                    pe.wait_ge(S("t_free"), e - 1)

            def parts_ready(e):
                pe.wait_ge(S("t_free"), e + 1)

            def turn_rows(name, rows, ready=None, events=range(4)):
                for g in events:
                    e = ev[name] + g
                    t_bank(e)
                    if ready:
                        ready(g)
                    for k in range(2):
                        for r in range(RT):
                            last = nc.tensor.transpose(TB[:, e % 2, (2 * k + r) * P:(2 * k + r + 1) * P],
                                                       rows[:, r, (2 * g + k) * P:(2 * g + k + 1) * P], ident[:, :])
                    last.then_inc(S("t_full"), 1)

            def turn_row_tile(name, rows, r, ready):
                for g in range(2):
                    e = ev[name] + 2 * r + g
                    ready(r, g)
                    t_bank(e)
                    for k in range(4):
                        last = nc.tensor.transpose(TB[:, e % 2, k * P:(k + 1) * P],
                                                   rows[:, r, (4 * g + k) * P:(4 * g + k + 1) * P], ident[:, :])
                    last.then_inc(S("t_full"), 1)

            def products(dst, k, r, slot, cols, first, last_, xh=None, xl=None):
                xh, xl = (xhi if xh is None else xh), (xlo if xl is None else xl)
                rows = slice(r * P, (r + 1) * P)
                mm(dst, xl[:, k, rows], whi[:, slot, cols], start=first, stop=False)
                mm(dst, xh[:, k, rows], wlo[:, slot, cols], start=False, stop=False)
                return mm(dst, xh[:, k, rows], whi[:, slot, cols], start=False, stop=last_)

            def turn_and_up(u, bank, name, rows, ready):
                turn_row_tile(name, rows, 0, ready)
                for r in range(RT):
                    for s in range(2):
                        slot = (u + s) % RING
                        if r == 0 and u + s > 0:
                            pe.wait_ge(S("w_lo"), u + s + 1)
                        for t in range(4):
                            k = 4 * s + t
                            if r == 0 and u + s == 0 and t % 2 == 0:
                                pe.wait_ge(S("w_lo" if t else "first_lo"), 1)
                            if r == 0 and k == 6:
                                turn_row_tile(name, rows, 1, ready)
                            if k % 4 == 0:
                                parts_ready(ev[name] + 2 * r + k // 4)
                            last = products(bank(r), k, r, slot, slice(t * 512, (t + 1) * 512), k == 0, k == KT - 1)
                        if r == RT - 1:
                            last.then_inc(S("w_used"), 1)

            def up(u, bank, j=0, between=None, tiles=0):
                for s in range(2):
                    slot = (u + s) % RING
                    pe.wait_ge(S("w_lo"), j * 3 + (u + s + 1))
                    for t in range(4):
                        k = 4 * s + t
                        if between and k == tiles:
                            between()
                        for r in range(RT):
                            last = products(bank(r), k, r, slot, slice(t * 512, (t + 1) * 512), k == 0, k == KT - 1)
                    last.then_inc(S("w_used"), 1)

            def down(u, k0, first, last_, j=0, xh=None, xl=None, ends=True, between=None):
                slot = u % RING
                pe.wait_ge(S("w_lo"), j * 3 + (u + 1))
                def tile(t, r):
                    for f in range(2):
                        ins = products(PA[:, 2 * r + f, :], k0 + t, r, slot,
                                       slice(t * D + f * 512, t * D + (f + 1) * 512),
                                       first and t == 0, last_ and t == 1, xh, xl)
                    return ins

                if between:
                    for r in range(RT):
                        for t in range(2):
                            last = tile(t, r)
                        if r == 0:
                            between()
                    last.then_inc(S("w_used"), 1)
                    return
                if not (last_ and ends):
                    for t in range(2):
                        for r in range(RT):
                            last = tile(t, r)
                    last.then_inc(S("w_used"), 1)
                    return
                for r in range(RT):
                    for t in range(2):
                        last = tile(t, r)
                    last.then_inc(S("w_used" if r else "first_rows"), 1)

            def attention(tag, keys, value, second_half=None):
                e0 = ev["pt" + tag]

                def logits(hd):
                    if hd >= 4:
                        pe.wait_ge(S("amin" + tag), 2 * (hd - 3))
                    rows = slice(HD * (hd % 2), HD * (hd % 2) + HD)
                    for r, (a, n_) in enumerate(((0, 128), (128, 256))):
                        dst = PA[:, hd % 4, a:a + n_]
                        last = mm(dst, qT[rows, hd // 2, r * P:(r + 1) * P], keys(hd)[rows, 0:n_],
                                  start=True, stop=True)
                    last.then_inc(S("logit" + tag), 1)

                def turn(hd):
                    t_bank(e0 + hd)
                    pe.wait_ge(S("prob" + tag), 2 * hd + 2)
                    for c in range(3):
                        last = nc.tensor.transpose(TB[:, (e0 + hd) % 2, c * P:(c + 1) * P],
                                                   pr[:, hd % 3, c * P:(c + 1) * P], ident[:, :])
                    last.then_inc(S("t_full"), 1)

                def pv(hd):
                    parts_ready(e0 + hd)
                    g = hd // 4
                    if hd % 4 == 0 and g >= 2:
                        pe.wait_ge(S("orow" + tag), 2 * (g - 1))
                    c = (hd % 4) * P
                    mm(PG[:, g % 2, c:c + HD], pT[:, hd % 3, 0:P], value(hd, 0), start=True, stop=True)
                    mm(PG[:, g % 2, c + HD:c + P], pT[:, hd % 3, P:2 * P], value(hd, 0), start=True, stop=False)
                    mm(PG[:, g % 2, c + HD:c + P], pT[:, hd % 3, 2 * P:3 * P], value(hd, 1), start=False, stop=True)\
                        .then_inc(S("pv" + tag), 1)

                for hd in range(AHEAD):
                    logits(hd)
                if second_half:
                    second_half()
                for i in range(HQ + 2):
                    if i + AHEAD < HQ:
                        if second_half and i + AHEAD == HQ // 2:
                            parts_ready(ev["q"] + 3)
                        logits(i + AHEAD)
                    if 1 <= i <= HQ:
                        turn(i - 1)
                    if i >= 2:
                        pv(i - 2)

            def out_proj(U, name):
                for j in range(4):
                    parts_ready(ev[name] + j)
                    down(U + j, 2 * j, j == 0, j == 3)

            def ffn(U, x_name, rows, ready, turn, hidden_ready, tiles):
                bank = lambda r: PG[:, r, :]
                turn_and_up(U, lambda r: PA[:, r, :], x_name, rows, ready)

                def step(i):
                    turn(i - 1)
                    up(U + 2 - 3, bank, i)
                    hidden_ready(i - 1)
                    down(U + 4 - 3, 0, False, False, i, fhi, flo)
                up(U + 2, bank, 0, lambda: turn(0), tiles)
                hidden_ready(0)
                down(U + 4, 0, True, False, 0, fhi, flo)
                with pe.Fori(2, NFF - 1) as i:
                    step(i)
                turn(NFF - 2)
                up(U + 3 * NFF - 4, bank)
                hidden_ready(NFF - 2)
                down(U + 3 * NFF - 2, 0, False, False, 0, fhi, flo, between=lambda: turn(NFF - 1))
                hidden_ready(NFF - 1)
                down(U + N_F - 1, 0, False, True)

            def swiglu(k, U, name, x_name, ready):
                T0 = ev[name]

                def turn(i):
                    pe.wait_ge(S("hidden"), i + (k * NFF + 1))
                    for f in range(2):
                        pe.wait_ge(S("t_free"), i * 2 + (T0 + f - 1))
                        for r in range(RT):
                            last = nc.tensor.transpose(TB[:, (T0 + f) % 2, r * P:(r + 1) * P],
                                                       fh[:, r, f * P:(f + 1) * P], ident[:, :])
                        last.then_inc(S("t_full"), 1)

                ffn(U, x_name, h, ready, turn, lambda i: pe.wait_ge(S("t_free"), i * 2 + (T0 + 2)), 3)

            pe.wait_ge(S("ident"), 1)
            turn_and_up(U_IN, lambda r: PG[:, r, :], "x", h, lambda r, g: pe.wait_ge(S(f"x_loaded{r}"), 16))
            pe.wait_ge(S("cst_loaded"), 64)
            e = ev["c0"]
            t_bank(e)
            nc.tensor.transpose(TB[0:BUCKETS, e % 2, 0:HQ], relrow[0:HQ, :], ident[0:HQ, 0:HQ]).then_inc(S("t_full"), 1)
            t_bank(e + 1)
            for j in range(4):
                last = nc.tensor.transpose(TB[:, (e + 1) % 2, 44 * j:44 * j + 44], cw4[0:44, j, :], ident[0:44, 0:44])
            last.then_inc(S("t_full"), 1)
            pe.wait_ge(S("w_lo"), 3)
            for k in range(KT):
                for r in range(RT):
                    last = products(PA[:, r, 0:136], k, r, 2, slice(k * 136, (k + 1) * 136), k == 0, k == KT - 1)
            last.then_inc(S("w_used"), 1)
            parts_ready(e)
            mm(PA[0:HQ, 2, 0:T], relT[0:BUCKETS, :], hot[0:BUCKETS, :], start=True, stop=True).then_inc(S("reldist"), 1)
            e = ev["cq"]
            pe.wait_ge(S("cqn"), 1)
            t_bank(e)
            for k in range(2):
                for r in range(RT):
                    last = nc.tensor.transpose(TB[:, e % 2, (2 * k + r) * P:(2 * k + r + 1) * P],
                                               cqn[:, r, k * P:(k + 1) * P], ident[:, :])
            last.then_inc(S("t_full"), 1)
            parts_ready(e)
            pe.wait_ge(S("relv"), 1)
            down(U_IQ, 0, True, True, ends=False)
            e = ev["ki"]
            pe.wait_ge(S("kd"), 1)
            t_bank(e)
            for g in range(2):
                for r in range(RT):
                    last = nc.tensor.transpose(TB[:, e % 2, (2 * g + r) * P:(2 * g + r + 1) * P],
                                               kd[:, r, g, :, :].rearrange("p a b -> p (a b)"), ident[:, :])
            last.then_inc(S("t_full"), 1)
            t_bank(e + 1)
            for r in range(RT):
                last = nc.tensor.transpose(TB[:, (e + 1) % 2, r * P:(r + 1) * P], pin[:, r, C_KI:C_WI], ident[:, :])
            last.then_inc(S("t_full"), 1)
            pe.wait_ge(S("qi_r"), 1)
            turn_rows("qi", qi)
            parts_ready(ev["qi"] + 3)
            for hd in range(HI):
                if hd >= 4:
                    pe.wait_ge(S("relu"), hd - 3)
                mm(PA[:, hd % 4, 0:128], qiT[:, hd, 0:P], kiT[:, 0:P], start=True, stop=True)
                mm(PA[:, hd % 4, 128:384], qiT[:, hd, P:T], kiT, start=True, stop=True).then_inc(S("iscore"), 1)
            pe.wait_ge(S("relu"), HI)
            pe.wait_ge(S("w_lo"), U_UQ + 1)
            for f in range(2):
                for r in range(RT):
                    for t in range(2):
                        last = products(PA[:, 2 * f + r, :], t, r, U_UQ % RING,
                                        slice(t * D + f * HALF, t * D + (f + 1) * HALF), t == 0, t == 1)
                last.then_inc(S("w_used" if f else "first_q"), 1)
            turn_rows("q", qr, lambda g: pe.wait_ge(S("q_r"), 1), range(2))
            parts_ready(ev["q"] + 1)
            attention("", lambda hd: kT[:, hd // 8, :],
                      lambda hd, r: pin[:, r, C_V + HD * (hd // 8):C_V + HD * (hd // 8) + HD],
                      lambda: turn_rows("q", qr, lambda g: pe.wait_ge(S("q_r"), 2), range(2, 4)))
            turn_rows("ao", orow, lambda g: pe.wait_ge(S("orow"), 2 * g + 2))
            out_proj(U_AO, "ao")
            swiglu(0, U_F0, "f0", "n1", lambda r, g: pe.wait_ge(S("norm"), 2 * r + g + 1))

            turn_and_up(U_H, lambda r: PG[:, r, :], "n2", h, lambda r, g: pe.wait_ge(S("norm"), 4 + 2 * r + g + 1))
            up(U_H + 2, lambda r: PA[:, r, :])
            up(U_H + 4, lambda r: PA[:, 2 + r, :])
            pe.wait_ge(S("f_sig"), 1)
            up(U_H + 6, lambda r: PG[:, r, :])
            pe.wait_ge(S("f_sig"), 2)
            up(U_H + 8, lambda r: PA[:, r, :])
            pe.wait_ge(S("qh"), 1)
            pe.wait_ge(S("logf"), 2)
            pe.wait_ge(S("hconst"), 1)
            for b in range(4):
                if b >= 2:
                    pe.wait_ge(S("bT"), b - 1)
                for c in range(2):
                    for r in range(RT):
                        last = mm(PA[:, 2 + b % 2, (2 * c + r) * P:(2 * c + r + 1) * P],
                                  lf[:, r, (2 * b + c) * DH:(2 * b + c + 1) * DH], ucum, start=True, stop=True)
                last.then_inc(S("cum"), 1)
            pe.wait_ge(S("kr"), 2)
            turn_rows("hk", kr)
            pe.wait_ge(S("qh"), 2)
            turn_rows("hq", qh)
            parts_ready(ev["hq"] + 3)
            pe.wait_ge(S("bT"), 4)
            pe.wait_ge(S("vi"), 1)
            for b in range(4):
                for r in range(RT):
                    for c in range(2):
                        rows = slice(r * P, (r + 1) * P)
                        last = mm(PA[:, b, (2 * r + c) * P:(2 * r + c + 1) * P],
                                  kTh[:, 2 * b + c, rows], qTh[:, 2 * b + c, rows], start=True, stop=True)
                last.then_inc(S("diag_full"), 1)

            def level(l):
                pe.wait_ge(S("lv_x"), 2 * TURN[l] + 2)
                d = level_buf(l)
                m = ((CHUNK,) + LEVELS)[l]
                for b in range(4):
                    pe.wait_ge(S("lv_taken"), 4 * l + b + 1)
                    for r in range(RT):
                        for c in range(2):
                            dr = d[:, 2 * b + c, r * P:(r + 1) * P]
                            o = (2 * r + c) * CHUNK
                            last = mm(PA[:, b, o:o + CHUNK], dr,
                                      dr.rearrange("p (b s m) -> p b s m", s=2, m=m)[:, :, 1, :],
                                      start=True, stop=True)
                    last.then_inc(S("lv_full"), 1)

            up(U_H + 10, lambda r: PG[:, r, :])
            level(0)
            pe.wait_ge(S("vi"), 2)
            up(U_H + 12, lambda r: PG[:, r, :], 0, lambda: level(1), 4)
            level(2)
            pe.wait_ge(S("g_raw"), 1)
            up(U_H + 14, lambda r: PG[:, r, :], 0, lambda: (level(3), level(4)), 4)
            level(5)
            pe.wait_ge(S("lv_x"), 2 * TURN["cross"] + 2)
            pe.wait_ge(S("g_raw"), 2)
            dx = level_buf("cross")
            for b in range(2):
                for c in range(4):
                    last = mm(PG[:, b, c * P:(c + 1) * P], dx[:, 4 * b + c, 0:P], dx[:, 4 * b + c, P:T],
                              start=True, stop=True)
                last.then_inc(S("lv_cross"), 1)
            level(6)
            for b in range(4):
                pe.wait_ge(S("lv_taken"), 32)
                pe.wait_ge(S("aT2"), 2)
                for c in range(2):
                    hd = 2 * b + c
                    cols = slice(hd * DH, (hd + 1) * DH)
                    o0, o1 = (PA[:, b, (2 * r + c) * P:(2 * r + c + 1) * P] for r in range(RT))
                    mm(o0, aT[:, 0, hd, :], vi[:, 0, cols], start=True, stop=True)
                    mm(o1, aT[:, 2, hd, :], vi[:, 0, cols], start=True, stop=False)
                    last = mm(o1, aT[:, 1, hd, :], vi[:, 1, cols], start=False, stop=True)
                last.then_inc(S("ho"), 1)
            turn_rows("ho", oh, lambda g: pe.wait_ge(S("oh"), g + 1))
            out_proj(U_HO, "ho")
            swiglu(1, U_F1, "f1", "n3", lambda r, g: pe.wait_ge(S("norm"), 4 * 2 + 2 * r + g + 1))

            banks = (lambda r: PG[:, r, :], lambda r: PA[:, r, :], lambda r: PA[:, 2 + r, :])
            for c in range(6):
                if c >= 3:
                    pe.wait_ge(S("qkv"), c - 2)
                if c == 0:
                    turn_and_up(U_M, banks[0], "y1", orow, lambda r, g: pe.wait_ge(S("y1_rows"), 2 * r + g + 1))
                else:
                    up(U_M + 2 * c, banks[c % 3])
            pe.wait_ge(S("qkv"), 2)
            turn_rows("q2", q2)
            pe.wait_ge(S("qkv"), 6)
            turn_rows("k2", k2)
            parts_ready(ev["k2"] + 3)
            attention("2", lambda hd: k2T[:, hd // 2, :],
                      lambda hd, r: v2[:, r, HD * hd:HD * hd + HD])
            turn_rows("ao2", orow, lambda g: pe.wait_ge(S("orow2"), 2 * g + 2))
            out_proj(U_MO, "ao2")

            T0 = ev["f2"]

            def conv_turn(i):
                pe.wait_ge(S("urow"), i + 1)
                for s in range(2):
                    pe.wait_ge(S("t_free"), i * 2 + (T0 + s - 1))
                    for f in range(2):
                        for r in range(RT):
                            last = nc.tensor.transpose(TB[:, (T0 + s) % 2, (2 * f + r) * P:(2 * f + r + 1) * P],
                                                       urow[:, r, s * FC + f * P:s * FC + (f + 1) * P], ident[:, :])
                    last.then_inc(S("t_full"), 1)

            ffn(U_F2, "y2", orow, lambda r, g: pe.wait_ge(S("norm"), 4 * 4 + 2 * r + g + 1), conv_turn,
                lambda i: pe.wait_ge(S("c_lo"), i + 1), 1)


INPUTS = ("x", "positions", "att_w_in", "att_g_cq", "att_w_uq", "att_w_iq", "att_g_ik", "att_b_ik", "att_w_o",
          "hgrn_lb_logits", "hgrn_w_in", "hgrn_g_norm", "hgrn_w_o", "ffn_w_gate", "ffn_w_up", "ffn_w_down",
          "ln_g", "ln_b", "attn_norm_2", "w_qkv_2", "w_o_2", "rel_bias_2", "ffn_norm_2", "w_up_2", "conv_w_2",
          "conv_b_2", "w_down_2", "final_norm_2")
ONE = ("x", "positions", "att_w_in", "att_g_cq", "att_w_uq", "att_w_iq", "att_g_ik", "att_b_ik", "att_w_o",
       "hgrn_w_in", "hgrn_g_norm", "hgrn_w_o", "attn_norm_2", "w_qkv_2", "w_o_2", "ffn_norm_2", "w_up_2",
       "conv_w_2", "conv_b_2", "w_down_2")


def kernel(**inputs):
    import concourse.bacc as bacc
    from concourse.bass_utils import run_bass_kernel_spmd as run

    nc = bacc.Bacc("TRN2", target_bir_lowering=False, num_devices=1)
    arrays = {name: np.ascontiguousarray(inputs[name]) for name in INPUTS}
    arrays["inv"], arrays["hot"] = shape_constants()
    feed, w = {}, {}
    for name, a in arrays.items():
        feed[f"in_{name}"] = a
        w[name] = nc.dram_tensor(f"in_{name}", a.shape, mybir.dt.from_np(a.dtype), kind="ExternalInput").ap()
        if name in ONE or name == "inv":
            w[name] = w[name][0]
    for k in range(2):
        w[f"ffn{k}"] = tuple(w[m][k] for m in ("ffn_w_gate", "ffn_w_up", "ffn_w_down"))
    w["ffn2"] = (w["w_up_2"][:, 0:FF2], w["w_up_2"][:, FF2:2 * FF2], w["w_down_2"])
    out = nc.dram_tensor("out_0", (1, T, D), F32, kind="ExternalOutput").ap()
    build(nc, w, out[0])
    r = run(nc, [feed], core_ids=[0])
    return r.results[0]["out_0"]
```
